# Optimizing a Trainium2 kernel written in Bass

```python
import math
import jax, jax.numpy as jnp
from jax import lax
import numpy as np
import jax
import jax.numpy as jnp

D_MODEL = 1024
BATCH = 1
SEQ = 256
DEPTH = 2

N_MIXERS = 2
BLOCK_Q = 128
DA_HEADS = 8
DA_HEAD_DIM = 64
SB_HEADS = 16
SB_HEAD_DIM = 64
REL_BUCKETS = 32
REL_MAX_DIST = 128
MOE_GROUPS = 4
MOE_EXPERTS_PER_GROUP = 8
MOE_TOP_K = 2
MOE_HIDDEN = 512
N_EXPERTS = MOE_GROUPS * MOE_EXPERTS_PER_GROUP
DEEPNORM_ALPHA = (2 * DEPTH) ** 0.25
DEEPNORM_BETA = (8 * DEPTH) ** -0.25
LN_EPS = 1e-5
RMS_EPS = 1e-6
NEG_INF = -1e30
N_DA_LAYERS = (DEPTH + 1) // 2
N_SB_LAYERS = DEPTH // 2


def layer_norm(x, g, b):
    xf = x.astype(jnp.float32)
    mu = jnp.mean(xf, axis=-1, keepdims=True)
    xc = xf - mu
    var = jnp.mean(xc * xc, axis=-1, keepdims=True)
    return (xc * lax.rsqrt(var + LN_EPS) * g.astype(jnp.float32) + b.astype(jnp.float32)).astype(x.dtype)

def rel_bucket(q_pos, k_pos):
    n = jnp.maximum(q_pos[:, None] - k_pos[None, :], 0)
    max_exact = REL_BUCKETS // 2
    nf = jnp.maximum(n, 1).astype(jnp.float32)
    large = max_exact + (jnp.log(nf / max_exact) / math.log(REL_MAX_DIST / max_exact)
                         * (REL_BUCKETS - max_exact)).astype(jnp.int32)
    large = jnp.minimum(large, REL_BUCKETS - 1)
    return jnp.where(n < max_exact, n, large)

def diff_attention(x, wq, wk, wv, wo, lq1, lk1, lq2, lk2, subln_g, rel_table, layer_idx):
    b, s, _ = x.shape
    q = (x @ wq).reshape(b, s, DA_HEADS, 2, DA_HEAD_DIM)
    k = (x @ wk).reshape(b, s, DA_HEADS, 2, DA_HEAD_DIM)
    v = (x @ wv).reshape(b, s, DA_HEADS, 2 * DA_HEAD_DIM)
    lam_init = 0.8 - 0.6 * math.exp(-0.3 * layer_idx)
    f32 = jnp.float32
    lam = (jnp.exp(jnp.sum(lq1.astype(f32) * lk1.astype(f32)))
           - jnp.exp(jnp.sum(lq2.astype(f32) * lk2.astype(f32))) + lam_init)
    k_pos = jnp.arange(s)
    scale = DA_HEAD_DIM ** -0.5
    g = subln_g.astype(f32)

    def block(i):
        start = i * BLOCK_Q
        qb = lax.dynamic_slice_in_dim(q, start, BLOCK_Q, axis=1)
        q_pos = start + jnp.arange(BLOCK_Q)
        bias = jnp.transpose(rel_table[rel_bucket(q_pos, k_pos)], (2, 0, 1)).astype(f32)
        logits = jnp.einsum('bqhcd,bkhcd->bhcqk', qb, k).astype(f32) * scale + bias[None, :, None]
        causal = k_pos[None, :] <= q_pos[:, None]
        logits = jnp.where(causal, logits, NEG_INF)
        p = jax.nn.softmax(logits, axis=-1)
        attn = p[:, :, 0] - lam * p[:, :, 1]
        o = jnp.einsum('bhqk,bkhe->bqhe', attn.astype(x.dtype), v).astype(f32)
        o = o * lax.rsqrt(jnp.mean(o * o, axis=-1, keepdims=True) + RMS_EPS) * g
        return (o * (1.0 - lam_init)).astype(x.dtype)

    blocks = lax.map(block, jnp.arange(s // BLOCK_Q))
    o = jnp.moveaxis(blocks, 0, 1).reshape(b, s, DA_HEADS * 2 * DA_HEAD_DIM)
    return o @ wo

def stick_breaking(x, wq, wk, wv, wo):
    b, s, _ = x.shape
    q = (x @ wq).reshape(b, s, SB_HEADS, SB_HEAD_DIM)
    k = (x @ wk).reshape(b, s, SB_HEADS, SB_HEAD_DIM)
    v = (x @ wv).reshape(b, s, SB_HEADS, SB_HEAD_DIM)
    k_pos = jnp.arange(s)
    scale = SB_HEAD_DIM ** -0.5

    def block(i):
        start = i * BLOCK_Q
        qb = lax.dynamic_slice_in_dim(q, start, BLOCK_Q, axis=1)
        q_pos = start + jnp.arange(BLOCK_Q)
        z = jnp.einsum('bqhd,bkhd->bhqk', qb, k).astype(jnp.float32) * scale
        strict = k_pos[None, :] < q_pos[:, None]
        log_fail = jnp.where(strict, jax.nn.log_sigmoid(-z), 0.0)
        later = lax.cumsum(log_fail, axis=3, reverse=True) - log_fail
        w = jnp.where(strict, jnp.exp(jax.nn.log_sigmoid(z) + later), 0.0)
        return jnp.einsum('bhqk,bkhd->bqhd', w.astype(x.dtype), v)

    blocks = lax.map(block, jnp.arange(s // BLOCK_Q))
    o = jnp.moveaxis(blocks, 0, 1).reshape(b, s, SB_HEADS * SB_HEAD_DIM)
    return o @ wo

def hier_moe(x, w_group, b_group, w_expert, b_expert, w1, w3, w2):
    b, s, d = x.shape
    t = b * s
    f32 = jnp.float32
    xt = x.reshape(t, d)
    g_prob = jax.nn.softmax((xt @ w_group + b_group).astype(f32), axis=-1)
    g_gate, g_idx = lax.top_k(g_prob, 1)
    e_logits = (xt @ w_expert + b_expert).astype(f32).reshape(t, MOE_GROUPS, MOE_EXPERTS_PER_GROUP)
    e_logits = jnp.take_along_axis(e_logits, g_idx[:, :, None], axis=1)[:, 0]
    e_prob = jax.nn.softmax(e_logits, axis=-1)
    e_gate, e_idx = lax.top_k(e_prob, MOE_TOP_K)
    e_gate = e_gate / jnp.sum(e_gate, axis=-1, keepdims=True)
    weight = g_gate * e_gate
    expert_id = g_idx * MOE_EXPERTS_PER_GROUP + e_idx
    gates = jnp.sum(jax.nn.one_hot(expert_id, N_EXPERTS, dtype=f32) * weight[..., None], axis=1)

    def step(acc, ew):
        w1e, w3e, w2e, ge = ew
        h = jax.nn.silu(xt @ w1e) * (xt @ w3e)
        return acc + ge[:, None] * (h @ w2e).astype(f32), None

    y, _ = lax.scan(step, jnp.zeros((t, d), f32), (w1, w3, w2, gates.T))
    return y.astype(x.dtype).reshape(b, s, d)

def first_inputs(seed: int = 0) -> dict:
    key = jax.random.key(seed)
    ks = jax.random.split(key, 26)
    nrm = jax.random.normal
    D = D_MODEL
    da_qk = DA_HEADS * 2 * DA_HEAD_DIM
    da_v = DA_HEADS * 2 * DA_HEAD_DIM
    sb_w = SB_HEADS * SB_HEAD_DIM
    inv = D ** -0.5
    return {
        "x": nrm(ks[0], (BATCH, SEQ, D), jnp.float32),
        "rel_table": 0.5 * nrm(ks[1], (REL_BUCKETS, DA_HEADS), jnp.float32),
        "da_wq": inv * nrm(ks[2], (N_DA_LAYERS, D, da_qk), jnp.float32),
        "da_wk": inv * nrm(ks[3], (N_DA_LAYERS, D, da_qk), jnp.float32),
        "da_wv": DEEPNORM_BETA * inv * nrm(ks[4], (N_DA_LAYERS, D, da_v), jnp.float32),
        "da_wo": DEEPNORM_BETA * da_v ** -0.5 * nrm(ks[5], (N_DA_LAYERS, da_v, D), jnp.float32),
        "da_lq1": 0.1 * nrm(ks[6], (N_DA_LAYERS, DA_HEAD_DIM), jnp.float32),
        "da_lk1": 0.1 * nrm(ks[7], (N_DA_LAYERS, DA_HEAD_DIM), jnp.float32),
        "da_lq2": 0.1 * nrm(ks[8], (N_DA_LAYERS, DA_HEAD_DIM), jnp.float32),
        "da_lk2": 0.1 * nrm(ks[9], (N_DA_LAYERS, DA_HEAD_DIM), jnp.float32),
        "da_subln_g": 1.0 + 0.02 * nrm(ks[10], (N_DA_LAYERS, 2 * DA_HEAD_DIM), jnp.float32),
        "sb_wq": inv * nrm(ks[11], (N_SB_LAYERS, D, sb_w), jnp.float32),
        "sb_wk": inv * nrm(ks[12], (N_SB_LAYERS, D, sb_w), jnp.float32),
        "sb_wv": DEEPNORM_BETA * inv * nrm(ks[13], (N_SB_LAYERS, D, sb_w), jnp.float32),
        "sb_wo": DEEPNORM_BETA * sb_w ** -0.5 * nrm(ks[14], (N_SB_LAYERS, sb_w, D), jnp.float32),
        "ln_mix_g": 1.0 + 0.02 * nrm(ks[15], (DEPTH, D), jnp.float32),
        "ln_mix_b": 0.02 * nrm(ks[16], (DEPTH, D), jnp.float32),
        "ln_ffn_g": 1.0 + 0.02 * nrm(ks[17], (DEPTH, D), jnp.float32),
        "ln_ffn_b": 0.02 * nrm(ks[18], (DEPTH, D), jnp.float32),
        "moe_w_group": inv * nrm(ks[19], (DEPTH, D, MOE_GROUPS), jnp.float32),
        "moe_b_group": 0.01 * nrm(ks[20], (DEPTH, MOE_GROUPS), jnp.float32),
        "moe_w_expert": inv * nrm(ks[21], (DEPTH, D, N_EXPERTS), jnp.float32),
        "moe_b_expert": 0.01 * nrm(ks[22], (DEPTH, N_EXPERTS), jnp.float32),
        "moe_w1": inv * nrm(ks[23], (DEPTH, N_EXPERTS, D, MOE_HIDDEN), jnp.float32),
        "moe_w3": inv * nrm(ks[24], (DEPTH, N_EXPERTS, D, MOE_HIDDEN), jnp.float32),
        "moe_w2": DEEPNORM_BETA * MOE_HIDDEN ** -0.5 * nrm(ks[25], (DEPTH, N_EXPERTS, MOE_HIDDEN, D), jnp.float32),
    }

def first_block(x, rel_table, da_wq, da_wk, da_wv, da_wo, da_lq1, da_lk1, da_lq2, da_lk2, da_subln_g,
              sb_wq, sb_wk, sb_wv, sb_wo, ln_mix_g, ln_mix_b, ln_ffn_g, ln_ffn_b,
              moe_w_group, moe_b_group, moe_w_expert, moe_b_expert, moe_w1, moe_w3, moe_w2):
    for layer in range(DEPTH):
        j = layer // N_MIXERS
        if layer % N_MIXERS == 0:
            mix = diff_attention(x, da_wq[j], da_wk[j], da_wv[j], da_wo[j], da_lq1[j], da_lk1[j],
                                 da_lq2[j], da_lk2[j], da_subln_g[j], rel_table, layer)
        else:
            mix = stick_breaking(x, sb_wq[j], sb_wk[j], sb_wv[j], sb_wo[j])
        x = layer_norm(DEEPNORM_ALPHA * x + mix, ln_mix_g[layer], ln_mix_b[layer])
        ffn = hier_moe(x, moe_w_group[layer], moe_b_group[layer], moe_w_expert[layer],
                       moe_b_expert[layer], moe_w1[layer], moe_w3[layer], moe_w2[layer])
        x = layer_norm(DEEPNORM_ALPHA * x + ffn, ln_ffn_g[layer], ln_ffn_b[layer])
    return x


CTX_LEN = 256
GRID_W = 64
EPS = 1e-6
N_MOD = 6
HEAD_DIM = 64
ATTN_WIDTH = D_MODEL // 2
N_HEADS = ATTN_WIDTH // HEAD_DIM
N_KV_HEADS = 2
Q_PER_KV = N_HEADS // N_KV_HEADS
ROPE_THETA = 10000.0
ATTN_BLOCK = 128
SSD_WIDTH = D_MODEL - ATTN_WIDTH
SSD_HEAD_DIM = 64
SSD_HEADS = SSD_WIDTH // SSD_HEAD_DIM
SSD_GROUPS = 2
HEADS_PER_GROUP = SSD_HEADS // SSD_GROUPS
D_STATE = 128
CONV_WIDTH = 5
SSD_CHUNK = 128
D_FF = -(-8 * D_MODEL // (3 * 256)) * 256
Q_DIM = N_HEADS * HEAD_DIM
KV_DIM = N_KV_HEADS * HEAD_DIM
BC_DIM = SSD_GROUPS * D_STATE
XBC_DIM = SSD_WIDTH + 2 * BC_DIM
IN_DIM = Q_DIM + 2 * KV_DIM + SSD_WIDTH + XBC_DIM + SSD_HEADS
IN_SPLITS = (Q_DIM, Q_DIM + KV_DIM, Q_DIM + 2 * KV_DIM, Q_DIM + 2 * KV_DIM + SSD_WIDTH,
             Q_DIM + 2 * KV_DIM + SSD_WIDTH + XBC_DIM)


def rmsnorm(x, w):
    xf = x.astype(jnp.float32)
    y = xf * lax.rsqrt(jnp.mean(xf * xf, axis=-1, keepdims=True) + EPS)
    return (y * w.astype(jnp.float32)).astype(x.dtype)

def axial_rope_tables(rows):
    row = jnp.repeat(jnp.arange(rows, dtype=jnp.float32), GRID_W)
    col = jnp.tile(jnp.arange(GRID_W, dtype=jnp.float32), rows)
    n_freq = HEAD_DIM // 4
    freqs = ROPE_THETA ** (-jnp.arange(n_freq, dtype=jnp.float32) / n_freq)
    ang = jnp.concatenate([row[:, None] * freqs, col[:, None] * freqs], axis=-1)
    return jnp.cos(ang), jnp.sin(ang)

def apply_rope(x, cos, sin):
    half = HEAD_DIM // 2
    x1, x2 = x[..., :half], x[..., half:]
    c = cos[None, :, None, :].astype(x.dtype)
    s = sin[None, :, None, :].astype(x.dtype)
    return jnp.concatenate([x1 * c - x2 * s, x1 * s + x2 * c], axis=-1)

def block_attention(q, k, v):
    b, n = q.shape[:2]
    nb = n // ATTN_BLOCK
    qb = q.reshape(b, nb, ATTN_BLOCK, N_KV_HEADS, Q_PER_KV, HEAD_DIM).transpose(1, 0, 2, 3, 4, 5)
    scale = HEAD_DIM ** -0.5

    def one_block(q_blk):
        s = jnp.einsum('bqkgd,bskd->bkgqs', q_blk, k).astype(jnp.float32) * scale
        p = jax.nn.softmax(s, axis=-1).astype(v.dtype)
        return jnp.einsum('bkgqs,bskd->bqkgd', p, v)

    o = lax.map(one_block, qb)
    return o.transpose(1, 0, 2, 3, 4, 5).reshape(b, n, N_HEADS * HEAD_DIM)

def depthwise_conv_silu(x, w, bias):
    y = lax.conv_general_dilated(
        x, w[:, None, :].astype(x.dtype), window_strides=(1,),
        padding=[(CONV_WIDTH // 2, CONV_WIDTH // 2)],
        dimension_numbers=('NWC', 'WIO', 'NWC'), feature_group_count=x.shape[-1])
    return jax.nn.silu(y + bias.astype(x.dtype))

def ssd_scan(x, dt, A, B, C, h0):
    b, L, H, P = x.shape
    nc = L // SSD_CHUNK
    f32 = jnp.float32
    Bh = jnp.repeat(B.astype(f32), HEADS_PER_GROUP, axis=2).reshape(b, nc, SSD_CHUNK, H, D_STATE)
    Ch = jnp.repeat(C.astype(f32), HEADS_PER_GROUP, axis=2).reshape(b, nc, SSD_CHUNK, H, D_STATE)
    xdt = (x.astype(f32) * dt[..., None]).reshape(b, nc, SSD_CHUNK, H, P)
    acum = jnp.cumsum((dt * A).reshape(b, nc, SSD_CHUNK, H), axis=2)
    lower = jnp.tril(jnp.ones((SSD_CHUNK, SSD_CHUNK), dtype=bool))[None, None, :, :, None]
    seg = acum[:, :, :, None, :] - acum[:, :, None, :, :]
    decay = jnp.exp(jnp.where(lower, seg, -jnp.inf))
    scores = jnp.einsum('bcihn,bcjhn->bcijh', Ch, Bh) * decay
    y_intra = jnp.einsum('bcijh,bcjhp->bcihp', scores, xdt)
    decay_to_end = jnp.exp(acum[:, :, -1:, :] - acum)
    chunk_states = jnp.einsum('bcjhn,bcjh,bcjhp->bchpn', Bh, decay_to_end, xdt)
    chunk_decay = jnp.exp(acum[:, :, -1, :])

    def step(h, inp):
        s_c, d_c = inp
        return h * d_c[:, :, None, None] + s_c, h

    h_final, h_in = lax.scan(step, h0, (chunk_states.transpose(1, 0, 2, 3, 4), chunk_decay.transpose(1, 0, 2)))
    h_in = h_in.transpose(1, 0, 2, 3, 4)
    y_inter = jnp.einsum('bcihn,bcih,bchpn->bcihp', Ch, jnp.exp(acum), h_in)
    return (y_intra + y_inter).reshape(b, L, H, P), h_final

def hybrid_mixer(h_lat, h_ctx, cos, sin, w_in, q_norm, k_norm, conv_w, conv_b, dt_bias_fwd, dt_bias_bwd,
                 a_log_fwd, a_log_bwd, d_skip, ssd_norm, w_out, with_ctx_out):
    b, n_lat, _ = h_lat.shape
    n_ctx = h_ctx.shape[1]
    f32 = jnp.float32
    q_l, k_l, v_l, z_l, xbc_l, dt_l = jnp.split(h_lat @ w_in, IN_SPLITS, axis=-1)
    q_c, k_c, v_c, z_c, xbc_c, dt_c = jnp.split(h_ctx @ w_in, IN_SPLITS, axis=-1)

    def heads(q, k, v, n):
        q = rmsnorm(q.reshape(b, n, N_HEADS, HEAD_DIM), q_norm)
        k = rmsnorm(k.reshape(b, n, N_KV_HEADS, HEAD_DIM), k_norm)
        return q, k, v.reshape(b, n, N_KV_HEADS, HEAD_DIM)

    q_l, k_l, v_l = heads(q_l, k_l, v_l, n_lat)
    q_c, k_c, v_c = heads(q_c, k_c, v_c, n_ctx)
    q_l = apply_rope(q_l, cos, sin)
    k_l = apply_rope(k_l, cos, sin)
    k_all = jnp.concatenate([k_c, k_l], axis=1)
    v_all = jnp.concatenate([v_c, v_l], axis=1)
    attn_l = block_attention(q_l, k_all, v_all)

    def ssd_inputs(xbc, n):
        xbc = depthwise_conv_silu(xbc, conv_w, conv_b)
        xs, Bs, Cs = jnp.split(xbc, (SSD_WIDTH, SSD_WIDTH + BC_DIM), axis=-1)
        return (xs.reshape(b, n, SSD_HEADS, SSD_HEAD_DIM), Bs.reshape(b, n, SSD_GROUPS, D_STATE),
                Cs.reshape(b, n, SSD_GROUPS, D_STATE))

    xs_l, B_l, C_l = ssd_inputs(xbc_l, n_lat)
    xs_c, B_c, C_c = ssd_inputs(xbc_c, n_ctx)
    ys_l, ys_c = [], []
    for dt_bias, a_log, reverse in ((dt_bias_fwd, a_log_fwd, False), (dt_bias_bwd, a_log_bwd, True)):
        A = -jnp.exp(a_log.astype(f32))
        d_l = jax.nn.softplus(dt_l.astype(f32) + dt_bias.astype(f32))
        d_c = jax.nn.softplus(dt_c.astype(f32) + dt_bias.astype(f32))
        flip = (lambda t: jnp.flip(t, axis=1)) if reverse else (lambda t: t)
        h0 = jnp.zeros((b, SSD_HEADS, SSD_HEAD_DIM, D_STATE), f32)
        y_c, h_ctx_final = ssd_scan(flip(xs_c), flip(d_c), A, flip(B_c), flip(C_c), h0)
        y_l, _ = ssd_scan(flip(xs_l), flip(d_l), A, flip(B_l), flip(C_l), h_ctx_final)
        ys_l.append(flip(y_l))
        ys_c.append(flip(y_c))

    def ssd_output(y, xs, z, n):
        y = (y + d_skip.astype(f32)[:, None] * xs.astype(f32)).astype(z.dtype).reshape(b, n, SSD_WIDTH)
        return rmsnorm(y * jax.nn.silu(z), ssd_norm)

    out_l = jnp.concatenate([attn_l, ssd_output(ys_l[0] + ys_l[1], xs_l, z_l, n_lat)], axis=-1) @ w_out
    if not with_ctx_out:
        return out_l, None
    attn_c = block_attention(q_c, k_c, v_c)
    out_c = jnp.concatenate([attn_c, ssd_output(ys_c[0] + ys_c[1], xs_c, z_c, n_ctx)], axis=-1) @ w_out
    return out_l, out_c

def swiglu(h, w_gate, w_up, w_down):
    return (jax.nn.silu(h @ w_gate) * (h @ w_up)) @ w_down

def second_inputs(seed: int = 0) -> dict:
    key = jax.random.key(seed)
    ks = jax.random.split(key, 24)
    f32 = jnp.float32
    L = DEPTH

    def nrm(k, shape, scale):
        return jax.random.normal(k, shape, f32) * scale

    def gain(k, shape):
        return 1.0 + 0.05 * jax.random.normal(k, shape, f32)

    dt0 = jnp.exp(jax.random.uniform(ks[14], (L, 2, SSD_HEADS), f32, math.log(1e-3), math.log(1e-1)))
    dt_bias = dt0 + jnp.log(-jnp.expm1(-dt0))
    a_log = jnp.log(jax.random.uniform(ks[15], (L, 2, SSD_HEADS), f32, 1.0, 16.0))
    nk = jax.random.split(ks[6], 4)
    return {
        'x': nrm(ks[0], (BATCH, SEQ, D_MODEL), 1.0),
        'c': nrm(ks[1], (BATCH, D_MODEL), 1.0),
        'ctx': nrm(ks[2], (BATCH, CTX_LEN, D_MODEL), 1.0),
        'c_ctx': nrm(ks[3], (D_MODEL,), 1.0),
        'w_mod': nrm(ks[4], (L, D_MODEL, N_MOD * D_MODEL), 0.5 * D_MODEL ** -0.5),
        'b_mod': nrm(ks[5], (L, N_MOD * D_MODEL), 0.02),
        'norm_mix_pre': gain(nk[0], (L, D_MODEL)),
        'norm_mix_post': gain(nk[1], (L, D_MODEL)),
        'norm_ffn_pre': gain(nk[2], (L, D_MODEL)),
        'norm_ffn_post': gain(nk[3], (L, D_MODEL)),
        'w_in': nrm(ks[10], (L, D_MODEL, IN_DIM), D_MODEL ** -0.5),
        'q_norm': gain(ks[11], (L, HEAD_DIM)),
        'k_norm': gain(ks[12], (L, HEAD_DIM)),
        'conv_w': nrm(ks[13], (L, CONV_WIDTH, XBC_DIM), CONV_WIDTH ** -0.5),
        'conv_b': nrm(ks[16], (L, XBC_DIM), 0.02),
        'dt_bias_fwd': dt_bias[:, 0],
        'dt_bias_bwd': dt_bias[:, 1],
        'a_log_fwd': a_log[:, 0],
        'a_log_bwd': a_log[:, 1],
        'd_skip': 1.0 + 0.1 * jax.random.normal(ks[17], (L, SSD_HEADS), f32),
        'ssd_norm': gain(ks[18], (L, SSD_WIDTH)),
        'w_out': nrm(ks[19], (L, D_MODEL, D_MODEL), D_MODEL ** -0.5),
        'w_gate': nrm(ks[20], (L, D_MODEL, D_FF), D_MODEL ** -0.5),
        'w_up': nrm(ks[21], (L, D_MODEL, D_FF), D_MODEL ** -0.5),
        'w_down': nrm(ks[22], (L, D_FF, D_MODEL), D_FF ** -0.5),
    }

def second_block(x, c, ctx, c_ctx, w_mod, b_mod, norm_mix_pre, norm_mix_post, norm_ffn_pre, norm_ffn_post,
              w_in, q_norm, k_norm, conv_w, conv_b, dt_bias_fwd, dt_bias_bwd, a_log_fwd, a_log_bwd, d_skip,
              ssd_norm, w_out, w_gate, w_up, w_down):
    n_lat = x.shape[1]
    rows = n_lat // GRID_W
    cos, sin = axial_rope_tables(rows)
    silu_c = jax.nn.silu(c)
    silu_cc = jax.nn.silu(c_ctx)
    x_lat, x_ctx = x, ctx
    for l in range(DEPTH):
        update_ctx = l < DEPTH - 1
        mod_l = (silu_c @ w_mod[l] + b_mod[l])[:, None, :]
        mod_c = (silu_cc @ w_mod[l] + b_mod[l])[None, None, :]
        sh1_l, sc1_l, g1_l, sh2_l, sc2_l, g2_l = jnp.split(mod_l, N_MOD, axis=-1)
        sh1_c, sc1_c, g1_c, sh2_c, sc2_c, g2_c = jnp.split(mod_c, N_MOD, axis=-1)

        h_l = rmsnorm(x_lat, norm_mix_pre[l]) * (1.0 + sc1_l) + sh1_l
        h_c = rmsnorm(x_ctx, norm_mix_pre[l]) * (1.0 + sc1_c) + sh1_c
        m_l, m_c = hybrid_mixer(h_l, h_c, cos, sin, w_in[l], q_norm[l], k_norm[l], conv_w[l], conv_b[l],
                                dt_bias_fwd[l], dt_bias_bwd[l], a_log_fwd[l], a_log_bwd[l], d_skip[l],
                                ssd_norm[l], w_out[l], update_ctx)
        x_lat = x_lat + g1_l * rmsnorm(m_l, norm_mix_post[l])

        f_l = rmsnorm(x_lat, norm_ffn_pre[l]) * (1.0 + sc2_l) + sh2_l
        x_lat = x_lat + g2_l * rmsnorm(swiglu(f_l, w_gate[l], w_up[l], w_down[l]), norm_ffn_post[l])

        if update_ctx:
            x_ctx = x_ctx + g1_c * rmsnorm(m_c, norm_mix_post[l])
            f_c = rmsnorm(x_ctx, norm_ffn_pre[l]) * (1.0 + sc2_c) + sh2_c
            x_ctx = x_ctx + g2_c * rmsnorm(swiglu(f_c, w_gate[l], w_up[l], w_down[l]), norm_ffn_post[l])
    return x_lat


def setup_inputs(seed=0):
    out = dict(first_inputs(seed))
    for name, value in second_inputs(seed + 1).items():
        if name != "x":
            out[name + "_2"] = value
    return out


def reference(
    x, rel_table, da_wq, da_wk, da_wv, da_wo, da_lq1, da_lk1, da_lq2, da_lk2, da_subln_g, sb_wq,
    sb_wk, sb_wv, sb_wo, ln_mix_g, ln_mix_b, ln_ffn_g, ln_ffn_b, moe_w_group, moe_b_group,
    moe_w_expert, moe_b_expert, moe_w1, moe_w3, moe_w2, c_2, ctx_2, c_ctx_2, w_mod_2, b_mod_2,
    norm_mix_pre_2, norm_mix_post_2, norm_ffn_pre_2, norm_ffn_post_2, w_in_2, q_norm_2,
    k_norm_2, conv_w_2, conv_b_2, dt_bias_fwd_2, dt_bias_bwd_2, a_log_fwd_2, a_log_bwd_2,
    d_skip_2, ssd_norm_2, w_out_2, w_gate_2, w_up_2, w_down_2,
):
    x = first_block(
        x, rel_table, da_wq, da_wk, da_wv, da_wo, da_lq1, da_lk1, da_lq2, da_lk2, da_subln_g,
        sb_wq, sb_wk, sb_wv, sb_wo, ln_mix_g, ln_mix_b, ln_ffn_g, ln_ffn_b, moe_w_group,
        moe_b_group, moe_w_expert, moe_b_expert, moe_w1, moe_w3, moe_w2,
    )
    return second_block(
        x, c_2, ctx_2, c_ctx_2, w_mod_2, b_mod_2, norm_mix_pre_2, norm_mix_post_2,
        norm_ffn_pre_2, norm_ffn_post_2, w_in_2, q_norm_2, k_norm_2, conv_w_2, conv_b_2,
        dt_bias_fwd_2, dt_bias_bwd_2, a_log_fwd_2, a_log_bwd_2, d_skip_2, ssd_norm_2, w_out_2,
        w_gate_2, w_up_2, w_down_2,
    )


_drawn_inputs = setup_inputs


def setup_inputs(seed=0):
    import zlib

    import numpy as np

    out = dict(_drawn_inputs(seed))
    spreads = {}
    factors = {'da_lq1': 4.206,
     'da_lk2': 6.759,
     'da_subln_g': 4.682,
     'moe_b_group': 5.202,
     'moe_b_expert': 7.425,
     'norm_mix_post_2': 2.763,
     'norm_ffn_post_2': 2.818,
     'q_norm_2': 8.0,
     'k_norm_2': 8.0,
     'conv_b_2': 4.811,
     'd_skip_2': 3.513,
     'ssd_norm_2': 2.776}
    for name, (base, spread) in spreads.items():
        noise = np.random.default_rng([zlib.crc32(name.encode()), seed]).standard_normal(out[name].shape)
        drawn = base * np.exp(spread * noise) if base else spread * noise
        out[name] = jnp.asarray(drawn.astype(out[name].dtype))
    for name, factor in factors.items():
        out[name] = (out[name] * factor).astype(out[name].dtype)
    return out
```

```python
import math
from contextlib import ExitStack

import numpy as np
import concourse.bass as bass
from concourse import mybir

F32 = mybir.dt.float32
I32 = mybir.dt.int32
ALU = mybir.AluOpType
ACT = mybir.ActivationFunctionType
AX = mybir.AxisListType

P = 128
D = 1024
KT = D // P
SEQ = 256
NT = SEQ // P
DEPTH = 2
BUCKETS, MAX_DIST = 32, 128
DA_HEADS = 8
N_EXPERTS, GROUPS, PER_GROUP, HIDDEN = 32, 4, 8, 512
ALPHA = (2 * DEPTH) ** 0.25
LN_EPS, RMS_EPS, EPS = 1e-5, 1e-6, 1e-6
NEG = -1e30
LAM_INIT = 0.8 - 0.6 * math.exp(-0.3 * 0)

RING = 4
SLOT = 8192
PER_SLOT = 32

C_ID, C_LE, C_GE, C_LT, C_GT, C_NEGD, C_NGE, C_IOTA, C_COS, C_SIN = (
    0, 128, 256, 384, 512, 640, 768, 896, 1152, 1216)
C_COLS = 1280
LEN_T = 512


def const_tables():
    k, i = np.arange(P)[:, None], np.arange(P)[None, :]
    c = np.zeros((P, C_COLS), np.float32)
    c[:, C_ID:C_ID + P] = k == i
    c[:, C_LE:C_LE + P] = k <= i
    c[:, C_GE:C_GE + P] = k >= i
    c[:, C_LT:C_LT + P] = k < i
    c[:, C_GT:C_GT + P] = k > i
    c[:, C_NEGD:C_NEGD + P] = np.where(k >= i, NEG, 0)
    c[:, C_NGE:C_NGE + P] = -(k >= i).astype(np.float32)
    c[:, C_IOTA:C_IOTA + 256] = np.arange(256)
    n_freq = 16
    freqs = np.float32(10000.0) ** (-np.arange(n_freq, dtype=np.float32) / np.float32(n_freq))
    pos = np.arange(SEQ)
    ang = np.concatenate([(pos // 64).astype(np.float32)[:, None] * freqs,
                          (pos % 64).astype(np.float32)[:, None] * freqs], -1)
    c[:, C_COS:C_COS + 64] = np.cos(ang).reshape(NT, P, 32).transpose(1, 0, 2).reshape(P, 64)
    c[:, C_SIN:C_SIN + 64] = np.sin(ang).reshape(NT, P, 32).transpose(1, 0, 2).reshape(P, 64)
    n = np.arange(LEN_T) - (SEQ - 1)
    half = BUCKETS // 2
    nf = np.maximum(n, 1).astype(np.float32)
    large = half + (np.log(nf / np.float32(half)) / np.float32(math.log(MAX_DIST / half))
                    * np.float32(BUCKETS - half)).astype(np.int32)
    bucket = np.where(n < half, n, np.minimum(large, BUCKETS - 1))
    hot = np.zeros((BUCKETS + 1, LEN_T), np.float32)
    hot[np.where(n < 0, BUCKETS, bucket), np.arange(LEN_T)] = 1
    return c, hot


def view(ap, *free):
    return bass.AP(ap.tensor, ap.offset, [list(ap.ap[0])] + [list(f) for f in free])


def program(nc, t, out, stop=None):
    ctx = ExitStack()
    with ctx:
        build(nc, ctx, t, out, stop)


def build(nc, ctx, t, out, stop):
    sems = {}

    def S(name):
        if name not in sems:
            sems[name] = ctx.enter_context(nc.semaphore(name))
        return sems[name]

    def chain(eng, name):
        n = [0]

        def link(ins):
            n[0] += 1
            ins.then_inc(S(name), 1)
            eng.wait_ge(S(name), n[0])
        return link

    ring = ctx.enter_context(nc.sbuf_tensor("ring", [P, RING * SLOT], F32))
    cst = ctx.enter_context(nc.sbuf_tensor("cst", [P, C_COLS], F32))
    small = ctx.enter_context(nc.sbuf_tensor("small", [P, 640], F32))
    ctrl = ctx.enter_context(nc.sbuf_tensor("ctrl", [P, 72], I32))
    ARENA = 18400
    arena = ctx.enter_context(nc.sbuf_tensor("arena", [P, ARENA], F32))
    PS = ctx.enter_context(nc.psum_tensor("ps", [P, 8, 512], F32))
    scratch = nc.dram_tensor("bias_scratch", [DA_HEADS, LEN_T], F32)

    top = [0]

    def area(cols):
        a = arena[:, top[0]:top[0] + cols]
        top[0] += cols
        assert top[0] <= ARENA, top[0]
        return a

    ident = cst[:, C_ID:C_ID + P]
    X = area(NT * D).rearrange("p (t d) -> p t d", t=NT)
    XT = area(NT * D).rearrange("p (k n) -> p k n", k=KT)
    MARK = top[0]

    def slot(n):
        return ring[:, (n % RING) * SLOT:(n % RING + 1) * SLOT]

    def square(n):
        return slot(n).rearrange("p (k c) -> p k c", k=KT)

    def load_square(sp, n, w):
        rows = w.rearrange("(k p) c -> p k c", p=P)
        for a in range(2):
            sp.dma_start(square(n)[:, 4 * a:4 * a + 4, :], rows[:, 4 * a:4 * a + 4, :]).then_inc(S(f"ring{n % RING}"), 16)

    N_A0, N_M0 = 0, 4
    N_A1 = N_M0 + 48
    N_M1 = N_A1 + 4
    N_B = N_M1 + 48

    def uses(n):
        return n // RING + 1 + (2 * ((n >= N_M0) + (n >= N_M1)) if n % RING < 3 else 0)

    def loaded(eng, n):
        eng.wait_ge(S(f"ring{n % RING}"), PER_SLOT * uses(n))

    TURNS = ("t0", "t1", "m0", "t2", "m1")
    NORMS = ("ln0", "ln1", "ln2", "ln3")

    def pe_turn(pe, src, ntile, tag, ready):
        w = ntile * P
        per_bank = 512 // w
        ready(pe)
        for k in range(KT):
            for tt in range(ntile):
                ins = pe.transpose(PS[:, k // per_bank, (k % per_bank) * w + tt * P:(k % per_bank) * w + (tt + 1) * P],
                                   src[:, tt, k * P:(k + 1) * P], ident)
            if k % per_bank == per_bank - 1:
                ins.then_inc(S("turned"), 1)

    def copy_turn_act(act, dst, tag):
        for b in range(2):
            act.wait_ge(S("turned"), 4 * TURNS.index(tag) + b + 1)
            act.copy(view(dst[:, 2 * b, 0:1], [1, 512]), PS[:, b, :]).then_inc(S("turned_act"), 1)

    def copy_turn_dve(dve, dst, tag):
        for b in range(2, 4):
            dve.wait_ge(S("turned"), 4 * TURNS.index(tag) + b + 1)
            dve.tensor_copy(view(dst[:, 2 * b, 0:1], [1, 512]), PS[:, b, :]).then_inc(S("turned_dve"), 1)

    def turned(eng, tag):
        eng.wait_ge(S("turned_act"), 2 * TURNS.index(tag) + 2)
        eng.wait_ge(S("turned_dve"), 2 * TURNS.index(tag) + 2)

    def pe_columns(pe, w, xT, bank, sem):
        for f in range(KT):
            o = PS[:, bank + f // 2, (f % 2) * 256:(f % 2) * 256 + 256]
            for k in range(KT):
                ins = pe.matmul(o, w[:, k, f * P:(f + 1) * P], xT[:, k, 0:256], start=(k == 0), stop=(k == KT - 1))
            if f % 2:
                ins.then_inc(S(sem), 1)

    def pe_rows(pe, w, xT, bank, sem):
        for tt in range(NT):
            for h in range(2):
                for k in range(KT):
                    ins = pe.matmul(PS[:, bank + 2 * tt + h, :], xT[:, k, tt * P:(tt + 1) * P],
                                    w[:, k, h * 512:(h + 1) * 512], start=(k == 0), stop=(k == KT - 1))
                ins.then_inc(S(sem), 1)

    def dve_layer_norm(dve, link, mix, mix_ready, g, b, params_ready, work, tag):
        xr, st = work
        n0 = NT * NORMS.index(tag)
        mv, sd = small[:, 0:2], small[:, 2:4]
        for tt in range(NT):
            for h in range(2):
                mix_ready(dve, tt, h)
                link(dve.scalar_tensor_tensor(xr[:, h * 512:(h + 1) * 512], X[:, tt, h * 512:(h + 1) * 512], ALPHA,
                                              mix(tt, h), ALU.mult, ALU.add))
                link(dve.bn_stats(st[:, 6 * h:6 * h + 6], xr[:, h * 512:(h + 1) * 512]))
            link(dve.bn_aggr(mv, st[:, 0:12]))
            if tt:
                dve.wait_ge(S("ln_sd"), n0 + tt)
            dve.tensor_scalar(sd[:, 0:1], mv[:, 1:2], LN_EPS, None, ALU.add).then_inc(S("ln_var"), 1)
            dve.wait_ge(S("ln_sd"), n0 + tt + 1)
            link(dve.reciprocal(sd[:, 1:2], sd[:, 1:2]))
            link(dve.tensor_scalar(xr, xr, mv[:, 0:1], sd[:, 1:2], ALU.subtract, ALU.mult))
            if tt == 0:
                params_ready(dve)
            link(dve.tensor_tensor(xr, xr, g, ALU.mult))
            dve.tensor_tensor(X[:, tt, :], xr, b, ALU.add).then_inc(S("ln_out"), 1)
            dve.wait_ge(S("ln_out"), n0 + tt + 1)

    def act_layer_norm(act, tag):
        sd = small[:, 2:4]
        n0 = NT * NORMS.index(tag)
        for tt in range(NT):
            act.wait_ge(S("ln_var"), n0 + tt + 1)
            act.activation(sd[:, 1:2], sd[:, 0:1], ACT.Sqrt).then_inc(S("ln_sd"), 1)

    N_MOD = 6
    mod_rows = nc.dram_tensor("mod_rows", [DEPTH, P, N_MOD, 256], F32)
    mod_buf = arena[:, ARENA - 512:ARENA].rearrange("p (b n) -> p b n", b=2)
    c_rows = arena[0:2 * KT, ARENA - 640:ARENA - 512]
    ccz = small[:, 204:460].rearrange("p (k m) -> p k m", k=KT)
    MOD_PLACE = (0, 1, 0, 2, 1, 2)
    MOD_USE = (0, 0, 1, 0, 1, 1)
    after_mod = lambda l: (("mod", N_MOD * l + 3), ("mod", N_MOD * l + 5), ("mod", N_MOD * l + 6), ("mix", 4 * l + 4))

    def mod_weights(m):
        p = MOD_PLACE[m]
        return ring[:, p * SLOT:(p + 1) * SLOT].rearrange("p (k c) -> p k c", k=KT)

    def mod_sp(sp, l, v_done):
        def load(m, name, v):
            sp.wait_ge(S(name), v)
            rows = t["w_mod_2"][l, :, m * D:(m + 1) * D].rearrange("(k p) c -> p k c", p=P)
            for a in range(2):
                sp.dma_start(mod_weights(m)[:, 4 * a:4 * a + 4, :], rows[:, 4 * a:4 * a + 4, :])\
                  .then_inc(S(f"ring{MOD_PLACE[m]}"), 16)

        def store(m):
            n = N_MOD * l + m
            sp.wait_ge(S("modrow"), n + 1)
            if n:
                sp.wait_ge(S("mod_out"), 16 * n)
            sp.dma_start(mod_rows.ap()[l, :, m, :], mod_buf[:, m % 2, :]).then_inc(S("mod_out"), 16)
        load(0, "q", 4 * l + 4)
        load(1, "k", 4 * l + 4)
        load(2, "mod", N_MOD * l + 1)
        store(0)
        sp.wait_ge(S("v"), 4 * l + 4)
        v_done(sp)
        load(3, "v", 4 * l + 4)
        load(4, "mod", N_MOD * l + 2)
        store(1)
        store(2)
        load(5, "mod", N_MOD * l + 4)
        for m in range(3, N_MOD):
            store(m)

    def mod_pe(pe, l, m, bank, before):
        n = N_MOD * l + m
        pe.wait_ge(S(f"ring{MOD_PLACE[m]}"), PER_SLOT * (uses((N_A0, N_A1)[l] + MOD_PLACE[m]) + 1 + MOD_USE[m]))
        pe.wait_ge(S("cc1"), 2)
        if before is not None:
            pe.wait_ge(S("modrow"), N_MOD * l + before + 1)
        w = mod_weights(m)
        for k in range(KT):
            for j in range(4):
                ins = pe.matmul(PS[32 * j:32 * j + 32, bank, 0:256], ccz[:, k, :], w[:, k, 256 * j:256 * j + 256],
                                start=(k == 0), stop=(k == KT - 1))
        ins.then_inc(S("mod"), 1)

    def mod_dve(dve, l, m, bank):
        n = N_MOD * l + m
        dve.wait_ge(S("mod"), n + 1)
        if n >= 2:
            dve.wait_ge(S("mod_out"), 16 * (n - 1))
        dve.tensor_copy(mod_buf[:, m % 2, :], PS[:, bank, 0:256]).then_inc(S("modrow"), 1)

    top[0] = MARK
    qz = area(2 * KT * 256).rearrange("p (c f n) -> p c f n", c=2, f=KT)
    kT = area(KT * 256).rearrange("p (f n) -> p f n", f=KT)
    V = area(NT * D).rearrange("p (t d) -> p t d", t=NT)
    O = area(NT * D).rearrange("p (t d) -> p t d", t=NT)
    Lg = area(2 * 512).rearrange("p (b c n) -> p b c n", b=2, c=2)
    Ex = area(2 * 512).rearrange("p (b c n) -> p b c n", b=2, c=2)
    At = area(2 * 256).rearrange("p (b n) -> p b n", b=2)
    AtT = area(2 * 256).rearrange("p (b k n) -> p b k n", b=2, k=2)
    bias = XT.rearrange("p k n -> p (k n)").rearrange("p (h n) -> p h n", h=DA_HEADS)
    hot_sb = Ex[0:BUCKETS + 1, 0].rearrange("p c n -> p (c n)")
    rel_sb = Lg[0:BUCKETS + 1, 0, 0, 0:DA_HEADS]
    tab_sb = Lg[0:DA_HEADS, 1].rearrange("p c n -> p (c n)")
    lam4 = At[:, 0, :].rearrange("p (a n) -> p a n", a=4)
    da_g = AtT[:, 0, 0, :]
    lam_s, neg_lam = small[:, 8:12], small[:, 12:13]
    nmax, ssum, rsum = small[:, 16:20], small[:, 20:24], small[:, 24:28]
    o_ss = small[:, 32:48]
    gain = small[:, 64:192]
    lnp = view(qz[:, 0, 0, 0:1], [1, 2048])
    xr = view(qz[:, 1, 0, 0:1], [1, 1024])
    st = small[:, 192:204]
    UNITS = DA_HEADS * NT
    MOD_UNITS = (4, 7, 10)

    def load_ln(sp, gname, bname, layer, dst, sem):
        sp.dma_start(dst[:, 0:D], bass.AP(t[gname].tensor, layer * D, [[0, P], [1, D]])).then_inc(S(sem), 16)
        sp.dma_start(dst[:, D:2 * D], bass.AP(t[bname].tensor, layer * D, [[0, P], [1, D]])).then_inc(S(sem), 16)

    def a0_sp(sp):
        sp.dma_start(X, t["x"].rearrange("b (t p) d -> p (b t) d", p=P)).then_inc(S("x_in"), 16)
        sp.dma_start(cst[:, :], t["consts"]).then_inc(S("consts_in"), 16)
        for v, name in enumerate(("c_2", "c_ctx_2")):
            sp.dma_start(c_rows[KT * v:KT * v + KT, :], bass.AP(t[name].tensor, 0, [[P, KT], [1, P]])).then_inc(S("c_in"), 16)
        sp.dma_start(rel_sb[0:BUCKETS, :], t["rel_table"]).then_inc(S("bias_in"), 16)
        sp.dma_start(hot_sb, t["hot"]).then_inc(S("bias_in"), 16)
        for n, name in enumerate(("da_lq1", "da_lk1", "da_lq2", "da_lk2")):
            sp.dma_start(lam4[:, n, :], bass.AP(t[name].tensor, 0, [[0, P], [1, 64]])).then_inc(S("lam_in"), 16)
        sp.dma_start(gain, bass.AP(t["da_subln_g"].tensor, 0, [[0, P], [1, P]])).then_inc(S("gain_in"), 16)
        load_square(sp, 0, t["da_wq"][0])
        load_square(sp, 1, t["da_wk"][0])
        load_square(sp, 2, t["da_wv"][0])
        load_square(sp, 3, t["da_wo"][0])
        sp.wait_ge(S("tab_sb"), 1)
        sp.dma_start(scratch.ap(), tab_sb).then_inc(S("tab_out"), 16)
        sp.wait_ge(S("tab_out"), 16)
        mod_sp(sp, 0, lambda e: e.dma_start(bias, bass.AP(scratch, P, [[1, P], [LEN_T, DA_HEADS], [1, SEQ]]))
               .then_inc(S("rel_bias"), 16))

    def a0_norm_sp(sp):
        sp.wait_ge(S("scores"), UNITS)
        load_ln(sp, "ln_mix_g", "ln_mix_b", 0, lnp, "ln_in0")

    def a0_pe(pe):
        pe.wait_ge(S("consts_in"), 16)
        pe_turn(pe, X, NT, "t0", lambda e: e.wait_ge(S("x_in"), 16))
        turned(pe, "t0")
        pe.wait_ge(S("bias_in"), 32)
        pe.wait_ge(S("zero"), 3)
        pe.matmul(PS[0:DA_HEADS, 0, :], rel_sb, hot_sb, start=True, stop=True).then_inc(S("tab_ps"), 1)
        pe.wait_ge(S("c_in"), 32)
        pe.transpose(PS[:, 7, 0:2 * KT], c_rows, ident[0:2 * KT, 0:2 * KT]).then_inc(S("cc0"), 1)
        loaded(pe, 0)
        pe.wait_ge(S("cc1"), 2)
        pe_columns(pe, square(0), XT, 4, "q")
        loaded(pe, 1)
        pe.wait_ge(S("tab_sb"), 1)
        pe_columns(pe, square(1), XT, 0, "k")
        pe.wait_ge(S("k_act"), 2)
        pe.wait_ge(S("k_dve"), 2)
        mod_pe(pe, 0, 0, 2, None)
        loaded(pe, 2)
        pe.wait_ge(S("q_act"), 2)
        pe.wait_ge(S("q_dve"), 2)
        pe_rows(pe, square(2), XT, 4, "v")
        mod_pe(pe, 0, 1, 3, None)
        mod_pe(pe, 0, 2, 2, 0)

        def z(u):
            h, i = divmod(u, 2)
            nk = P * (i + 1)
            if u < 2:
                pe.wait_ge(S("v_act"), 2)
                pe.wait_ge(S("v_dve"), 2)
            else:
                pe.wait_ge(S("da_logits"), u - 1)
            for c in range(2):
                ins = pe.matmul(PS[:, 4 + u % 2, c * 256:c * 256 + nk], qz[:, c, h, i * P:(i + 1) * P], kT[:, h, 0:nk],
                                start=True, stop=True)
            ins.then_inc(S("scores"), 1)

        def turn_weights(u):
            pe.wait_ge(S("da_attn"), u + 1)
            if u >= 2:
                pe.wait_ge(S("da_attn_sb"), u - 1)
            for kb in range(u % 2 + 1):
                ins = pe.transpose(PS[:, 6 + u % 2, kb * P:(kb + 1) * P], At[:, u % 2, kb * P:(kb + 1) * P], ident)
            ins.then_inc(S("da_attn_t"), 1)

        def values(u):
            h, i = divmod(u, 2)
            pe.wait_ge(S("da_attn_sb"), u + 1)
            if u >= 2:
                pe.wait_ge(S("values_out"), u - 1)
            for kb in range(i + 1):
                ins = pe.matmul(PS[:, u % 2, 0:P], AtT[:, u % 2, kb, :], V[:, kb, h * P:(h + 1) * P],
                                start=(kb == 0), stop=(kb == i))
            ins.then_inc(S("values"), 1)

        z(0)
        z(1)
        for u in range(UNITS):
            turn_weights(u)
            if u + 2 < UNITS:
                z(u + 2)
            if u in MOD_UNITS:
                m = 3 + MOD_UNITS.index(u)
                mod_pe(pe, 0, m, 2 + m % 2, m - 2)
            if u:
                values(u - 1)
        values(UNITS - 1)
        pe_turn(pe, O, NT, "t1", lambda e: e.wait_ge(S("da_out"), 1))
        loaded(pe, 3)
        turned(pe, "t1")
        pe_rows(pe, square(3), XT, 4, "mix")

    def a0_act(act):
        copy_turn_act(act, XT, "t0")
        act.wait_ge(S("cc0"), 2)
        for v in range(2):
            act.activation(ccz[:, :, v:v + 1], PS[:, 7, KT * v:KT * v + KT].rearrange("p (k m) -> p k m", m=1), ACT.Silu)\
               .then_inc(S("cc1"), 1)
        act.wait_ge(S("tab_ps"), 1)
        act.copy(tab_sb, PS[0:DA_HEADS, 0, :]).then_inc(S("tab_sb"), 1)
        act.wait_ge(S("zero"), 1)

        def heads(bank, sem, out_sem, scale):
            for b in (0, 2):
                act.wait_ge(S(sem), b + 1)
                for c in range(2):
                    if scale:
                        ins = act.mul(qz[64 * c:64 * c + 64, c, 2 * b:2 * b + 2, :],
                                      PS[64 * c:64 * c + 64, bank + b, :].rearrange("p (f n) -> p f n", f=2), 0.125)
                if not scale:
                    ins = act.copy(kT[:, 2 * b:2 * b + 2, :], PS[:, bank + b, :].rearrange("p (f n) -> p f n", f=2))
                ins.then_inc(S(out_sem), 1)
        heads(4, "q", "q_act", True)
        heads(0, "k", "k_act", False)
        for b in range(2):
            act.wait_ge(S("v"), 2 * b + 1)
            act.copy(V[:, b, 0:512], PS[:, 4 + 2 * b, :]).then_inc(S("v_act"), 1)
        act.wait_ge(S("lam_dot"), 1)
        act.activation(lam_s[:, 2:4], lam_s[:, 0:2], ACT.Exp).then_inc(S("lam_exp"), 1)

        def expo(u):
            nk = P * (u % 2 + 1)
            act.wait_ge(S("da_max"), u + 1)
            if u >= 2:
                act.wait_ge(S("da_attn"), u - 1)
            for c in range(2):
                ins = act.activation(Ex[:, u % 2, c, 0:nk], Lg[:, u % 2, c, 0:nk], ACT.Exp,
                                     bias=nmax[:, 2 * (u % 2) + c:2 * (u % 2) + c + 1],
                                     accum_out=ssum[:, 2 * (u % 2) + c:2 * (u % 2) + c + 1])
            ins.then_inc(S("da_exp"), 1)

        def output(u):
            h, i = divmod(u, 2)
            act.wait_ge(S("values"), u + 1)
            act.copy(O[:, i, h * P:(h + 1) * P], PS[:, u % 2, 0:P]).then_inc(S("values_out"), 1)

        expo(0)
        for u in range(UNITS):
            if u + 1 < UNITS:
                expo(u + 1)
            i = u % 2
            act.wait_ge(S("da_attn_t"), u + 1)
            if u >= 2:
                act.wait_ge(S("values"), u - 1)
            act.copy(view(AtT[:, u % 2, 0, 0:1], [1, P * (i + 1)]), PS[:, 6 + u % 2, 0:P * (i + 1)]).then_inc(S("da_attn_sb"), 1)
            if u:
                output(u - 1)
        output(UNITS - 1)
        act.wait_ge(S("da_ms"), 1)
        act.activation(o_ss, o_ss, ACT.Sqrt).then_inc(S("da_sd"), 1)
        copy_turn_act(act, XT, "t1")
        act_layer_norm(act, "ln0")

    def a0_dve(dve, link):
        dve.memset(view(qz[:, 0, 0, 0:1], [1, 4096]), 0.0).then_inc(S("zero"), 1)
        dve.memset(rel_sb[BUCKETS:BUCKETS + 1, :], NEG).then_inc(S("zero"), 2)
        dve.memset(view(ccz[:, 0, 0:1], [1, 256]), 0.0).then_inc(S("cc0"), 1)
        copy_turn_dve(dve, XT, "t0")
        dve.wait_ge(S("lam_in"), 64)
        link(dve.tensor_tensor(lam4[:, 0:3:2, :], lam4[:, 0:3:2, :], lam4[:, 1:4:2, :], ALU.mult))
        dve.tensor_reduce(lam_s[:, 0:2], lam4[:, 0:3:2, :], AX.X, ALU.add).then_inc(S("lam_dot"), 1)
        dve.wait_ge(S("zero"), 1)
        for b in (1, 3):
            dve.wait_ge(S("q"), b + 1)
            for c in range(2):
                ins = dve.tensor_scalar(qz[64 * c:64 * c + 64, c, 2 * b:2 * b + 2, :],
                                        PS[64 * c:64 * c + 64, 4 + b, :].rearrange("p (f n) -> p f n", f=2), 0.125, None, ALU.mult)
            ins.then_inc(S("q_dve"), 1)
        for b in (1, 3):
            dve.wait_ge(S("k"), b + 1)
            dve.tensor_copy(kT[:, 2 * b:2 * b + 2, :], PS[:, b, :].rearrange("p (f n) -> p f n", f=2)).then_inc(S("k_dve"), 1)
        mod_dve(dve, 0, 0, 2)
        for b in range(2):
            dve.wait_ge(S("v"), 2 * b + 2)
            dve.tensor_copy(V[:, b, 512:1024], PS[:, 5 + 2 * b, :]).then_inc(S("v_dve"), 1)
        mod_dve(dve, 0, 1, 3)
        mod_dve(dve, 0, 2, 2)
        dve.wait_ge(S("lam_exp"), 1)
        link(dve.tensor_tensor(neg_lam, lam_s[:, 3:4], lam_s[:, 2:3], ALU.subtract))
        link(dve.tensor_scalar(neg_lam, neg_lam, -LAM_INIT, None, ALU.add))
        dve.wait_ge(S("tab_out"), 16)

        def logits(u):
            h, i = divmod(u, 2)
            nk = P * (i + 1)
            dve.wait_ge(S("scores"), u + 1)
            if u == 0:
                dve.wait_ge(S("rel_bias"), 16)
            if u >= 2:
                dve.wait_ge(S("da_exp"), u - 1)
            b = view(bias[:, h, P * i + P - 1:P * i + P], [0, 2], [-1, nk])
            dve.tensor_tensor(Lg[:, u % 2, :, 0:nk], PS[:, 4 + u % 2, :].rearrange("p (c n) -> p c n", c=2)[:, :, 0:nk], b,
                              ALU.add).then_inc(S("da_logits"), 1)
            dve.wait_ge(S("da_logits"), u + 1)
            dve.tensor_reduce(nmax[:, 2 * (u % 2):2 * (u % 2) + 2], Lg[:, u % 2, :, 0:nk], AX.X, ALU.max,
                              negate=True).then_inc(S("da_max"), 1)

        def combine(u):
            i = u % 2
            nk = P * (i + 1)
            b = 2 * (u % 2)
            dve.wait_ge(S("da_exp"), u + 1)
            link(dve.reciprocal(rsum[:, b:b + 2], ssum[:, b:b + 2]))
            link(dve.tensor_scalar(rsum[:, b + 1:b + 2], rsum[:, b + 1:b + 2], neg_lam, None, ALU.mult))
            link(dve.tensor_scalar(Ex[:, u % 2, 1, 0:nk], Ex[:, u % 2, 1, 0:nk], rsum[:, b + 1:b + 2], None, ALU.mult))
            if u >= 2:
                dve.wait_ge(S("da_attn_t"), u - 1)
            dve.scalar_tensor_tensor(At[:, u % 2, 0:nk], Ex[:, u % 2, 0, 0:nk], rsum[:, b:b + 1], Ex[:, u % 2, 1, 0:nk],
                                     ALU.mult, ALU.add).then_inc(S("da_attn"), 1)

        logits(0)
        for u in range(UNITS):
            if u + 1 < UNITS:
                logits(u + 1)
            combine(u)
            if u - 1 in MOD_UNITS:
                m = 3 + MOD_UNITS.index(u - 1)
                mod_dve(dve, 0, m, 2 + m % 2)
        dve.wait_ge(S("values_out"), UNITS)
        sq = view(kT[:, 0, 0:1], [1, 2048])
        Of = view(O[:, 0, 0:1], [1, 2048])
        link(dve.tensor_tensor(sq, Of, Of, ALU.mult))
        link(dve.tensor_reduce(o_ss, sq.rearrange("p (h e) -> p h e", e=P), AX.X, ALU.add))
        dve.tensor_scalar(o_ss, o_ss, 1.0 / P, RMS_EPS, ALU.mult, ALU.add).then_inc(S("da_ms"), 1)
        dve.wait_ge(S("gain_in"), 16)
        link(dve.tensor_scalar(gain, gain, 1.0 - LAM_INIT, None, ALU.mult))
        dve.wait_ge(S("da_sd"), 1)
        link(dve.reciprocal(o_ss, o_ss))
        Oh = Of.rearrange("p (h e) -> p h e", e=P)
        link(dve.tensor_tensor(Oh, Oh, view(o_ss[:, 0:1], [1, 16], [0, P]), ALU.mult))
        dve.tensor_tensor(Oh, Oh, view(gain[:, 0:1], [0, 16], [1, P]), ALU.mult).then_inc(S("da_out"), 1)
        copy_turn_dve(dve, XT, "t1")
        dve_layer_norm(dve, link, lambda tt, h: PS[:, 4 + 2 * tt + h, :],
                       lambda e, tt, h: e.wait_ge(S("mix"), 2 * tt + h + 1),
                       lnp[:, 0:D], lnp[:, D:2 * D], lambda e: e.wait_ge(S("ln_in0"), 32), (xr, st), "ln0")

    CAP = 64
    PAIRS = N_EXPERTS // 2
    UNROLL = 4
    MOE_BASE = MARK + 4096

    def moe(layer, tag, n0, params_free, first_free, ln_tag, x_ready, norm_sp):
        top[0] = MOE_BASE
        s = lambda name: S(f"moe_{name}")
        wr = area(KT * 36).rearrange("p (k n) -> p k n", k=KT)
        brow = area(36)
        lnp = area(2 * D)
        xr = area(D)
        ones = area(P)
        zeros = area(512)
        lg = area(72).rearrange("p (t n) -> p t n", t=NT)
        g4a, g4b = area(8).rearrange("p (t n) -> p t n", t=NT), area(8).rearrange("p (t n) -> p t n", t=NT)
        desc = area(32)
        M, oh1, oh2, tmp, mask, gates, rank = (area(64).rearrange("p (t n) -> p t n", t=NT) for _ in range(7))
        c2 = area(32)
        col = lambda n: c2[:, 2 * n:2 * n + 2]
        gmax, gsum, tm, m1, m2, ex, wa, wb = (col(n) for n in range(8))
        pm, rounds, base = area(16), area(16), area(17)
        sel = area(256).rearrange("p (t e c) -> p t e c", t=NT, e=2)
        selg = area(256).rearrange("p (t s) -> p t s", t=NT)
        sgT = area(256)
        xeT = area(KT * P).rearrange("p (k s) -> p k s", k=KT)
        hs, hh = area(HIDDEN), area(HIDDEN)
        hT = area(512).rearrange("p (k s) -> p k s", k=4)
        Y = area(D)
        st = small[:, 192:204]
        cR, cB = 36 * layer, 36 * layer + 16
        b2 = lambda a, n: view(a, [1, NT], [0, n])

        w_up = lambda name, e: t[name][layer, e, :, :].rearrange("a (k p) n -> p (a k) n", p=P)

        def load(sp, n, name, p):
            dst = ring[:, (n % RING) * SLOT:(n % RING + 1) * SLOT].rearrange("p (e k n) -> p e k n", e=2, k=4 if name == "moe_w2" else KT)
            for e in range(2):
                sp.dma_start(dst[:, e], w_up(name, bass.ds(2 * p + e, 1))).then_inc(S(f"ring{n % RING}"), 16)

        def sp_(sp):
            for c in range(3):
                load(sp, *first(sp, c))
            norm_sp(sp)
            params_free(sp)
            sp.dma_start(wr[:, :, 0:GROUPS], t["moe_w_group"][layer].rearrange("(k p) n -> p k n", p=P)).then_inc(s("router_in"), 16)
            sp.dma_start(wr[:, :, GROUPS:36], t["moe_w_expert"][layer].rearrange("(k p) n -> p k n", p=P)).then_inc(s("router_in"), 16)
            sp.dma_start(brow[:, 0:GROUPS], bass.AP(t["moe_b_group"].tensor, layer * GROUPS, [[0, P], [1, GROUPS]])).then_inc(s("router_in"), 16)
            sp.dma_start(brow[:, GROUPS:36], bass.AP(t["moe_b_expert"].tensor, layer * N_EXPERTS, [[0, P], [1, N_EXPERTS]])).then_inc(s("router_in"), 16)
            load_ln(sp, "ln_ffn_g", "ln_ffn_b", layer, lnp, "ln_in1")
            load(sp, *first(sp, 3))
            sp.wait_ge(s("ctrl"), layer + 1)

            def step(sp, p, o):
                done = sp.value_load(ctrl[0:1, bass.ds(cB + p, 1)], min_val=1, max_val=128)
                sp.wait_ge(s("h1"), done)
                load(sp, n0 + o + 1, "moe_w3", p)
                sp.wait_ge(s("h3"), done)
                load(sp, n0 + o + 2, "moe_w2", p)
                return done
            with sp.Fori(0, PAIRS // UNROLL - 1) as it:
                for j in range(1, UNROLL + 1):
                    done = step(sp, it * UNROLL + j, 3 * j)
                    sp.wait_ge(s("y"), done)
                    load(sp, n0 + 3 * j + 3, "moe_w1", it * UNROLL + j + 1)
            for p in range(PAIRS - UNROLL + 1, PAIRS):
                done = step(sp, p, 3 * p)
                if p + 1 < PAIRS:
                    sp.wait_ge(s("y"), done)
                    load(sp, n0 + 3 * p + 3, "moe_w1", p + 1)

        def first(sp, c):
            sp.wait_ge(S(first_free[c][0]), first_free[c][1])
            return n0 + c, ("moe_w1", "moe_w3", "moe_w2")[c % 3], c // 3

        def freed(sp, c):
            total = sp.value_load(ctrl[0:1, cB + PAIRS - (c == 0):cB + PAIRS - (c == 0) + 1], min_val=1, max_val=128)
            sp.wait_ge(s(("y", "h1", "h3", "y")[c]), total)

        def for_rounds(eng, body):
            eng.wait_ge(s("ctrl"), layer + 1)
            with eng.Fori(0, PAIRS // UNROLL) as it:
                for j in range(UNROLL):
                    n_rounds = eng.value_load(ctrl[0:1, bass.ds(it * UNROLL + (cR + j), 1)], min_val=1, max_val=4)
                    before = eng.value_load(ctrl[0:1, bass.ds(it * UNROLL + (cB + j), 1)], min_val=0, max_val=128)
                    with eng.Fori(0, n_rounds) as r:
                        body(j, it, r, before + r)

        def pe_(pe):
            pe_turn(pe, X, NT, tag, x_ready)
            pe.wait_ge(s("router_in"), 64 * layer + 64)
            turned(pe, tag)
            for tt in range(NT):
                for k in range(KT):
                    ins = pe.matmul(PS[:, 0, 36 * tt:36 * tt + 36], XT[:, k, tt * P:(tt + 1) * P], wr[:, k, :],
                                    start=(k == 0), stop=(k == KT - 1))
            ins.then_inc(s("router_ps"), 1)
            pe.wait_ge(s("mask"), layer + 1)
            lt = cst[:, C_LT:C_LT + P]
            for o, terms in ((0, ((lt, 0),)), (32, ((ones, 0), (lt, 1))), (64, ((ones, 0), (ones, 1)))):
                for a, (w, tt) in enumerate(terms):
                    ins = pe.matmul(PS[:, 1, o:o + 32], w, mask[:, tt, :], start=(a == 0), stop=(a == len(terms) - 1))
            ins.then_inc(s("router_ps"), 1)
            for b in range(4):
                ins = pe.matmul(PS[:, 4 + b, :], zeros[:, 0:P], zeros, start=True, stop=False, skip_group_check=True)
            ins.then_inc(s("sgT_ps"), 1)

            def scatter(last=False):
                for tt in range(NT):
                    for h in range(2):
                        ins = pe.matmul(PS[:, 4 + 2 * tt + h, :], sgT[:, tt * P:(tt + 1) * P], Y[:, h * 512:(h + 1) * 512],
                                        start=False, stop=last, skip_group_check=True)
                return ins

            def body(j, it, r, g):
                w = [slot(n0 + 3 * j + c).rearrange("p (e k n) -> p e k n", e=2, k=(KT, KT, 4)[c]) for c in range(3)]

                def arrived(c):
                    pe.wait_ge(S(f"ring{(n0 + 3 * j + c) % RING}"),
                               it * (3 * PER_SLOT) + PER_SLOT * uses(n0 + 3 * j + c))
                pe.wait_ge(s("sel"), g + 1)
                pe.wait_ge(s("y_act"), g + (1 + layer))
                pe.wait_ge(s("y_dve"), g + (1 + layer))
                for k in range(KT):
                    for tt in range(NT):
                        ins = pe.matmul(PS[:, k // 4, (k % 4) * P:(k % 4 + 1) * P], X[:, tt, k * P:(k + 1) * P],
                                        view(sel[:, tt, 0, 0:1], [1, P]), start=(tt == 0), stop=(tt == NT - 1))
                    if k == 3:
                        ins.then_inc(s("xe"), 1)
                ins.then_inc(s("xe"), 1)
                scatter()
                for tt in range(NT):
                    ins = pe.transpose(PS[:, 3, tt * P:(tt + 1) * P], selg[:, tt, :], ident)
                ins.then_inc(s("sgT_ps"), 1)
                pe.wait_ge(s("xe_act"), g + 1)
                pe.wait_ge(s("xe_dve"), g + 1)
                for c, sem in ((0, "h1"), (1, "h3")):
                    arrived(c)
                    if c == 1:
                        pe.wait_ge(s("sgT"), g + (2 + layer))
                    for k in range(KT):
                        for e in range(2):
                            ins = pe.matmul(PS[CAP * e:CAP * e + CAP, 2 + c, :], xeT[:, k, CAP * e:CAP * e + CAP], w[c][:, e, k, :],
                                            start=(k == 0), stop=(k == KT - 1))
                    ins.then_inc(s(sem), 1)
                pe.wait_ge(s("h"), g + 1)
                for k in range(4):
                    ins = pe.transpose(PS[:, 2, k * P:(k + 1) * P], hh[:, k * P:(k + 1) * P], ident)
                ins.then_inc(s("hT_ps"), 1)
                pe.wait_ge(s("hT"), g + 1)
                arrived(2)
                for h in range(2):
                    for k in range(4):
                        for e in range(2):
                            ins = pe.matmul(PS[CAP * e:CAP * e + CAP, h, :], hT[:, k, CAP * e:CAP * e + CAP],
                                            w[2][:, e, k, h * 512:(h + 1) * 512], start=(k == 0), stop=(k == 3))
                    if h == 0:
                        ins.then_inc(s("y_half"), 1)
                ins.then_inc(s("y"), 1)
            for_rounds(pe, body)
            total = pe.value_load(ctrl[0:1, cB + PAIRS:cB + PAIRS + 1], min_val=1, max_val=128)
            pe.wait_ge(s("y_act"), total + (1 + layer))
            pe.wait_ge(s("y_dve"), total + (1 + layer))
            scatter(last=True).then_inc(s("done"), 1)

        def act_(act):
            copy_turn_act(act, XT, tag)
            act.wait_ge(s("router_arg"), 2 * layer + 1)
            act.activation(g4a, g4a, ACT.Exp).then_inc(s("router_exp"), 1)
            act.wait_ge(s("router_arg"), 2 * layer + 2)
            act.activation(ex, ex, ACT.Exp).then_inc(s("router_exp"), 1)
            act.wait_ge(s("zeros"), layer + 1)
            act.copy(sgT, view(zeros, [1, 256])).then_inc(s("sgT"), 1)
            act.copy(Y[:, 0:512], zeros).then_inc(s("y_act"), 1)

            def body(j, it, r, g):
                act.wait_ge(s("xe"), g * 2 + 1)
                act.copy(view(xeT[:, 0, 0:1], [1, 512]), PS[:, 0, :]).then_inc(s("xe_act"), 1)
                act.wait_ge(s("sgT_ps"), g + (2 + layer))
                act.copy(sgT, PS[:, 3, 0:256]).then_inc(s("sgT"), 1)
                act.wait_ge(s("h1"), g + 1)
                act.activation(hs, PS[:, 2, :], ACT.Silu).then_inc(s("silu"), 1)
                act.wait_ge(s("hT_ps"), g + 1)
                act.copy(view(hT[:, 0, 0:1], [1, 512]), PS[:, 2, :]).then_inc(s("hT"), 1)
                act.wait_ge(s("y_half"), g + 1)
                act.copy(Y[:, 0:512], PS[:, 0, :]).then_inc(s("y_act"), 1)
            for_rounds(act, body)
            act_layer_norm(act, ln_tag)

        def dve_(dve, link):
            params_free(dve)
            link(dve.memset(ones, 1.0))
            dve.memset(zeros, 0.0).then_inc(s("zeros"), 1)
            dve.wait_ge(s("zeros"), layer + 1)
            dve.tensor_copy(Y[:, 512:D], zeros).then_inc(s("y_dve"), 1)
            link(dve.tensor_scalar(desc, cst[:, C_IOTA:C_IOTA + 32], -1.0, 32.0, ALU.mult, ALU.add))
            copy_turn_dve(dve, XT, tag)
            dve.wait_ge(s("router_in"), 64 * layer + 64)
            dve.wait_ge(s("router_ps"), 2 * layer + 1)
            link(dve.tensor_tensor(lg, PS[:, 0, 0:72].rearrange("p (t n) -> p t n", t=NT), view(brow, [0, NT], [1, 36]), ALU.add))
            l4 = lg[:, :, 0:GROUPS]
            link(dve.tensor_reduce(gmax, l4, AX.X, ALU.max))
            dve.tensor_tensor(g4a, l4, b2(gmax, 4), ALU.subtract).then_inc(s("router_arg"), 1)
            link(dve.tensor_tensor(g4b, l4, b2(gmax, 4), ALU.is_ge))
            link(dve.tensor_tensor(g4b, g4b, view(desc, [0, NT], [1, 4]), ALU.mult))
            link(dve.tensor_reduce(tm, g4b, AX.X, ALU.max))
            link(dve.tensor_tensor(g4b, g4b, b2(tm, 4), ALU.is_equal))
            link(dve.tensor_scalar(g4b, g4b, -NEG, NEG, ALU.mult, ALU.add))
            link(dve.tensor_tensor(M.rearrange("p t (g e) -> p t g e", g=GROUPS),
                                   lg[:, :, GROUPS:36].rearrange("p t (g e) -> p t g e", g=GROUPS),
                                   view(g4b[:, 0, 0:1], [4, NT], [1, GROUPS], [0, PER_GROUP]), ALU.add))

            def best(top_val, onehot):
                link(dve.tensor_reduce(top_val, M, AX.X, ALU.max))
                link(dve.tensor_tensor(onehot, M, b2(top_val, 32), ALU.is_ge))
                link(dve.tensor_tensor(onehot, onehot, view(desc, [0, NT], [1, 32]), ALU.mult))
                link(dve.tensor_reduce(tm, onehot, AX.X, ALU.max))
                link(dve.tensor_tensor(onehot, onehot, b2(tm, 32), ALU.is_equal))
            best(m1, oh1)
            link(dve.scalar_tensor_tensor(M, oh1, NEG, M, ALU.mult, ALU.add))
            best(m2, oh2)
            dve.tensor_tensor(ex, m2, m1, ALU.subtract).then_inc(s("router_arg"), 1)
            dve.tensor_tensor(mask, oh1, oh2, ALU.add).then_inc(s("mask"), 1)
            dve.wait_ge(s("router_exp"), 2 * layer + 1)
            link(dve.tensor_reduce(gsum, g4a, AX.X, ALU.add))
            dve.wait_ge(s("router_exp"), 2 * layer + 2)
            link(dve.scalar_tensor_tensor(gsum, ex, 1.0, gsum, ALU.add, ALU.mult))
            link(dve.reciprocal(wa, gsum))
            link(dve.tensor_tensor(wb, wa, ex, ALU.mult))
            link(dve.tensor_tensor(oh1, oh1, b2(wa, 32), ALU.mult))
            link(dve.tensor_tensor(oh2, oh2, b2(wb, 32), ALU.mult))
            link(dve.tensor_tensor(gates, oh1, oh2, ALU.add))
            dve.wait_ge(s("router_ps"), 2 * layer + 2)
            link(dve.scalar_tensor_tensor(rank, PS[:, 1, 0:64].rearrange("p (t n) -> p t n", t=NT), 1.0, mask, ALU.add, ALU.mult))
            link(dve.tensor_scalar(rank, rank, -1.0, None, ALU.add))
            link(dve.tensor_reduce(pm, PS[:, 1, 64:96].rearrange("p (a e) -> p a e", e=2), AX.X, ALU.max))
            link(dve.tensor_scalar(rounds, pm, CAP + 0.5, 1.0, ALU.is_gt, ALU.add))
            for m in range(2, SEQ // CAP):
                link(dve.scalar_tensor_tensor(rounds, pm, m * CAP + 0.5, rounds, ALU.is_gt, ALU.add))
            if layer:
                link(dve.tensor_copy(base[:, 0:1], ctrl[:, cB - 36 + PAIRS:cB - 36 + PAIRS + 1]))
            else:
                link(dve.memset(base[:, 0:1], 0.0))
            link(dve.tensor_tensor_scan(base[:, 1:17], ones[:, 0:16], rounds, base[:, 0:1], ALU.mult, ALU.add))
            link(dve.tensor_copy(ctrl[:, cR:cR + 16], rounds))
            dve.tensor_copy(ctrl[:, cB:cB + 17], base).then_inc(s("ctrl"), 1)

            def body(j, it, r, g):
                pair = it * (2 * UNROLL) + 2 * j
                dve.wait_ge(s("sgT_ps"), g + (1 + layer))
                slots = cst[:, bass.ds(r * CAP + C_IOTA, CAP)]
                for tt in range(NT):
                    ins = dve.tensor_tensor(sel[:, tt], view(rank[:, tt, bass.ds(pair, 2)], [1, 2], [0, CAP]),
                                            view(slots, [0, 2], [1, CAP]), ALU.is_equal)
                    ins.then_inc(s("eq"), 1)
                dve.wait_ge(s("eq"), g * 2 + 2)
                for tt in range(NT):
                    ins = dve.tensor_tensor(selg[:, tt, :].rearrange("p (e c) -> p e c", e=2), sel[:, tt],
                                            view(gates[:, tt, bass.ds(pair, 2)], [1, 2], [0, CAP]), ALU.mult)
                ins.then_inc(s("sel"), 1)
                dve.wait_ge(s("xe"), g * 2 + 2)
                dve.tensor_copy(view(xeT[:, 4, 0:1], [1, 512]), PS[:, 1, :]).then_inc(s("xe_dve"), 1)
                dve.wait_ge(s("silu"), g + 1)
                dve.wait_ge(s("h3"), g + 1)
                dve.tensor_tensor(hh, PS[:, 3, :], hs, ALU.mult).then_inc(s("h"), 1)
                dve.wait_ge(s("y"), g + 1)
                dve.tensor_copy(Y[:, 512:D], PS[:, 1, :]).then_inc(s("y_dve"), 1)

            for_rounds(dve, body)
            dve_layer_norm(dve, link, lambda tt, h: PS[:, 4 + 2 * tt + h, :],
                           lambda e, tt, h: e.wait_ge(s("done"), layer + 1),
                           lnp[:, 0:D], lnp[:, D:2 * D], lambda e: e.wait_ge(S("ln_in1"), 32 * layer + 32), (xr, st), ln_tag)

        return {"sp": sp_, "pe": pe_, "act": act_, "dve": dve_, "freed": freed}

    m0 = moe(0, "m0", N_M0, lambda e: e.wait_ge(S("da_out"), 1),
             after_mod(0), "ln1", lambda e: e.wait_ge(S("ln_out"), 2), a0_norm_sp)

    top[0] = MARK
    qz1 = area(2 * KT * 256).rearrange("p (c f n) -> p c f n", c=2, f=KT)
    kT1 = area(KT * 256).rearrange("p (f n) -> p f n", f=KT)
    V1 = area(NT * D).rearrange("p (t d) -> p t d", t=NT)
    ZB = (0, 2, 6)
    ONE_SB = 384
    lnv = area(2 * 2 * ONE_SB).rearrange("p (b c n) -> p b c n", b=2, c=2)
    spv = area(2 * 2 * ONE_SB).rearrange("p (b c n) -> p b c n", b=2, c=2)
    wT = area(2 * 2 * ONE_SB).rearrange("p (b c n) -> p b c n", b=2, c=2)
    ones1 = area(P)
    lnp1 = view(qz1[:, 0, 0, 0:1], [1, 2048])
    xr1 = view(qz1[:, 1, 0, 0:1], [1, 1024])

    def a1_sp(sp):
        for c, name in enumerate(("sb_wq", "sb_wk", "sb_wv", "sb_wo")):
            m0["freed"](sp, c)
            load_square(sp, N_A1 + c, t[name][0])
        mod_sp(sp, 1, lambda e: None)

    def a1_norm_sp(sp):
        sp.wait_ge(S("scores"), 16 + KT)
        load_ln(sp, "ln_mix_g", "ln_mix_b", 1, lnp1, "ln_in0")

    def a1_pe(pe):
        pe_turn(pe, X, NT, "t2", lambda e: e.wait_ge(S("ln_out"), 4))
        loaded(pe, N_A1)
        turned(pe, "t2")
        pe_columns(pe, square(N_A1), XT, 4, "q")
        loaded(pe, N_A1 + 1)
        pe_columns(pe, square(N_A1 + 1), XT, 0, "k")
        pe.wait_ge(S("k_act"), 2 + 2)
        pe.wait_ge(S("k_dve"), 2 + 2)
        mod_pe(pe, 1, 0, 2, None)
        loaded(pe, N_A1 + 2)
        pe.wait_ge(S("q_act"), 2 + 2)
        pe.wait_ge(S("q_dve"), 2 + 2)
        pe_rows(pe, square(N_A1 + 2), XT, 4, "v")
        mod_pe(pe, 1, 1, 3, None)
        mod_pe(pe, 1, 2, 2, 0)
        negd, nge = cst[:, C_NEGD:C_NEGD + P], cst[:, C_NGE:C_NGE + P]

        def z(f):
            if f == 1:
                pe.wait_ge(S("modrow"), N_MOD + 3)
            if f == 2:
                pe.wait_ge(S("v_act"), 2 + 2)
                pe.wait_ge(S("v_dve"), 2 + 2)
            if f >= 3:
                pe.wait_ge(S("sb_w"), f - 2)
            for c in range(2):
                b = PS[:, ZB[f % 3] + c, :]
                pe.matmul(b[:, 0:256], kT1[:, f, 0:P], qz1[:, c, f, :], start=True, stop=False, skip_group_check=True)
                pe.matmul(b[:, 256:384], kT1[:, f, P:2 * P], qz1[:, c, f, P:2 * P], start=False, stop=False, skip_group_check=True)
                pe.matmul(b[:, 0:P], ident, negd, start=False, stop=False, skip_group_check=True)
                ins = pe.matmul(b[:, 256:384], ident, negd, start=False, stop=False, skip_group_check=True)
            ins.then_inc(S("scores"), 1)

        def cumulate(f):
            pe.wait_ge(S("sb_soft"), f + 1)
            for c in range(2):
                b, s_ = PS[:, ZB[f % 3] + c, :], spv[:, f % 2, c, :]
                pe.matmul(b[:, 0:384], nge, s_, start=False, stop=False, skip_group_check=True)
                ins = pe.matmul(b[:, P:256], ones1, s_[:, 256:384], start=False, stop=True, skip_group_check=True)
            ins.then_inc(S("sb_cum"), 1)

        def pv(f):
            pe.wait_ge(S("sb_w"), f + 1)
            if f == 0:
                pe.wait_ge(S("v_act"), 2 + 2)
                pe.wait_ge(S("v_dve"), 2 + 2)
            if f:
                pe.wait_ge(S("values_out"), 16 + f)
            for c in range(2):
                o = PS[64 * c:64 * c + 64, 4, 0:256]
                vcol = (2 * f + c) * 64
                pe.matmul(o, V1[:, 0, vcol:vcol + 64], wT[:, f % 2, c, 0:256], start=True, stop=False, skip_group_check=True)
                ins = pe.matmul(o[:, P:256], V1[:, 1, vcol:vcol + 64], wT[:, f % 2, c, 256:384], start=False, stop=True,
                                skip_group_check=True)
            ins.then_inc(S("values"), 1)

        z(0)
        z(1)
        for f in range(KT):
            cumulate(f)
            if f + 2 < KT:
                z(f + 2)
            if f in (2, 4, 6):
                m = 2 + f // 2
                mod_pe(pe, 1, m, 5, m - 1)
            if f:
                pv(f - 1)
        pv(KT - 1)
        loaded(pe, N_A1 + 3)
        pe.wait_ge(S("values_out"), 16 + KT)
        pe_rows(pe, square(N_A1 + 3), XT, 4, "mix")

    def a1_act(act):
        copy_turn_act(act, XT, "t2")
        act.wait_ge(S("zero"), 2 + 1)
        for b in (0, 2):
            act.wait_ge(S("q"), 4 + b + 1)
            for c in range(2):
                ins = act.mul(qz1[64 * c:64 * c + 64, c, 2 * b:2 * b + 2, :],
                              PS[64 * c:64 * c + 64, 4 + b, :].rearrange("p (f n) -> p f n", f=2), 0.125)
            ins.then_inc(S("q_act"), 1)
        for b in (0, 2):
            act.wait_ge(S("k"), 4 + b + 1)
            act.copy(kT1[:, 2 * b:2 * b + 2, :], PS[:, b, :].rearrange("p (f n) -> p f n", f=2)).then_inc(S("k_act"), 1)
        for b in range(2):
            act.wait_ge(S("v"), 4 + 2 * b + 1)
            act.copy(V1[:, b, 0:512], PS[:, 4 + 2 * b, :]).then_inc(S("v_act"), 1)

        def softlog(f):
            l = lnv[:, f % 2]
            act.wait_ge(S("scores"), 16 + f + 1)
            if f >= 2:
                act.wait_ge(S("sb_soft"), f - 1)
            act.activation(l, PS[:, ZB[f % 3]:ZB[f % 3] + 2, 0:384], ACT.Abs).then_inc(S("sb_abs"), 1)
            act.wait_ge(S("sb_abs"), f + 1)
            act.activation(l, l, ACT.Exp, scale=-1.0).then_inc(S("sb_e"), 1)
            act.wait_ge(S("sb_e"), f + 1)
            act.activation(l, l, ACT.Ln, bias=1.0).then_inc(S("sb_ln"), 1)

        softlog(0)
        for f in range(KT):
            if f + 1 < KT:
                softlog(f + 1)
            act.wait_ge(S("sb_cum"), f + 1)
            if f >= 2:
                act.wait_ge(S("values"), 16 + f - 1)
            act.activation(wT[:, f % 2], PS[:, ZB[f % 3]:ZB[f % 3] + 2, 0:384], ACT.Exp).then_inc(S("sb_w"), 1)
        act_layer_norm(act, "ln2")

    def a1_dve(dve, link):
        dve.memset(view(qz1[:, 0, 0, 0:1], [1, 4096]), 0.0).then_inc(S("zero"), 1)
        copy_turn_dve(dve, XT, "t2")
        link(dve.memset(ones1, -1.0))
        dve.wait_ge(S("zero"), 2 + 1)
        for b in (1, 3):
            dve.wait_ge(S("q"), 4 + b + 1)
            for c in range(2):
                ins = dve.tensor_scalar(qz1[64 * c:64 * c + 64, c, 2 * b:2 * b + 2, :],
                                        PS[64 * c:64 * c + 64, 4 + b, :].rearrange("p (f n) -> p f n", f=2), 0.125, None, ALU.mult)
            ins.then_inc(S("q_dve"), 1)
        for b in (1, 3):
            dve.wait_ge(S("k"), 4 + b + 1)
            dve.tensor_copy(kT1[:, 2 * b:2 * b + 2, :], PS[:, b, :].rearrange("p (f n) -> p f n", f=2)).then_inc(S("k_dve"), 1)
        mod_dve(dve, 1, 0, 2)
        for b in range(2):
            dve.wait_ge(S("v"), 4 + 2 * b + 2)
            dve.tensor_copy(V1[:, b, 512:1024], PS[:, 5 + 2 * b, :]).then_inc(S("v_dve"), 1)
        mod_dve(dve, 1, 1, 3)
        mod_dve(dve, 1, 2, 2)

        def outputs(f):
            dve.wait_ge(S("values"), 16 + f + 1)
            dve.tensor_copy(XT[:, f, :], PS[:, 4, 0:256]).then_inc(S("values_out"), 1)

        for f in range(KT):
            dve.wait_ge(S("sb_ln"), f + 1)
            if f >= 2:
                dve.wait_ge(S("sb_cum"), f - 1)
            dve.scalar_tensor_tensor(spv[:, f % 2], PS[:, ZB[f % 3]:ZB[f % 3] + 2, 0:384], 0.0, lnv[:, f % 2],
                                     ALU.max, ALU.add).then_inc(S("sb_soft"), 1)
            if f >= 2:
                outputs(f - 2)
            if f in (3, 5, 7):
                mod_dve(dve, 1, 2 + f // 2, 5)
        outputs(KT - 2)
        outputs(KT - 1)
        dve_layer_norm(dve, link, lambda tt, h: PS[:, 4 + 2 * tt + h, :],
                       lambda e, tt, h: e.wait_ge(S("mix"), 4 + 2 * tt + h + 1),
                       lnp1[:, 0:D], lnp1[:, D:2 * D], lambda e: e.wait_ge(S("ln_in0"), 64), (xr1, small[:, 192:204]), "ln2")

    m1 = moe(1, "m1", N_M1, lambda e: e.wait_ge(S("values"), 16 + KT),
             after_mod(1), "ln3", lambda e: e.wait_ge(S("ln_out"), 6), a1_norm_sp)

    N_HEADS, KV_HEADS, HD = 8, 2, 64
    Q_DIM, KV_DIM, SSD_W, STATE, SSD_H = 512, 128, 512, 128, 8
    XBC = SSD_W + 4 * STATE
    IN_DIM = Q_DIM + 2 * KV_DIM + SSD_W + XBC + SSD_H
    D_FF = 2816
    FT = D_FF // P
    TAPS = 5
    TT = 4
    RING_B = 3
    USES_A = uses(N_B) - 1

    X4 = arena[:, 0:4096].rearrange("p (t d) -> p t d", t=TT)
    MULTI, GATES, MISC = 4096, 4096 + 11264, 4096 + 11264 + 2048
    extra = ring[:, 3 * SLOT:4 * SLOT]

    def at(base, off, cols):
        return (extra if base == "extra" else arena)[:, (0 if base == "extra" else MULTI) + off:
                                                     (0 if base == "extra" else MULTI) + off + cols]

    G = arena[:, GATES:GATES + 2048].rearrange("p (v d) -> p v d", v=2)
    VC = arena[:, MISC:MISC + 128]
    modc = arena[:, MISC + 128:MISC + 224].rearrange("p (s v k) -> p s v k", s=6, v=2)
    g2row = arena[:, MISC + 224:MISC + 480]
    affine = arena[:, MISC + 480:MISC + 512].rearrange("p (a v k) -> p a v k", a=2, v=2)
    VR = arena[:, MISC + 768:MISC + 896]
    rs4 = arena[:, MISC + 896:MISC + 912]
    qk_ss = arena[:, MISC + 912:MISC + 952]
    u_max, u_sum, u_r = (arena[:, MISC + 952 + 2 * a:MISC + 954 + 2 * a] for a in range(3))
    V_BMOD, V_NMP, V_NFP, V_CW, V_CB, N_VEC = 0, 48, 56, 64, 104, 112

    HT = at("extra", 0, 4096).rearrange("p (k n) -> p k n", k=KT)
    xhat = at("extra", 4096, 4096).rearrange("p (t d) -> p t d", t=TT)
    modrow = at("m", 0, 1536).rearrange("p (s n) -> p s n", s=6)
    brow2 = at("m", 2048, 1024)
    prow2 = at("m", 3072, 1024)
    QK = at("m", 0, 2560).rearrange("p (t n) -> p t n", t=TT)
    Vr = at("m", 2560, 512).rearrange("p (t n) -> p t n", t=TT)
    Z = at("m", 3072, 2048).rearrange("p (t n) -> p t n", t=TT)
    cv = at("m", 5120, 4096).rearrange("p (i n) -> p i n", i=8)
    Y = at("m", 5120, 2048).rearrange("p (t n) -> p t n", t=TT)
    catT = at("m", 7168, 4096).rearrange("p (i n) -> p i n", i=8)
    dt = at("m", 9216, 64).rearrange("p (d t h) -> p d t h", d=2, t=TT)
    dA = at("m", 9280, 64).rearrange("p (d t h) -> p d t h", d=2, t=TT)
    EX = at("m", 9344, 128)
    xdt, xde = (at("m", 9472, 512), at("m", 7168, 512)), (at("m", 9984, 512), at("m", 7680, 512))
    ytmp = at("m", 10496, 512)
    CBm = at("m", 11008, 256).rearrange("p (g n) -> p g n", g=2)
    xs = at("extra", 0, 2048).rearrange("p (t n) -> p t n", t=TT)
    Br = at("extra", 2048, 1024).rearrange("p (t n) -> p t n", t=TT)
    Rb = at("extra", 3072, 2048).rearrange("p (b h n) -> p b h n", b=2, h=SSD_H)
    Es = at("extra", 5120, 2048).rearrange("p (b h n) -> p b h n", b=2, h=SSD_H)
    ST = at("extra", 7168, 1024).rearrange("p (d n) -> p d n", d=2)
    qT = at("extra", 0, 2048).rearrange("p (f n) -> p f n", f=4)
    kz = at("extra", 2048, 2048).rearrange("p (g c n) -> p g c n", g=KV_HEADS, c=2)
    Eb = at("extra", 4096, 1024).rearrange("p (b n) -> p b n", b=2)
    KD = at("extra", 7168, 1024).rearrange("p (t g n) -> p t g n", t=TT, g=KV_HEADS)
    PT = at("extra", 5120, 1024).rearrange("p (b n) -> p b n", b=2)
    hT = at("m", 0, FT * 512)
    sg = at("extra", 4096, 2048).rearrange("p (b n) -> p b n", b=4)
    rows = small[:, 204:640]
    r_bias, r_A, r_skip = rows[:, 0:16], rows[:, 16:32], rows[:, 32:40]
    r_qk = rows[:, 40:168]
    ones_b = at("m", 9600, 128)

    LAYER0 = dict(
        vec_in=80, vec_ps=2, mod_in=16, rows_in=112, g1_in=32, g2_in=32, ssdn_in=16, A=1, affine=1, y0=1,
        norm_sq=8, norm_ms=2, norm_sd=2, norm_hat=8, norm_turned=16, norm_act=8, norm_dve=8,
        gate_ps=2, gate=4, dtx=2, dtabs=2, dtln=1, cv=9, xs=4, Br=4, xsB_ps=4, CB=2, dA=1,
        dec=2, R=8, seg=8, expd=8, xdt=8, st_ps=6, state=6, score=8, y_ps=8, y=8, qk=4, stat=TT + 1, stat_sd=TT + 1,
        qkT_ps=6, qT=4, kT=4, lg=32, nmax=32, p=32, pn=32, pT_ps=32, PT=32, o_ps=32, oT=16,
        ygated=4, yT_ps=4, yT=4, out=8, res_sq=8, res_ms=8, res_sd=8, x1=4, gu=FT, sg=FT, hT=FT, down_slot=2, down=8,
        x2=4, **{"in": 21, "in_act": 9, "in_dve": 12})

    def hybrid(l):
        s = lambda name: S(f"b_{name}")
        past = lambda name: l * LAYER0[name]
        both = l == 0
        tiles = range(TT) if both else range(2)
        nv = 2 if both else 1
        ntok = 512 if both else 256
        SSDN = at("extra", 6144, 512)
        PER_LAYER = 13
        NB0 = l * PER_LAYER

        def first(tag, what):
            if tag in ("pre", "r1"):
                return 0
            return {"ms": 1, "sd": 1, "turned": 8, "act": 4, "dve": 4}.get(what, 4) if tag == "ffn" else len(tiles)

        def slot_b(n):
            return ring[:, ((NB0 + n) % RING_B) * SLOT:((NB0 + n) % RING_B + 1) * SLOT]

        def kview(n, cols):
            return slot_b(n)[:, 0:KT * cols].rearrange("p (k c) -> p k c", k=KT)

        def ready(eng, n):
            eng.wait_ge(S(f"ring{(NB0 + n) % RING_B}"), PER_SLOT * (USES_A + (NB0 + n) // RING_B + 1))

        products = [("xbc", i, "dve") for i in range(8)] + [("dt", 0, "act")]
        n_dt = len(products)
        products += [("z2", tt, "act") for tt in tiles]
        n_z2 = len(products)
        for tt in range(TT):
            if tt in tiles:
                products.append(("q", tt, "act"))
            products.append(("kvz", tt, "dve"))
        seen = {"act": 0, "dve": 0}
        count = []
        for _, _, e in products:
            seen[e] += 1
            count.append(seen[e])

        GU = [(512 * c, min(512, D_FF - 512 * c)) for c in range(6)]
        DOWN = [(8 * c, min(8, FT - 8 * c)) for c in range(3)]
        frees = [("in", n_z2), ("in", n_dt), ("in", len(products)), ("out", len(tiles) * 2)]
        done_ff = 0
        for c0, w in GU:
            done_ff += w // P
            frees.append(("gu", done_ff))
        frees += [("down_slot", 1), ("down_slot", 2), ("down", len(tiles) * 2)]

        IN_SLOTS = (1, 2, 0)

        def load(sp, n):
            sem = S(f"ring{(NB0 + n) % RING_B}")
            if n < 3:
                c0 = IN_SLOTS[n] * D
                cols = min(D, IN_DIM - c0)
                src = t["w_in_2"][l, :, c0:c0 + cols]
            elif n == 3:
                src, cols = t["w_out_2"][l], D
            elif n < 10:
                c0, w = GU[n - 4]
                dst = slot_b(n)[:, 0:KT * 2 * w].rearrange("p (k a c) -> p k a c", k=KT, a=2)
                for a, name in enumerate(("w_gate_2", "w_up_2")):
                    sp.dma_start(dst[:, :, a, :], t[name][l, :, c0:c0 + w].rearrange("(k p) c -> p k c", p=P)).then_inc(sem, 16)
                return
            else:
                r0, nr = DOWN[n - 10]
                dst = slot_b(n)[:, 0:nr * D].rearrange("p (k c) -> p k c", k=nr)
                src = t["w_down_2"][l, r0 * P:(r0 + nr) * P, :].rearrange("(k p) c -> p k c", p=P)
                for a in range(2):
                    sp.dma_start(dst[:, a * nr // 2:(a + 1) * nr // 2], src[:, a * nr // 2:(a + 1) * nr // 2]).then_inc(sem, 16)
                return
            src = src.rearrange("(k p) c -> p k c", p=P)
            for a in range(2):
                sp.dma_start(kview(n, cols)[:, 4 * a:4 * a + 4], src[:, 4 * a:4 * a + 4]).then_inc(sem, 16)

        def row_dma(sp, dst, name, off, n, sem):
            sp.dma_start(dst, bass.AP(t[name].tensor, off, [[0, P], [1, n]])).then_inc(s(sem), 16)

        def sp_(sp):
            def vectors():
                for name, r0, nr, off in (("b_mod_2", V_BMOD, 48, l * 6 * D), ("norm_mix_pre_2", V_NMP, 8, l * D),
                                          ("norm_ffn_pre_2", V_NFP, 8, l * D),
                                          ("conv_w_2", V_CW, 40, l * TAPS * XBC), ("conv_b_2", V_CB, 8, l * XBC)):
                    sp.dma_start(VR[r0:r0 + nr, :], bass.AP(t[name].tensor, off, [[P, nr], [1, P]])).then_inc(s("vec_in"), 16)
                for d, name in enumerate(("dt_bias_fwd_2", "dt_bias_bwd_2")):
                    row_dma(sp, r_bias[:, 8 * d:8 * d + 8], name, l * SSD_H, SSD_H, "rows_in")
                for d, name in enumerate(("a_log_fwd_2", "a_log_bwd_2")):
                    row_dma(sp, r_A[:, 8 * d:8 * d + 8], name, l * SSD_H, SSD_H, "rows_in")
                row_dma(sp, r_skip, "d_skip_2", l * SSD_H, SSD_H, "rows_in")
                row_dma(sp, r_qk[:, 0:64], "q_norm_2", l * HD, HD, "rows_in")
                row_dma(sp, r_qk[:, 64:128], "k_norm_2", l * HD, HD, "rows_in")
                sp.wait_ge(S("mod_out"), 16 * N_MOD * DEPTH)
                sp.dma_start(modrow, mod_rows.ap()[l]).then_inc(s("mod_in"), 16)
                row_dma(sp, brow2, "b_mod_2", l * 6 * D + 2 * D, D, "g1_in")
                row_dma(sp, prow2, "norm_mix_post_2", l * D, D, "g1_in")

            if l == 0:
                m1["freed"](sp, 0)
                load(sp, 0)
                m1["freed"](sp, 1)
                load(sp, 1)
                m1["freed"](sp, 2)
                load(sp, 2)
                sp.wait_ge(S("moe_done"), 2)
                sp.dma_start(X4[:, 2:4, :], t["ctx_2"].rearrange("b (t p) d -> p (b t) d", p=P)).then_inc(S("ctx_in"), 16)
                sp.wait_ge(S("ln_out"), 8)
                vectors()
            for n in range(3 if l == 0 else 0, PER_LAYER):
                if n >= RING_B:
                    name, v = frees[n - RING_B]
                    sp.wait_ge(s(name), past(name) + v)
                else:
                    name, v = (("down_slot", 1), ("down_slot", 2), ("down", 8))[n]
                    sp.wait_ge(S(f"b_{name}"), v)
                load(sp, n)
                if l == 1 and n == RING_B - 1:
                    sp.wait_ge(S("b_x2"), TT)
                    vectors()
                if n == 3:
                    sp.wait_ge(s("y"), past("y") + y_before[-1])
                    row_dma(sp, SSDN, "ssd_norm_2", l * SSD_W, SSD_W, "ssdn_in")
                if n == 6:
                    sp.wait_ge(s("x1"), past("x1") + len(tiles))
                    row_dma(sp, brow2, "b_mod_2", l * 6 * D + 5 * D, D, "g2_in")
                    row_dma(sp, prow2, "norm_ffn_post_2", l * D, D, "g2_in")
            if l == 1:
                for tt in range(2):
                    sp.wait_ge(s("x2"), past("x2") + tt + 1)
                    sp.dma_start(out[0, tt * P:(tt + 1) * P, :], X4[:, tt, :]).then_inc(S("out_dma"), 16)
                sp.wait_ge(S("out_dma"), 32)

        def norm_pe(pe, tag, ntiles):
            for k in range(KT):
                for tt in range(ntiles):
                    if k == 0:
                        pe.wait_ge(s("norm_hat"), past("norm_hat") + first(tag, "hat") + tt + 1)
                    ins = pe.transpose(PS[:, k, tt * P:(tt + 1) * P], xhat[:, tt, k * P:(k + 1) * P], ident)
                ins.then_inc(s("norm_turned"), 1)

        def norm_act(act, tag, ntiles, a, sh):
            for tt in range(ntiles):
                if tt == 0:
                    tag_ready(act, tag)
                act.activation(HT[:, 2 * tt:2 * tt + 2, :] if ntiles == 4 else HT[:, 4 * tt:4 * tt + 2, :],
                               X4[:, tt, :].rearrange("p (a n) -> p a n", a=2), ACT.Square,
                               accum_out=rs4[:, tt:tt + 1]).then_inc(s("norm_sq"), 1)
            act.wait_ge(s("norm_ms"), past("norm_ms") + first(tag, "ms") + 1)
            act.activation(rs4[:, 0:ntiles], rs4[:, 0:ntiles], ACT.Sqrt).then_inc(s("norm_sd"), 1)
            act.wait_ge(s("affine"), past("affine") + 1)
            for k in range(0, KT, 2):
                act.wait_ge(s("norm_turned"), past("norm_turned") + first(tag, "turned") + k + 1)
                for v in range(ntiles // 2):
                    ins = act.activation(HT[:, k, v * 256:(v + 1) * 256], PS[:, k, v * 256:(v + 1) * 256], ACT.Identity,
                                         bias=modc[:, sh, v, k:k + 1], scale=affine[:, a, v, k:k + 1])
                ins.then_inc(s("norm_act"), 1)

        def tag_ready(eng, tag):
            if tag == "pre" and l == 0:
                eng.wait_ge(S("ctx_in"), 16)
                eng.wait_ge(S("ln_out"), 8)
            elif tag == "pre":
                eng.wait_ge(S("b_x2"), TT)
            else:
                eng.wait_ge(s("x1"), past("x1") + len(tiles))

        def norm_dve(dve, link, tag, ntiles, a, sh):
            dve.wait_ge(s("norm_sq"), past("norm_sq") + first(tag, "sq") + ntiles)
            dve.tensor_scalar(rs4[:, 0:ntiles], rs4[:, 0:ntiles], 1.0 / D, EPS, ALU.mult, ALU.add).then_inc(s("norm_ms"), 1)
            dve.wait_ge(s("norm_sd"), past("norm_sd") + first(tag, "sd") + 1)
            link(dve.reciprocal(rs4[:, 0:ntiles], rs4[:, 0:ntiles]))
            for tt in range(ntiles):
                dve.tensor_scalar(xhat[:, tt, :], X4[:, tt, :], rs4[:, tt:tt + 1], None, ALU.mult).then_inc(s("norm_hat"), 1)

        def norm_out_dve(dve, tag, ntiles, a, sh):
            for k in range(1, KT, 2):
                dve.wait_ge(s("norm_turned"), past("norm_turned") + first(tag, "turned") + k + 1)
                for v in range(ntiles // 2):
                    ins = dve.tensor_scalar(HT[:, k, v * 256:(v + 1) * 256], PS[:, k, v * 256:(v + 1) * 256],
                                            affine[:, a, v, k:k + 1], modc[:, sh, v, k:k + 1], ALU.mult, ALU.add)
                ins.then_inc(s("norm_dve"), 1)

        def normed(eng, tag):
            eng.wait_ge(s("norm_act"), past("norm_act") + first(tag, "act") + 4)
            eng.wait_ge(s("norm_dve"), past("norm_dve") + first(tag, "dve") + 4)

        def gate_pe(pe, row, tag):
            for v in range(nv):
                for j in range(4):
                    ins = pe.matmul(PS[:, 2 * v + j // 2, (j % 2) * 256:(j % 2) * 256 + 256],
                                    view(ident[:, 32 * j + v:32 * j + v + 1], [0, P]), row, start=True, stop=True)
            ins.then_inc(s("gate_ps"), 1)

        def gate_dve(dve, link, tag):
            dve.wait_ge(s("gate_ps"), past("gate_ps") + (1 if tag == "g1" else 2))
            dve.wait_ge(s(f"{tag}_in"), past(f"{tag}_in") + 32)
            for v in range(nv):
                link(dve.tensor_tensor(G[:, v, :], view(PS[:, 2 * v, 0:1], [1, D]), brow2, ALU.add))
                dve.tensor_tensor(G[:, v, :], G[:, v, :], prow2, ALU.mult).then_inc(s("gate"), 1)

        def residual_act(act, ps_sem, tag):
            for n, tt in enumerate(tiles):
                act.wait_ge(s(ps_sem), past(ps_sem) + 2 * n + 2)
                act.activation(xhat[:, tt, :].rearrange("p (a n) -> p a n", a=2), PS[:, 2 * tt:2 * tt + 2, :], ACT.Square,
                               accum_out=rs4[:, 4 + tt:5 + tt]).then_inc(s("res_sq"), 1)
                act.wait_ge(s("res_ms"), past("res_ms") + first(tag, "ms") + n + 1)
                act.activation(rs4[:, 8 + tt:9 + tt], rs4[:, 8 + tt:9 + tt], ACT.Sqrt).then_inc(s("res_sd"), 1)

        def residual_dve(dve, link, tag, done):
            for n, tt in enumerate(tiles):
                dve.wait_ge(s("res_sq"), past("res_sq") + first(tag, "sq") + n + 1)
                dve.tensor_scalar(rs4[:, 8 + tt:9 + tt], rs4[:, 4 + tt:5 + tt], 1.0 / D, EPS, ALU.mult, ALU.add)\
                   .then_inc(s("res_ms"), 1)
                dve.wait_ge(s("res_sd"), past("res_sd") + first(tag, "sd") + n + 1)
                link(dve.reciprocal(rs4[:, 8 + tt:9 + tt], rs4[:, 8 + tt:9 + tt]))
                tmp = xhat[:, tt, :]
                link(dve.scalar_tensor_tensor(tmp, view(PS[:, 2 * tt, 0:1], [1, D]), rs4[:, 8 + tt:9 + tt], G[:, tt // 2, :],
                                              ALU.mult, ALU.mult))
                dve.tensor_tensor(X4[:, tt, :], X4[:, tt, :], tmp, ALU.add).then_inc(s(done), 1)
                dve.wait_ge(s(done), past(done) + n + 1)

        ORDER = ((2, 3, 0, 1), (3, 2, 1, 0))
        STEPS = [(d, c, ORDER[d][c]) for c in range(TT) for d in range(2)]
        y_before = [sum(tt in tiles for _, _, tt in STEPS[:i]) for i in range(len(STEPS) + 1)]
        st_before = [sum(c < TT - 1 for _, c, _ in STEPS[:i]) for i in range(len(STEPS) + 1)]
        MASK = (C_LE, C_GE)
        AFTER = (C_GT, C_LT)

        UN = [(f, tt, c) for f in range(4) for tt in tiles for c in range(2)]

        def keys(tt):
            return (0, 512) if tt < 2 else (256, 256)

        def pe_(pe):
            pe.wait_ge(s("vec_in"), past("vec_in") + 16 * 5)
            if l == 0:
                pe.wait_ge(S("ln_out"), 8)
            else:
                pe.wait_ge(S("b_x2"), TT)
            pe.transpose(PS[:, 7, 0:N_VEC], VR[0:N_VEC, :], ident[0:N_VEC, 0:N_VEC]).then_inc(s("vec_ps"), 1)
            pe.wait_ge(s("mod_in"), past("mod_in") + 16)
            for n in range(6):
                for h in range(2):
                    ins = pe.transpose(PS[:, n // 2, (n % 2) * 256 + h * P:(n % 2) * 256 + h * P + P], modrow[:, n, h * P:(h + 1) * P], ident)
            ins.then_inc(s("vec_ps"), 1)
            pe.wait_ge(s("affine"), past("affine") + 1)
            gate_pe(pe, modrow[:, 2, :], "g1")
            pe.wait_ge(s("gate"), past("gate") + nv)
            norm_pe(pe, "pre", TT)
            normed(pe, "pre")
            wB, wC, wA = kview(0, D), kview(1, IN_DIM - 2 * D), kview(2, D)
            for n, (kind, i, _) in enumerate(products):
                if n in (0, 6, n_z2):
                    ready(pe, (0, 6, n_z2).index(n))
                if n >= 8:
                    e = products[n - 8][2]
                    pe.wait_ge(s(f"in_{e}"), past(f"in_{e}") + count[n - 8])
                bank = PS[:, n % 8, :]
                if kind == "dt":
                    for tt in range(TT):
                        for k in range(KT):
                            ins = pe.matmul(bank[:, 8 * tt:8 * tt + 8], HT[:, k, tt * P:(tt + 1) * P], wC[:, k, 256:264],
                                            start=(k == 0), stop=(k == KT - 1))
                    ins.then_inc(s("in"), 1)
                    continue
                for k in range(KT):
                    if kind == "xbc":
                        w = wB[:, k, 256 + i * P:256 + (i + 1) * P] if i < 6 else wC[:, k, (i - 6) * P:(i - 5) * P]
                        o, a, b = bank, w, HT[:, k, :]
                    else:
                        a = HT[:, k, i * P:(i + 1) * P]
                        if kind == "q":
                            o, b = bank, wA[:, k, 0:512]
                        elif kind == "kvz":
                            n_c_ = 512 if i in tiles else 256
                            o, b = bank[:, 0:n_c_], wA[:, k, 512:512 + n_c_]
                        else:
                            o, b = bank[:, 0:256], wB[:, k, 0:256]
                    ins = pe.matmul(o, a, b, start=(k == 0), stop=(k == KT - 1))
                ins.then_inc(s("in"), 1)
            pe.wait_ge(s("in_act"), past("in_act") + seen["act"])
            pe.wait_ge(s("in_dve"), past("in_dve") + seen["dve"])
            pe.wait_ge(s("cv"), past("cv") + 8)
            for tt in range(TT):
                if tt >= 2:
                    pe.wait_ge(s("xs"), past("xs") + tt - 1)
                    pe.wait_ge(s("Br"), past("Br") + tt - 1)
                for i in range(6):
                    b = 2 * (tt % 2) + i // 4
                    ins = pe.transpose(PS[:, b, (i % 4) * P:(i % 4) * P + P], cv[:, i, tt * P:(tt + 1) * P], ident)
                ins.then_inc(s("xsB_ps"), 1)
            for tt in range(TT):
                for g in range(2):
                    ins = pe.matmul(PS[:, 6 + tt // 2, (tt % 2) * 256 + g * P:(tt % 2) * 256 + g * P + P], cv[:, 4 + g, tt * P:(tt + 1) * P],
                                    cv[:, 6 + g, tt * P:(tt + 1) * P], start=True, stop=True)
            ins.then_inc(s("CB"), 1)
            pe.wait_ge(s("dA"), past("dA") + 1)
            for d in range(2):
                for a, w in enumerate((cst[:, MASK[d]:MASK[d] + P], cst[:, AFTER[d]:AFTER[d] + P])):
                    pe.matmul(PS[:, 5, 64 * d + 32 * a:64 * d + 32 * a + 32], w, dA[:, d].rearrange("p t h -> p (t h)"), start=True, stop=True)
            ins = pe.matmul(PS[:, 5, 128:192], ones_b, dA.rearrange("p d t h -> p (d t h)"), start=True, stop=True)
            ins.then_inc(s("CB"), 1)
            pe.wait_ge(s("dec"), past("dec") + 2)
            pe.wait_ge(s("xs"), past("xs") + TT)
            pe.wait_ge(s("Br"), past("Br") + TT)
            for i, (d, c, tt) in enumerate(STEPS):
                if tt in tiles:
                    yi = y_before[i]
                    pe.wait_ge(s("R"), past("R") + yi + 1)
                    pe.wait_ge(s("expd"), past("expd") + yi)
                    for a in range(2):
                        ins = pe.matmul(PS[:, a, :], cst[:, AFTER[d]:AFTER[d] + P], view(Rb[:, yi % 2, 4 * a, 0:1], [1, 512]), start=True, stop=True)
                    ins.then_inc(s("seg"), 1)
                if c < TT - 1:
                    pe.wait_ge(s("xdt"), past("xdt") + i + 1)
                    if c:
                        pe.wait_ge(s("state"), past("state") + st_before[i - 1])
                    for g in range(2):
                        ins = pe.matmul(PS[:, 2 + d, 256 * g:256 * g + 256], Br[:, tt, P * g:P * g + P], xde[i % 2][:, 256 * g:256 * g + 256],
                                        start=True, stop=True)
                    ins.then_inc(s("st_ps"), 1)
                if tt in tiles:
                    pe.wait_ge(s("score"), past("score") + yi + 1)
                    pe.wait_ge(s("xdt"), past("xdt") + i + 1)
                    pe.wait_ge(s("y"), past("y") + yi)
                    for h in range(SSD_H):
                        ins = pe.matmul(PS[:, 4, 64 * h:64 * h + 64], Es[:, yi % 2, h, :], xdt[i % 2][:, 64 * h:64 * h + 64], start=True, stop=True)
                    if c:
                        pe.wait_ge(s("state"), past("state") + st_before[i - 1])
                        for g in range(2):
                            ins = pe.matmul(PS[:, 5, 256 * g:256 * g + 256], cv[:, 6 + g, tt * P:(tt + 1) * P], ST[:, d, 256 * g:256 * g + 256],
                                            start=True, stop=True)
                    ins.then_inc(s("y_ps"), 1)
            pe.wait_ge(s("qk"), past("qk") + TT)
            pe.wait_ge(s("y"), past("y") + y_before[-1])
            pe.wait_ge(s("state"), past("state") + st_before[-1])
            for f in range(4):
                for tt in tiles:
                    ins = pe.transpose(PS[:, f, tt * P:(tt + 1) * P], QK[:, tt, f * P:(f + 1) * P], ident)
                ins.then_inc(s("qkT_ps"), 1)
            for g in range(2):
                for tt in range(TT):
                    ins = pe.transpose(PS[:, 4 + g, tt * P:(tt + 1) * P], KD[:, tt, g, :], ident)
                ins.then_inc(s("qkT_ps"), 1)
            pe.wait_ge(s("qT"), past("qT") + 4)
            pe.wait_ge(s("kT"), past("kT") + 4)

            def logits(u):
                f, tt, c = UN[u]
                k0, nk = keys(tt)
                if u >= 2:
                    pe.wait_ge(s("p"), past("p") + u - 1)
                pe.matmul(PS[:, u % 2, 0:nk], qT[:, f, tt * P:(tt + 1) * P], kz[:, f // 2, c, k0:k0 + nk], start=True, stop=True)\
                  .then_inc(s("lg"), 1)

            def turn_weights(u):
                nk = keys(UN[u][1])[1]
                pe.wait_ge(s("pn"), past("pn") + u + 1)
                if u >= 2:
                    pe.wait_ge(s("PT"), past("PT") + u - 1)
                for kb in range(nk // P):
                    ins = pe.transpose(PS[:, 2 + u % 2, kb * P:(kb + 1) * P], Eb[:, u % 2, kb * P:(kb + 1) * P], ident)
                ins.then_inc(s("pT_ps"), 1)

            def values(u):
                f, tt, c = UN[u]
                k0, nk = keys(tt)
                pe.wait_ge(s("PT"), past("PT") + u + 1)
                pair = u // 2
                if pair >= 2:
                    pe.wait_ge(s("oT"), past("oT") + pair - 1)
                for kb in range(nk // P):
                    ins = pe.matmul(PS[64 * c:64 * c + 64, 4 + pair % 2, 0:P], Vr[:, k0 // P + kb, HD * (f // 2):HD * (f // 2) + HD],
                                    PT[:, u % 2, kb * P:(kb + 1) * P], start=(kb == 0), stop=(kb == nk // P - 1))
                ins.then_inc(s("o_ps"), 1)

            logits(0)
            logits(1)
            for u in range(len(UN)):
                turn_weights(u)
                if u + 2 < len(UN):
                    logits(u + 2)
                if u:
                    values(u - 1)
            values(len(UN) - 1)
            pe.wait_ge(s("ygated"), past("ygated") + len(tiles))
            for n, tt in enumerate(tiles):
                for i in range(4):
                    ins = pe.transpose(PS[:, 6 + n % 2, i * P:(i + 1) * P], Y[:, tt, i * P:(i + 1) * P], ident)
                ins.then_inc(s("yT_ps"), 1)
                if n:
                    pe.wait_ge(s("yT"), past("yT") + n)
            ready(pe, 3)
            pe.wait_ge(s("yT"), past("yT") + len(tiles))
            pe.wait_ge(s("oT"), past("oT") + len(UN) // 2)
            w = kview(3, D)
            for tt in tiles:
                for h in range(2):
                    for k in range(KT):
                        ins = pe.matmul(PS[:, 2 * tt + h, :], catT[:, k, tt * P:(tt + 1) * P], w[:, k, 512 * h:512 * h + 512],
                                        start=(k == 0), stop=(k == KT - 1))
                    ins.then_inc(s("out"), 1)
            pe.wait_ge(s("x1"), past("x1") + len(tiles))
            gate_pe(pe, g2row, "g2")
            pe.wait_ge(s("gate"), past("gate") + 2 * nv)
            norm_pe(pe, "ffn", len(tiles))
            normed(pe, "ffn")
            i = 0
            for c, (c0, wd) in enumerate(GU):
                ready(pe, 4 + c)
                w = slot_b(4 + c)[:, 0:KT * 2 * wd].rearrange("p (k a c) -> p k a c", k=KT, a=2)
                for j in range(wd // P):
                    if i >= 4:
                        pe.wait_ge(s("hT"), past("hT") + i - 3)
                    for a in range(2):
                        for k in range(KT):
                            ins = pe.matmul(PS[:, 2 * (i % 4) + a, 0:ntok], w[:, k, a, j * P:(j + 1) * P], HT[:, k, 0:ntok],
                                            start=(k == 0), stop=(k == KT - 1))
                    ins.then_inc(s("gu"), 1)
                    i += 1
            pe.wait_ge(s("hT"), past("hT") + FT)
            for c, (r0, nr) in enumerate(DOWN):
                ready(pe, 10 + c)
                w = slot_b(10 + c)[:, 0:nr * D].rearrange("p (k c) -> p k c", k=nr)
                if c < 2:
                    for r in range(nr):
                        for tt in tiles:
                            for h in range(2):
                                ins = pe.matmul(PS[:, 2 * tt + h, :], hTv[:, r0 + r, tt * P:(tt + 1) * P], w[:, r, 512 * h:512 * h + 512],
                                                start=(r0 + r == 0), stop=False)
                    ins.then_inc(s("down_slot"), 1)
                else:
                    for tt in tiles:
                        for h in range(2):
                            for r in range(nr):
                                ins = pe.matmul(PS[:, 2 * tt + h, :], hTv[:, r0 + r, tt * P:(tt + 1) * P], w[:, r, 512 * h:512 * h + 512],
                                                start=False, stop=(r == nr - 1))
                            ins.then_inc(s("down"), 1)

        hTv = hT[:, 0:FT * ntok].rearrange("p (f n) -> p f n", f=FT)

        def act_(act):
            act.wait_ge(s("rows_in"), past("rows_in") + 16 * 7)
            act.activation(r_A, r_A, ACT.Exp).then_inc(s("A"), 1)
            norm_act(act, "pre", TT, 0, 0)
            for i in range(8):
                act.wait_ge(s("in_dve"), past("in_dve") + i + 1)
                act.activation(cv[:, i, :], cv[:, i, :], ACT.Silu).then_inc(s("cv"), 1)
            for n, (kind, i, e) in enumerate(products):
                if e == "act":
                    act.wait_ge(s("in"), past("in") + n + 1)
                bank = PS[:, n % 8, :]
                if kind == "q":
                    act.copy(QK[:, i, 0:512], bank).then_inc(s("in_act"), 1)
                elif kind == "z2":
                    act.copy(Z[:, i, 256:512], bank[:, 0:256]).then_inc(s("in_act"), 1)
                elif kind == "dt":
                    act.copy(dt[:, 0], bank[:, 0:32].rearrange("p (t h) -> p t h", t=TT)).then_inc(s("in_act"), 1)
                    act.wait_ge(s("dtx"), past("dtx") + 2)
                    act.activation(dA, dt, ACT.Abs).then_inc(s("dtabs"), 1)
                    act.wait_ge(s("dtabs"), past("dtabs") + 1)
                    act.activation(dA, dA, ACT.Exp, scale=-1.0).then_inc(s("dtabs"), 1)
                    act.wait_ge(s("dtabs"), past("dtabs") + 2)
                    act.activation(dA, dA, ACT.Ln, bias=1.0).then_inc(s("dtln"), 1)
                elif kind == "kvz":
                    h0 = 0 if i in tiles else 8
                    act.wait_ge(s("stat"), past("stat") + i + 1)
                    act.activation(qk_ss[:, 10 * i + h0:10 * i + 10], qk_ss[:, 10 * i + h0:10 * i + 10], ACT.Sqrt).then_inc(s("stat_sd"), 1)
            act.wait_ge(s("in_dve"), past("in_dve") + seen["dve"])
            nz = len(tiles) * 512
            for tt in range(TT):
                act.wait_ge(s("xsB_ps"), past("xsB_ps") + tt + 1)
                act.copy(xs[:, tt, :], PS[:, 2 * (tt % 2), :]).then_inc(s("xs"), 1)
                act.copy(Br[:, tt, :], PS[:, 2 * (tt % 2) + 1, 0:256]).then_inc(s("Br"), 1)
            act.wait_ge(s("CB"), past("CB") + 2)
            act.activation(EX, PS[:, 5, 0:128], ACT.Exp).then_inc(s("dec"), 1)
            act.activation(small[:, 0:64], PS[:, 5, 128:192], ACT.Exp).then_inc(s("dec"), 1)
            act.activation(view(Z[:, 0, 0:1], [1, nz]), view(Z[:, 0, 0:1], [1, nz]), ACT.Silu).then_inc(s("cv"), 1)
            for n in range(y_before[-1]):
                act.wait_ge(s("seg"), past("seg") + n + 1)
                if n >= 2:
                    act.wait_ge(s("y_ps"), past("y_ps") + n - 1)
                act.activation(view(Es[:, n % 2, 0, 0:1], [1, 1024]), view(PS[:, 0, 0:1], [1, 1024]), ACT.Exp).then_inc(s("expd"), 1)
            for f in range(4):
                act.wait_ge(s("qkT_ps"), past("qkT_ps") + f + 1)
                act.copy(qT[:, f, 0:ntok], PS[:, f, 0:ntok]).then_inc(s("qT"), 1)

            def expo(u):
                nk = keys(UN[u][1])[1]
                b = u % 2
                act.wait_ge(s("nmax"), past("nmax") + u + 1)
                if u >= 2:
                    act.wait_ge(s("pT_ps"), past("pT_ps") + u - 1)
                act.activation(Eb[:, b, 0:nk], PS[:, b, 0:nk], ACT.Exp, bias=u_max[:, b:b + 1], accum_out=u_sum[:, b:b + 1]).then_inc(s("p"), 1)

            expo(0)
            for u in range(len(UN)):
                if u + 1 < len(UN):
                    expo(u + 1)
                nk = keys(UN[u][1])[1]
                act.wait_ge(s("pT_ps"), past("pT_ps") + u + 1)
                if u >= 2:
                    act.wait_ge(s("o_ps"), past("o_ps") + u - 1)
                act.copy(PT[:, u % 2, 0:nk], PS[:, 2 + u % 2, 0:nk]).then_inc(s("PT"), 1)
            act.wait_ge(s("stat"), past("stat") + TT + 1)
            act.activation(rs4[:, 0:len(tiles)], rs4[:, 0:len(tiles)], ACT.Sqrt).then_inc(s("stat_sd"), 1)
            for n, tt in enumerate(tiles):
                act.wait_ge(s("yT_ps"), past("yT_ps") + n + 1)
                act.copy(catT[:, 4:8, tt * P:(tt + 1) * P], PS[:, 6 + n % 2, :].rearrange("p (i n) -> p i n", i=4)).then_inc(s("yT"), 1)
            residual_act(act, "out", "r1")
            norm_act(act, "ffn", len(tiles), 1, 3)
            for i in range(FT):
                act.wait_ge(s("gu"), past("gu") + i + 1)
                if i >= 4:
                    act.wait_ge(s("hT"), past("hT") + i - 3)
                act.activation(sg[:, i % 4, 0:ntok], PS[:, 2 * (i % 4), 0:ntok], ACT.Silu).then_inc(s("sg"), 1)
            residual_act(act, "down", "r2")

        def softplus(dve, link):
            dve.wait_ge(s("in_act"), past("in_act") + 1)
            dve.wait_ge(s("rows_in"), past("rows_in") + 16 * 7)
            for n, d in enumerate((1, 0)):
                dve.tensor_tensor(dt[:, d], dt[:, 0], view(r_bias[:, 8 * d:8 * d + 1], [0, TT], [1, SSD_H]), ALU.add)\
                   .then_inc(s("dtx"), 1)
                dve.wait_ge(s("dtx"), past("dtx") + n + 1)
            link(dve.memset(ones_b, 1.0))
            dve.wait_ge(s("A"), past("A") + 1)
            link(dve.tensor_scalar(r_A, r_A, -1.0, None, ALU.mult))
            dve.wait_ge(s("dtln"), past("dtln") + 1)
            dve.wait_ge(s("dtx"), past("dtx") + 2)
            flat = lambda a: a.rearrange("p d t h -> p (d t h)")
            link(dve.scalar_tensor_tensor(flat(dt), flat(dt), 0.0, flat(dA), ALU.max, ALU.add))
            dve.tensor_tensor(dA, dt, view(r_A, [8, 2], [0, TT], [1, SSD_H]), ALU.mult).then_inc(s("dA"), 1)

        def head_norm(dve, link, tt):
            hh = lambda a: a.rearrange("p (h e) -> p h e", e=HD)
            h0 = 0 if tt in tiles else 8
            nh = 10 - h0
            w5 = at("extra", 4096, 1920).rearrange("p (t n) -> p t n", t=3)
            if tt == 0:
                link(dve.tensor_scalar(r_qk[:, 0:64], r_qk[:, 0:64], 0.125, None, ALU.mult))
            row = QK[:, tt, HD * h0:640]
            sq = w5[:, 0, HD * h0:640]
            ss = qk_ss[:, 10 * tt + h0:10 * tt + 10]
            link(dve.tensor_tensor(sq, row, row, ALU.mult))
            link(dve.tensor_reduce(ss, hh(sq), AX.X, ALU.add))
            dve.tensor_scalar(ss, ss, 1.0 / HD, EPS, ALU.mult, ALU.add).then_inc(s("stat"), 1)
            dve.wait_ge(s("stat_sd"), past("stat_sd") + tt + 1)
            link(dve.reciprocal(ss, ss))
            qk = hh(row)
            link(dve.tensor_tensor(qk, qk, view(ss, [1, nh], [0, HD]), ALU.mult))
            if h0 == 0:
                link(dve.tensor_tensor(qk[:, 0:8], qk[:, 0:8], view(r_qk[:, 0:1], [0, 8], [1, HD]), ALU.mult))
            link(dve.tensor_tensor(qk[:, nh - 2:nh], qk[:, nh - 2:nh], view(r_qk[:, 64:65], [0, 2], [1, HD]), ALU.mult))
            if tt < 2:
                quarter = lambda a: a.rearrange("p h (a e) -> p (h a) e", a=2)
                cos, sin = (view(cst[:, o + 32 * tt:o + 32 * tt + 1], [0, 2 * nh], [1, 32]) for o in (C_COS, C_SIN))
                tc, ts = hh(w5[:, 1, :]), hh(w5[:, 2, :])
                link(dve.tensor_tensor(quarter(tc), quarter(qk), cos, ALU.mult))
                link(dve.tensor_tensor(quarter(ts), quarter(qk), sin, ALU.mult))
                link(dve.tensor_tensor(qk[:, :, 0:32], tc[:, :, 0:32], ts[:, :, 32:64], ALU.subtract))
                link(dve.tensor_tensor(qk[:, :, 32:64], ts[:, :, 0:32], tc[:, :, 32:64], ALU.add))

        def dve_(dve, link):
            dve.wait_ge(s("vec_ps"), past("vec_ps") + 1)
            link(dve.tensor_copy(VC[:, 0:N_VEC], PS[:, 7, 0:N_VEC]))
            dve.wait_ge(s("mod_in"), past("mod_in") + 16)
            link(dve.tensor_copy(g2row, modrow[:, 5, :]))
            dve.wait_ge(s("vec_ps"), past("vec_ps") + 2)
            for v in range(2):
                link(dve.tensor_tensor(view(modc[:, 0, v, 0:1], [16, 6], [1, 2], [2, 4]), view(PS[:, 0, v:v + 1], [256, 6], [P, 2], [32, 4]),
                                       view(VC[:, 0:1], [8, 6], [1, 2], [2, 4]), ALU.add))
            for a, (sc, nw) in enumerate(((1, V_NMP), (4, V_NFP))):
                for v in range(2):
                    ins = dve.scalar_tensor_tensor(affine[:, a, v, :], modc[:, sc, v, :], 1.0, VC[:, nw:nw + 8], ALU.add, ALU.mult)
                    if a == 0 or v == 0:
                        link(ins)
            ins.then_inc(s("affine"), 1)
            norm_dve(dve, link, "pre", TT, 0, 0)
            gate_dve(dve, link, "g1")
            norm_out_dve(dve, "pre", TT, 0, 0)
            for n, (kind, i, e) in enumerate(products):
                if kind == "dt":
                    softplus(dve, link)
                if e != "dve":
                    continue
                dve.wait_ge(s("in"), past("in") + n + 1)
                bank = PS[:, n % 8, :]
                if kind == "kvz":
                    if i in tiles:
                        link(dve.tensor_copy(Z[:, i, 0:256], bank[:, 256:512]))
                    link(dve.tensor_copy(Vr[:, i, :], bank[:, 128:256]))
                    dve.tensor_copy(QK[:, i, 512:640], bank[:, 0:128]).then_inc(s("in_dve"), 1)
                    dve.wait_ge(s("in_dve"), past("in_dve") + count[n])
                    if i in tiles:
                        dve.wait_ge(s("in_act"), past("in_act") + count[n - 1])
                    head_norm(dve, link, i)
                else:
                    src = bank.rearrange("p (v n) -> p v n", v=2)
                    dst = cv[:, i, :].rearrange("p (v n) -> p v n", v=2)
                    tap = lambda w: VC[:, V_CW + 8 * w + i:V_CW + 8 * w + i + 1]
                    link(dve.tensor_scalar(dst, src, tap(2), VC[:, V_CB + i:V_CB + i + 1], ALU.mult, ALU.add))
                    for w in (0, 1, 3, 4):
                        sh = w - 2
                        a, b = max(0, -sh), 256 - max(0, sh)
                        ins = dve.scalar_tensor_tensor(dst[:, :, a:b], src[:, :, a + sh:b + sh], tap(w), dst[:, :, a:b], ALU.mult, ALU.add)
                        if w < 4:
                            link(ins)
                    ins.then_inc(s("in_dve"), 1)
            dve.wait_ge(s("CB"), past("CB") + 1)
            dve.wait_ge(s("dec"), past("dec") + 2)
            hb = lambda a: a.rearrange("p (h n) -> p h n", h=SSD_H)
            e_in = lambda d, tt: view(EX[:, 64 * d + 8 * tt:64 * d + 8 * tt + 1], [1, SSD_H], [0, HD])
            e_tot = lambda d, tt: view(small[:, 32 * d + 8 * tt:32 * d + 8 * tt + 1], [1, SSD_H], [0, HD])

            dve.wait_ge(s("y0"), past("y0") + 1)
            for i, (d, c, tt) in enumerate(STEPS):
                if tt in tiles:
                    yi = y_before[i]
                    if yi:
                        dve.wait_ge(s("score"), past("score") + yi)
                    link(dve.tensor_tensor(CBm, PS[:, 6 + tt // 2, (tt % 2) * 256:(tt % 2) * 256 + 256].rearrange("p (g n) -> p g n", g=2),
                                           view(cst[:, MASK[d]:MASK[d] + 1], [0, 2], [1, P]), ALU.mult))
                    dve.wait_ge(s("expd"), past("expd") + yi + 1)
                    e4 = Es[:, yi % 2].rearrange("p (g h) n -> p g h n", g=2)
                    dve.tensor_tensor(e4, e4, view(CBm[:, 0, 0:1], [P, 2], [0, 4], [1, P]), ALU.mult).then_inc(s("score"), 1)
                if c < TT - 1:
                    dve.wait_ge(s("st_ps"), past("st_ps") + st_before[i] + 1)
                    if c == 0:
                        dve.tensor_copy(ST[:, d], PS[:, 2 + d, :]).then_inc(s("state"), 1)
                    else:
                        if tt in tiles:
                            dve.wait_ge(s("y_ps"), past("y_ps") + y_before[i] + 1)
                        link(dve.tensor_tensor(hb(ST[:, d]), hb(ST[:, d]), e_tot(d, tt), ALU.mult))
                        dve.tensor_tensor(ST[:, d], ST[:, d], PS[:, 2 + d, :], ALU.add).then_inc(s("state"), 1)
                    dve.wait_ge(s("state"), past("state") + st_before[i] + 1)
                if tt in tiles:
                    dve.wait_ge(s("y_ps"), past("y_ps") + yi + 1)
                    if c:
                        link(dve.tensor_tensor(hb(ytmp), hb(PS[:, 5, :]), e_in(d, tt), ALU.mult))
                        link(dve.tensor_tensor(Y[:, tt], Y[:, tt], ytmp, ALU.add))
                    dve.tensor_tensor(Y[:, tt], Y[:, tt], PS[:, 4, :], ALU.add).then_inc(s("y"), 1)
                    dve.wait_ge(s("y"), past("y") + yi + 1)
            dve.wait_ge(s("y_ps"), past("y_ps") + y_before[-1])
            for tt in range(TT):
                dve.tensor_copy(KD[:, tt].rearrange("p g (a e) -> p g a e", a=2),
                                view(QK[:, tt, Q_DIM:Q_DIM + 1], [HD, KV_HEADS], [0, 2], [1, HD])).then_inc(s("qk"), 1)
            dve.wait_ge(s("y"), past("y") + y_before[-1])
            link(dve.memset(view(kz[:, 0, 0, 0:1], [1, 2048]), 0.0))
            for g in range(2):
                dve.wait_ge(s("qkT_ps"), past("qkT_ps") + 4 + g + 1)
                for c in range(2):
                    dve.tensor_copy(kz[64 * c:64 * c + 64, g, c, :], PS[64 * c:64 * c + 64, 4 + g, :]).then_inc(s("kT"), 1)

            def peak(u):
                nk = keys(UN[u][1])[1]
                dve.wait_ge(s("lg"), past("lg") + u + 1)
                if u >= 2:
                    dve.wait_ge(s("p"), past("p") + u - 1)
                dve.tensor_reduce(u_max[:, u % 2:u % 2 + 1], PS[:, u % 2, 0:nk], AX.X, ALU.max, negate=True).then_inc(s("nmax"), 1)

            peak(0)
            for u in range(len(UN)):
                f, tt, c = UN[u]
                nk = keys(tt)[1]
                if u + 1 < len(UN):
                    peak(u + 1)
                b = u % 2
                dve.wait_ge(s("p"), past("p") + u + 1)
                link(dve.reciprocal(u_r[:, b:b + 1], u_sum[:, b:b + 1]))
                dve.tensor_scalar(Eb[:, b, 0:nk], Eb[:, b, 0:nk], u_r[:, b:b + 1], None, ALU.mult).then_inc(s("pn"), 1)
                if u % 2 and u >= 3:
                    o_copy(dve, u // 2 - 1)
            o_copy(dve, len(UN) // 2 - 1)
            dve.wait_ge(s("cv"), past("cv") + 9)
            for tt in tiles:
                yt = Y[:, tt]
                link(dve.tensor_tensor(yt, yt, Z[:, tt], ALU.mult))
                link(dve.tensor_tensor(Z[:, tt], yt, yt, ALU.mult))
                link(dve.tensor_reduce(rs4[:, tt:tt + 1], Z[:, tt], AX.X, ALU.add))
            dve.tensor_scalar(rs4[:, 0:len(tiles)], rs4[:, 0:len(tiles)], 1.0 / SSD_W, EPS, ALU.mult, ALU.add).then_inc(s("stat"), 1)
            dve.wait_ge(s("stat_sd"), past("stat_sd") + TT + 1)
            link(dve.reciprocal(rs4[:, 0:len(tiles)], rs4[:, 0:len(tiles)]))
            dve.wait_ge(s("ssdn_in"), past("ssdn_in") + 16)
            for tt in tiles:
                dve.scalar_tensor_tensor(Y[:, tt], Y[:, tt], rs4[:, tt:tt + 1], SSDN, ALU.mult, ALU.mult).then_inc(s("ygated"), 1)
            residual_dve(dve, link, "r1", "x1")
            norm_dve(dve, link, "ffn", len(tiles), 1, 3)
            gate_dve(dve, link, "g2")
            norm_out_dve(dve, "ffn", len(tiles), 1, 3)
            for i in range(FT):
                dve.wait_ge(s("sg"), past("sg") + i + 1)
                dve.tensor_tensor(hTv[:, i, :], sg[:, i % 4, 0:ntok], PS[:, 2 * (i % 4) + 1, 0:ntok], ALU.mult).then_inc(s("hT"), 1)
            residual_dve(dve, link, "r2", "x2")

        def pool_(pool, link):
            hb = lambda a: a.rearrange("p (h n) -> p h n", h=SSD_H)
            pool.wait_ge(s("dA"), past("dA") + 1)
            pool.wait_ge(s("xs"), past("xs") + TT)
            pool.wait_ge(s("Br"), past("Br") + TT)

            def decay(i):
                d, c, tt = STEPS[i]
                if tt in tiles:
                    yi = y_before[i]
                    if yi >= 2:
                        pool.wait_ge(s("seg"), past("seg") + yi - 1)
                    pool.tensor_tensor(Rb[:, yi % 2], view(cst[:, MASK[d]:MASK[d] + 1], [0, SSD_H], [1, P]),
                                       view(dA[:, d, tt, 0:1], [1, SSD_H], [0, P]), ALU.mult).then_inc(s("R"), 1)

            def inputs(i):
                d, c, tt = STEPS[i]
                if i >= 2:
                    pool.wait_ge(s("y_ps"), past("y_ps") + y_before[i - 1])
                    pool.wait_ge(s("st_ps"), past("st_ps") + st_before[i - 1])
                link(pool.tensor_tensor(hb(xdt[i % 2]), hb(xs[:, tt]), view(dt[:, d, tt, 0:1], [1, SSD_H], [0, HD]), ALU.mult))
                e_end = view(EX[:, 64 * d + 32 + 8 * tt:64 * d + 33 + 8 * tt], [1, SSD_H], [0, HD])
                pool.tensor_tensor(hb(xde[i % 2]), hb(xdt[i % 2]), e_end, ALU.mult).then_inc(s("xdt"), 1)

            decay(0)
            pool.wait_ge(s("dec"), past("dec") + 2)
            inputs(0)
            for tt in tiles:
                ins = pool.tensor_tensor(Y[:, tt].rearrange("p (h n) -> p h n", h=SSD_H), xs[:, tt].rearrange("p (h n) -> p h n", h=SSD_H),
                                         view(r_skip, [1, SSD_H], [0, HD]), ALU.mult)
                if tt == tiles[-1]:
                    ins.then_inc(s("y0"), 1)
                else:
                    link(ins)
            pool.wait_ge(s("CB"), past("CB") + 1)
            for i in range(1, len(STEPS)):
                decay(i)
                inputs(i)

        def o_copy(dve, pair):
            f, tt, _ = UN[2 * pair]
            dve.wait_ge(s("o_ps"), past("o_ps") + 2 * pair + 2)
            dve.tensor_copy(catT[:, f, tt * P:(tt + 1) * P], PS[:, 4 + pair % 2, 0:P]).then_inc(s("oT"), 1)

        return {"sp": sp_, "pe": pe_, "act": act_, "dve": dve_, "pool": pool_}

    b0, b1 = hybrid(0), hybrid(1)

    final = {"a0": ("ln_out", 2), "m0": ("ln_out", 4), "a1": ("ln_out", 6), "m1": ("ln_out", 8), "b0": ("b_x2", 4)}
    block = ctx.enter_context(nc.Block())
    stages = ["a0", "m0", "a1", "m1", "b0", "b1"]
    last = stages.index(stop) if stop else len(stages) - 1

    @block.sync
    def _(sp):
        a0_sp(sp)
        if last >= 1:
            m0["sp"](sp)
        if last >= 2:
            a1_sp(sp)
        if last >= 3:
            m1["sp"](sp)
        if last >= 4:
            b0["sp"](sp)
        if last >= 5:
            b1["sp"](sp)
        if stop and last < 5:
            sp.wait_ge(S(final[stop][0]), final[stop][1])
            sp.dma_start(out.rearrange("b (t p) d -> p (b t) d", p=P), X).then_inc(S("out_dma"), 16)
            sp.wait_ge(S("out_dma"), 16)

    @block.tensor
    def _(pe):
        a0_pe(pe)
        if last >= 1:
            m0["pe"](pe)
        if last >= 2:
            a1_pe(pe)
        if last >= 3:
            m1["pe"](pe)
        if last >= 4:
            b0["pe"](pe)
        if last >= 5:
            b1["pe"](pe)

    @block.scalar
    def _(act):
        a0_act(act)
        if last >= 1:
            m0["act"](act)
        if last >= 2:
            a1_act(act)
        if last >= 3:
            m1["act"](act)
        if last >= 4:
            b0["act"](act)
        if last >= 5:
            b1["act"](act)

    @block.gpsimd
    def _(pool):
        link = chain(pool, "pool_step")
        if last >= 4:
            b0["pool"](pool, link)
        if last >= 5:
            b1["pool"](pool, link)

    @block.vector
    def _(dve):
        link = chain(dve, "dve_step")
        a0_dve(dve, link)
        if last >= 1:
            m0["dve"](dve, link)
        if last >= 2:
            a1_dve(dve, link)
        if last >= 3:
            m1["dve"](dve, link)
        if last >= 4:
            b0["dve"](dve, link)
        if last >= 5:
            b1["dve"](dve, link)


_INS = [
    "x", "rel_table", "da_wq", "da_wk", "da_wv", "da_wo", "da_lq1", "da_lk1", "da_lq2", "da_lk2",
    "da_subln_g", "sb_wq", "sb_wk", "sb_wv", "sb_wo", "ln_mix_g", "ln_mix_b", "ln_ffn_g", "ln_ffn_b",
    "moe_w_group", "moe_b_group", "moe_w_expert", "moe_b_expert", "moe_w1", "moe_w3", "moe_w2", "c_2",
    "ctx_2", "c_ctx_2", "w_mod_2", "b_mod_2", "norm_mix_pre_2", "norm_mix_post_2", "norm_ffn_pre_2",
    "norm_ffn_post_2", "w_in_2", "q_norm_2", "k_norm_2", "conv_w_2", "conv_b_2", "dt_bias_fwd_2",
    "dt_bias_bwd_2", "a_log_fwd_2", "a_log_bwd_2", "d_skip_2", "ssd_norm_2", "w_out_2", "w_gate_2", "w_up_2",
    "w_down_2",
]


def kernel(**inputs):
    import numpy as _np
    import concourse.bacc as _bacc
    from concourse import mybir as _mybir
    from concourse.bass_utils import run_bass_kernel_spmd as _run

    nc = _bacc.Bacc("TRN2", target_bir_lowering=False, num_devices=1)
    arrays, t = {}, {}

    def operand(name, a):
        a = _np.ascontiguousarray(a)
        arrays[f"in_{name}_dram"] = a
        t[name] = nc.dram_tensor(f"in_{name}_dram", a.shape, _mybir.dt.from_np(a.dtype), kind="ExternalInput").ap()

    for name in _INS:
        operand(name, inputs[name])
    consts, hot = const_tables()
    operand("consts", consts)
    operand("hot", hot)
    out = nc.dram_tensor("out_0_dram", (1, SEQ, D), F32, kind="ExternalOutput").ap()
    program(nc, t, out)
    r = _run(nc, [arrays], core_ids=[0])
    return r.results[0]["out_0_dram"]
```

```python
import math
from contextlib import ExitStack

import numpy as np
import concourse.bass as bass
from concourse import mybir

F32 = mybir.dt.float32
I32 = mybir.dt.int32
F32R = mybir.dt.float32r
ALU = mybir.AluOpType
ACT = mybir.ActivationFunctionType
AX = mybir.AxisListType

P = 128
D = 1024
KT = D // P
SEQ = 256
NT = SEQ // P
DEPTH = 2
BUCKETS, MAX_DIST = 32, 128
DA_HEADS = 8
N_EXPERTS, GROUPS, PER_GROUP, HIDDEN = 32, 4, 8, 512
ALPHA = (2 * DEPTH) ** 0.25
LN_EPS, EPS = 1e-5, 1e-6
NEG = -1e30
LAM_INIT = 0.8 - 0.6 * math.exp(-0.3 * 0)

RING = 4
SLOT = 8192
PER_SLOT = 32

C_ID, C_LE, C_GE, C_LT, C_GT, C_NEGD, C_NGE, C_IOTA, C_COS, C_SIN = (
    0, 128, 256, 384, 512, 640, 768, 896, 1152, 1216)
C_EPS, C_LN_EPS = 1280, 1281
C_COLS = 1282
LEN_T = 512


def const_tables():
    k, i = np.arange(P)[:, None], np.arange(P)[None, :]
    c = np.zeros((P, C_COLS), np.float32)
    c[:, C_ID:C_ID + P] = k == i
    c[:, C_LE:C_LE + P] = k <= i
    c[:, C_GE:C_GE + P] = k >= i
    c[:, C_LT:C_LT + P] = k < i
    c[:, C_GT:C_GT + P] = k > i
    c[:, C_NEGD:C_NEGD + P] = np.where(k >= i, NEG, 0)
    c[:, C_NGE:C_NGE + P] = -(k >= i).astype(np.float32)
    c[:, C_IOTA:C_IOTA + 256] = np.arange(256)
    n_freq = 16
    freqs = np.float32(10000.0) ** (-np.arange(n_freq, dtype=np.float32) / np.float32(n_freq))
    pos = np.arange(SEQ)
    ang = np.concatenate([(pos // 64).astype(np.float32)[:, None] * freqs,
                          (pos % 64).astype(np.float32)[:, None] * freqs], -1)
    c[:, C_COS:C_COS + 64] = np.cos(ang).reshape(NT, P, 32).transpose(1, 0, 2).reshape(P, 64)
    c[:, C_SIN:C_SIN + 64] = np.sin(ang).reshape(NT, P, 32).transpose(1, 0, 2).reshape(P, 64)
    c[:, C_EPS], c[:, C_LN_EPS] = EPS, LN_EPS
    n = np.arange(LEN_T) - (SEQ - 1)
    half = BUCKETS // 2
    nf = np.maximum(n, 1).astype(np.float32)
    large = half + (np.log(nf / np.float32(half)) / np.float32(math.log(MAX_DIST / half))
                    * np.float32(BUCKETS - half)).astype(np.int32)
    bucket = np.where(n < half, n, np.minimum(large, BUCKETS - 1))
    hot = np.zeros((BUCKETS + 1, LEN_T), np.float32)
    hot[np.where(n < 0, BUCKETS, bucket), np.arange(LEN_T)] = 1
    return c, hot


def view(ap, *free):
    return bass.AP(ap.tensor, ap.offset, [list(ap.ap[0])] + [list(f) for f in free])


def program(nc, t, out, stop=None):
    ctx = ExitStack()
    with ctx:
        build(nc, ctx, t, out, stop)


def build(nc, ctx, t, out, stop):
    sems = {}

    def S(name):
        if name not in sems:
            sems[name] = ctx.enter_context(nc.semaphore(name))
        return sems[name]

    def chain(eng, name):
        n = [0]

        def link(ins):
            n[0] += 1
            ins.then_inc(S(name), 1)
            eng.wait_ge(S(name), n[0])
        return link

    ring_at = -(-nc.sbuf_base // 32) * 32
    ring = ctx.enter_context(nc.sbuf_tensor("ring", [P, RING * SLOT], F32))
    cst = ctx.enter_context(nc.sbuf_tensor("cst", [P, C_COLS], F32))
    small = ctx.enter_context(nc.sbuf_tensor("small", [P, 640], F32))
    ctrl = ctx.enter_context(nc.sbuf_tensor("ctrl", [P, 72], I32))
    ARENA = 18400
    arena_at = -(-nc.sbuf_base // 32) * 32
    arena = ctx.enter_context(nc.sbuf_tensor("arena", [P, ARENA], F32))
    ring_r = [nc.alloc_sbuf_tensor_at(f"ring_r{p}", [P, SLOT], F32R, offset=ring_at + 4 * SLOT * p) for p in range(RING)]
    R_FROM, R_COLS = 4096, 11264
    arena_r = nc.alloc_sbuf_tensor_at("arena_r", [P, R_COLS], F32R, offset=arena_at + 4 * R_FROM)

    def as_r(a):
        r, start = (ring_r[a.offset // SLOT], a.offset // SLOT * SLOT) if a.tensor.name == ring.name else (arena_r, R_FROM)
        return bass.AP(r, a.offset - start, [list(r[:, :].ap[0])] + [list(d) for d in a.ap[1:]])

    PS = ctx.enter_context(nc.psum_tensor("ps", [P, 8, 512], F32))
    scratch = nc.dram_tensor("bias_scratch", [DA_HEADS, LEN_T], F32)

    top = [0]

    def area(cols):
        a = arena[:, top[0]:top[0] + cols]
        top[0] += cols
        assert top[0] <= ARENA, top[0]
        return a

    ident = cst[:, C_ID:C_ID + P]
    eps, ln_eps = cst[:, C_EPS:C_EPS + 1], cst[:, C_LN_EPS:C_LN_EPS + 1]
    X = area(NT * D).rearrange("p (t d) -> p t d", t=NT)
    XT = area(NT * D).rearrange("p (k n) -> p k n", k=KT)
    MARK = top[0]

    def slot(n):
        return ring[:, (n % RING) * SLOT:(n % RING + 1) * SLOT]

    def square(n):
        return slot(n).rearrange("p (k c) -> p k c", k=KT)

    def load_square(sp, n, w):
        rows = w.rearrange("(k p) c -> p k c", p=P)
        for a in range(2):
            sp.dma_start(square(n)[:, 4 * a:4 * a + 4, :], rows[:, 4 * a:4 * a + 4, :]).then_inc(S(f"ring{n % RING}"), 16)

    N_A0, N_M0 = 0, 4
    N_A1 = N_M0 + 48
    N_M1 = N_A1 + 4
    N_B = N_M1 + 48

    def uses(n):
        return n // RING + 1 + (2 * ((n >= N_M0) + (n >= N_M1)) if n % RING < 3 else 0)

    def loaded(eng, n):
        eng.wait_ge(S(f"ring{n % RING}"), PER_SLOT * uses(n))

    TURNS = ("t0", "t1", "m0", "t2", "m1")
    NORMS = ("ln0", "ln1", "ln2", "ln3")

    def pe_turn(pe, src, ntile, tag, ready):
        w = ntile * P
        per_bank = 512 // w
        ready(pe)
        for k in range(KT):
            for tt in range(ntile):
                ins = pe.transpose(PS[:, k // per_bank, (k % per_bank) * w + tt * P:(k % per_bank) * w + (tt + 1) * P],
                                   src[:, tt, k * P:(k + 1) * P], ident)
            if k % per_bank == per_bank - 1:
                ins.then_inc(S("turned"), 1)

    def copy_turn_act(act, dst, tag):
        for b in range(2):
            act.wait_ge(S("turned"), 4 * TURNS.index(tag) + b + 1)
            act.copy(view(dst[:, 2 * b, 0:1], [1, 512]), PS[:, b, :]).then_inc(S("turned_act"), 1)

    def copy_turn_dve(dve, dst, tag):
        for b in range(2, 4):
            dve.wait_ge(S("turned"), 4 * TURNS.index(tag) + b + 1)
            dve.tensor_copy(view(dst[:, 2 * b, 0:1], [1, 512]), PS[:, b, :]).then_inc(S("turned_dve"), 1)

    def turned(eng, tag):
        eng.wait_ge(S("turned_act"), 2 * TURNS.index(tag) + 2)
        eng.wait_ge(S("turned_dve"), 2 * TURNS.index(tag) + 2)

    def pe_columns(pe, w, xT, bank, sem):
        for f in range(KT):
            o = PS[:, bank + f // 2, (f % 2) * 256:(f % 2) * 256 + 256]
            for k in range(KT):
                ins = pe.matmul(o, w[:, k, f * P:(f + 1) * P], xT[:, k, 0:256], start=(k == 0), stop=(k == KT - 1))
            if f % 2:
                ins.then_inc(S(sem), 1)

    def pe_rows(pe, w, xT, bank, sem):
        for tt in range(NT):
            for h in range(2):
                for k in range(KT):
                    ins = pe.matmul(PS[:, bank + 2 * tt + h, :], xT[:, k, tt * P:(tt + 1) * P],
                                    w[:, k, h * 512:(h + 1) * 512], start=(k == 0), stop=(k == KT - 1))
                ins.then_inc(S(sem), 1)

    def dve_layer_norm(dve, link, mix, mix_ready, g, b, params_ready, work, tag):
        xr, st = work
        n0 = NT * NORMS.index(tag)
        mv, sd = small[:, 0:2], small[:, 2:4]
        for tt in range(NT):
            for h in range(2):
                mix_ready(dve, tt, h)
                link(dve.scalar_tensor_tensor(xr[:, h * 512:(h + 1) * 512], X[:, tt, h * 512:(h + 1) * 512], ALPHA,
                                              mix(tt, h), ALU.mult, ALU.add))
                link(dve.bn_stats(st[:, 6 * h:6 * h + 6], xr[:, h * 512:(h + 1) * 512]))
            if tt:
                dve.wait_ge(S("ln_sd"), n0 + tt)
            dve.bn_aggr(mv, st[:, 0:12]).then_inc(S("ln_var"), 1)
            dve.wait_ge(S("ln_sd"), n0 + tt + 1)
            link(dve.reciprocal(sd[:, 1:2], sd[:, 1:2]))
            if tt == 0:
                params_ready(dve)
            link(dve.scalar_tensor_tensor(xr, xr, mv[:, 0:1], g, ALU.subtract, ALU.mult))
            dve.scalar_tensor_tensor(X[:, tt, :], xr, sd[:, 1:2], b, ALU.mult, ALU.add).then_inc(S("ln_out"), 1)
            dve.wait_ge(S("ln_out"), n0 + tt + 1)

    def act_layer_norm(act, tag):
        mv, sd = small[:, 0:2], small[:, 2:4]
        n0 = NT * NORMS.index(tag)
        for tt in range(NT):
            act.wait_ge(S("ln_var"), n0 + tt + 1)
            act.activation(sd[:, 1:2], mv[:, 1:2], ACT.Sqrt, bias=ln_eps).then_inc(S("ln_sd"), 1)

    N_MOD = 6
    mod_rows = nc.dram_tensor("mod_rows", [DEPTH, P, N_MOD, 256], F32)
    mod_buf = arena[:, ARENA - 512:ARENA].rearrange("p (b n) -> p b n", b=2)
    c_rows = arena[0:2 * KT, ARENA - 640:ARENA - 512]
    ccz = small[:, 204:460].rearrange("p (k m) -> p k m", k=KT)
    MOD_PLACE = (0, 1, 0, 2, 1, 2)
    MOD_USE = (0, 0, 1, 0, 1, 1)
    after_mod = lambda l: (("mod", N_MOD * l + 3), ("mod", N_MOD * l + 5), ("mod", N_MOD * l + 6), ("mix", 4 * l + 4))

    def mod_weights(m):
        p = MOD_PLACE[m]
        return ring[:, p * SLOT:(p + 1) * SLOT].rearrange("p (k c) -> p k c", k=KT)

    def mod_sp(sp, l, v_done):
        def load(m, name, v):
            sp.wait_ge(S(name), v)
            rows = t["w_mod_2"][l, :, m * D:(m + 1) * D].rearrange("(k p) c -> p k c", p=P)
            for a in range(2):
                sp.dma_start(mod_weights(m)[:, 4 * a:4 * a + 4, :], rows[:, 4 * a:4 * a + 4, :])\
                  .then_inc(S(f"ring{MOD_PLACE[m]}"), 16)

        def store(m):
            n = N_MOD * l + m
            sp.wait_ge(S("modrow"), n + 1)
            if n:
                sp.wait_ge(S("mod_out"), 16 * n)
            sp.dma_start(mod_rows.ap()[l, :, m, :], mod_buf[:, m % 2, :]).then_inc(S("mod_out"), 16)
        load(0, "q", 4 * l + 4)
        load(1, "k", 4 * l + 4)
        load(2, "mod", N_MOD * l + 1)
        store(0)
        sp.wait_ge(S("v"), 4 * l + 4)
        v_done(sp)
        load(3, "v", 4 * l + 4)
        load(4, "mod", N_MOD * l + 2)
        store(1)
        store(2)
        load(5, "mod", N_MOD * l + 4)
        for m in range(3, N_MOD):
            store(m)

    def mod_pe(pe, l, m, bank, before):
        n = N_MOD * l + m
        pe.wait_ge(S(f"ring{MOD_PLACE[m]}"), PER_SLOT * (uses((N_A0, N_A1)[l] + MOD_PLACE[m]) + 1 + MOD_USE[m]))
        pe.wait_ge(S("cc1"), 2)
        if before is not None:
            pe.wait_ge(S("modrow"), N_MOD * l + before + 1)
        w = mod_weights(m)
        for k in range(KT):
            for j in range(4):
                ins = pe.matmul(PS[32 * j:32 * j + 32, bank, 0:256], ccz[:, k, :], w[:, k, 256 * j:256 * j + 256],
                                start=(k == 0), stop=(k == KT - 1))
        ins.then_inc(S("mod"), 1)

    def mod_dve(dve, l, m, bank):
        n = N_MOD * l + m
        dve.wait_ge(S("mod"), n + 1)
        if n >= 2:
            dve.wait_ge(S("mod_out"), 16 * (n - 1))
        dve.tensor_copy(mod_buf[:, m % 2, :], PS[:, bank, 0:256]).then_inc(S("modrow"), 1)

    top[0] = MARK
    qz = area(2 * KT * 256).rearrange("p (c f n) -> p c f n", c=2, f=KT)
    kT = area(KT * 256).rearrange("p (f n) -> p f n", f=KT)
    V = area(NT * D).rearrange("p (t d) -> p t d", t=NT)
    O = area(NT * D).rearrange("p (t d) -> p t d", t=NT)
    Lg = area(2 * 512).rearrange("p (b c n) -> p b c n", b=2, c=2)
    Ex = area(2 * 512).rearrange("p (b c n) -> p b c n", b=2, c=2)
    At = area(2 * 256).rearrange("p (b n) -> p b n", b=2)
    AtT = area(2 * 256).rearrange("p (b k n) -> p b k n", b=2, k=2)
    bias = XT.rearrange("p k n -> p (k n)").rearrange("p (h n) -> p h n", h=DA_HEADS)
    hot_sb = Ex[0:BUCKETS + 1, 0].rearrange("p c n -> p (c n)")
    rel_sb = Lg[0:BUCKETS + 1, 0, 0, 0:DA_HEADS]
    tab_sb = Lg[0:DA_HEADS, 1].rearrange("p c n -> p (c n)")
    lam4 = At[:, 0, :].rearrange("p (a n) -> p a n", a=4)
    da_g = AtT[:, 0, 0, :]
    lam_s, neg_lam = small[:, 8:12], small[:, 12:13]
    nmax, ssum, rsum = small[:, 16:20], small[:, 20:24], small[:, 24:28]
    o_ss = small[:, 32:48]
    gain = small[:, 64:192]
    lnp = view(qz[:, 0, 0, 0:1], [1, 2048])
    xr = view(qz[:, 1, 0, 0:1], [1, 1024])
    st = small[:, 192:204]
    UNITS = DA_HEADS * NT
    MOD_UNITS = (4, 7, 10)

    def load_ln(sp, gname, bname, layer, dst, sem):
        sp.dma_start(dst[:, 0:D], bass.AP(t[gname].tensor, layer * D, [[0, P], [1, D]])).then_inc(S(sem), 16)
        sp.dma_start(dst[:, D:2 * D], bass.AP(t[bname].tensor, layer * D, [[0, P], [1, D]])).then_inc(S(sem), 16)

    def a0_sp(sp):
        sp.dma_start(X, t["x"].rearrange("b (t p) d -> p (b t) d", p=P)).then_inc(S("x_in"), 16)
        sp.dma_start(cst[:, :], t["consts"]).then_inc(S("consts_in"), 16)
        for v, name in enumerate(("c_2", "c_ctx_2")):
            sp.dma_start(c_rows[KT * v:KT * v + KT, :], bass.AP(t[name].tensor, 0, [[P, KT], [1, P]])).then_inc(S("tables_in"), 16)
        sp.dma_start(rel_sb[0:BUCKETS, :], t["rel_table"]).then_inc(S("tables_in"), 16)
        sp.dma_start(hot_sb, t["hot"]).then_inc(S("tables_in"), 16)
        for n, name in enumerate(("da_lq1", "da_lk1", "da_lq2", "da_lk2")):
            sp.dma_start(lam4[:, n, :], bass.AP(t[name].tensor, 0, [[0, P], [1, 64]])).then_inc(S("lam_in"), 16)
        sp.dma_start(gain, bass.AP(t["da_subln_g"].tensor, 0, [[0, P], [1, P]])).then_inc(S("lam_in"), 16)
        load_square(sp, 0, t["da_wq"][0])
        load_square(sp, 1, t["da_wk"][0])
        load_square(sp, 2, t["da_wv"][0])
        load_square(sp, 3, t["da_wo"][0])
        sp.wait_ge(S("cc1"), 3)
        sp.dma_start(scratch.ap(), tab_sb).then_inc(S("tab_dma"), 16)
        sp.wait_ge(S("tab_dma"), 16)
        mod_sp(sp, 0, lambda e: e.dma_start(bias, bass.AP(scratch, P, [[1, P], [LEN_T, DA_HEADS], [1, SEQ]]))
               .then_inc(S("tab_dma"), 16))

    def a0_norm_sp(sp):
        sp.wait_ge(S("scores"), UNITS)
        load_ln(sp, "ln_mix_g", "ln_mix_b", 0, lnp, "ln_in0")

    def a0_pe(pe):
        pe.wait_ge(S("consts_in"), 16)
        pe_turn(pe, X, NT, "t0", lambda e: e.wait_ge(S("x_in"), 16))
        turned(pe, "t0")
        pe.wait_ge(S("tables_in"), 64)
        pe.wait_ge(S("zero"), 3)
        pe.matmul(PS[0:DA_HEADS, 0, :], rel_sb, hot_sb, start=True, stop=True).then_inc(S("tab_ps"), 1)
        pe.transpose(PS[:, 7, 0:2 * KT], c_rows, ident[0:2 * KT, 0:2 * KT]).then_inc(S("cc0"), 1)
        loaded(pe, 0)
        pe.wait_ge(S("cc1"), 2)
        pe_columns(pe, square(0), XT, 4, "q")
        loaded(pe, 1)
        pe.wait_ge(S("cc1"), 3)
        pe_columns(pe, square(1), XT, 0, "k")
        pe.wait_ge(S("k_act"), 2)
        pe.wait_ge(S("k_dve"), 2)
        mod_pe(pe, 0, 0, 2, None)
        loaded(pe, 2)
        pe.wait_ge(S("q_act"), 2)
        pe.wait_ge(S("q_dve"), 2)
        pe_rows(pe, square(2), XT, 4, "v")
        mod_pe(pe, 0, 1, 3, None)
        mod_pe(pe, 0, 2, 2, 0)

        def z(u):
            h, i = divmod(u, 2)
            nk = P * (i + 1)
            if u < 2:
                pe.wait_ge(S("v_act"), 2)
                pe.wait_ge(S("v_dve"), 2)
            else:
                pe.wait_ge(S("da_logits"), u - 1)
            for c in range(2):
                ins = pe.matmul(PS[:, 4 + u % 2, c * 256:c * 256 + nk], qz[:, c, h, i * P:(i + 1) * P], kT[:, h, 0:nk],
                                start=True, stop=True)
            ins.then_inc(S("scores"), 1)

        def turn_weights(u):
            pe.wait_ge(S("da_attn"), u + 1)
            if u >= 2:
                pe.wait_ge(S("da_attn_sb"), u - 1)
            for kb in range(u % 2 + 1):
                ins = pe.transpose(PS[:, 6 + u % 2, kb * P:(kb + 1) * P], At[:, u % 2, kb * P:(kb + 1) * P], ident)
            ins.then_inc(S("da_attn_t"), 1)

        def values(u):
            h, i = divmod(u, 2)
            pe.wait_ge(S("da_attn_sb"), u + 1)
            if u >= 2:
                pe.wait_ge(S("values_out"), u - 1)
            for kb in range(i + 1):
                ins = pe.matmul(PS[:, u % 2, 0:P], AtT[:, u % 2, kb, :], V[:, kb, h * P:(h + 1) * P],
                                start=(kb == 0), stop=(kb == i))
            ins.then_inc(S("values"), 1)

        z(0)
        z(1)
        for u in range(UNITS):
            if u + 2 < UNITS:
                z(u + 2)
            turn_weights(u)
            if u in MOD_UNITS:
                m = 3 + MOD_UNITS.index(u)
                mod_pe(pe, 0, m, 2 + m % 2, m - 2)
            if u:
                values(u - 1)
        values(UNITS - 1)
        pe_turn(pe, O, NT, "t1", lambda e: e.wait_ge(S("da_out"), 1))
        loaded(pe, 3)
        turned(pe, "t1")
        pe_rows(pe, square(3), XT, 4, "mix")

    def a0_act(act):
        copy_turn_act(act, XT, "t0")
        act.wait_ge(S("cc0"), 2)
        for v in range(2):
            act.activation(ccz[:, :, v:v + 1], PS[:, 7, KT * v:KT * v + KT].rearrange("p (k m) -> p k m", m=1), ACT.Silu)\
               .then_inc(S("cc1"), 1)
        act.wait_ge(S("tab_ps"), 1)
        act.copy(tab_sb, PS[0:DA_HEADS, 0, :]).then_inc(S("cc1"), 1)
        act.wait_ge(S("zero"), 1)

        def heads(bank, sem, out_sem, scale):
            for b in (0, 2):
                act.wait_ge(S(sem), b + 1)
                for c in range(2):
                    if scale:
                        ins = act.mul(qz[64 * c:64 * c + 64, c, 2 * b:2 * b + 2, :],
                                      PS[64 * c:64 * c + 64, bank + b, :].rearrange("p (f n) -> p f n", f=2), 0.125)
                if not scale:
                    ins = act.copy(kT[:, 2 * b:2 * b + 2, :], PS[:, bank + b, :].rearrange("p (f n) -> p f n", f=2))
                ins.then_inc(S(out_sem), 1)
        heads(4, "q", "q_act", True)
        heads(0, "k", "k_act", False)
        for b in range(2):
            act.wait_ge(S("v"), 2 * b + 1)
            act.copy(V[:, b, 0:512], PS[:, 4 + 2 * b, :]).then_inc(S("v_act"), 1)
        act.wait_ge(S("lam_dot"), 1)
        act.activation(lam_s[:, 2:4], lam_s[:, 0:2], ACT.Exp).then_inc(S("lam_exp"), 1)

        def expo(u):
            nk = P * (u % 2 + 1)
            act.wait_ge(S("da_max"), u + 1)
            if u >= 2:
                act.wait_ge(S("da_attn"), u - 1)
            for c in range(2):
                ins = act.activation(Ex[:, u % 2, c, 0:nk], Lg[:, u % 2, c, 0:nk], ACT.Exp,
                                     bias=nmax[:, 2 * (u % 2) + c:2 * (u % 2) + c + 1],
                                     accum_out=ssum[:, 2 * (u % 2) + c:2 * (u % 2) + c + 1])
            ins.then_inc(S("da_exp"), 1)

        def output(u):
            h, i = divmod(u, 2)
            act.wait_ge(S("values"), u + 1)
            act.copy(O[:, i, h * P:(h + 1) * P], PS[:, u % 2, 0:P]).then_inc(S("values_out"), 1)

        expo(0)
        expo(1)
        for u in range(UNITS):
            i = u % 2
            act.wait_ge(S("da_attn_t"), u + 1)
            if u >= 2:
                act.wait_ge(S("values"), u - 1)
            act.copy(view(AtT[:, u % 2, 0, 0:1], [1, P * (i + 1)]), PS[:, 6 + u % 2, 0:P * (i + 1)]).then_inc(S("da_attn_sb"), 1)
            if u + 2 < UNITS:
                expo(u + 2)
            if u:
                output(u - 1)
        output(UNITS - 1)
        act.wait_ge(S("da_ms"), 1)
        act.activation(o_ss, o_ss, ACT.Sqrt, scale=1.0 / P, bias=eps).then_inc(S("da_sd"), 1)
        copy_turn_act(act, XT, "t1")
        act_layer_norm(act, "ln0")

    def a0_dve(dve, link):
        dve.memset(view(qz[:, 0, 0, 0:1], [1, 4096]), 0.0).then_inc(S("zero"), 1)
        dve.memset(rel_sb[BUCKETS:BUCKETS + 1, :], NEG).then_inc(S("zero"), 2)
        dve.memset(view(ccz[:, 0, 0:1], [1, 256]), 0.0).then_inc(S("cc0"), 1)
        copy_turn_dve(dve, XT, "t0")
        dve.wait_ge(S("lam_in"), 80)
        link(dve.tensor_tensor(lam4[:, 0:3:2, :], lam4[:, 0:3:2, :], lam4[:, 1:4:2, :], ALU.mult))
        dve.tensor_reduce(lam_s[:, 0:2], lam4[:, 0:3:2, :], AX.X, ALU.add).then_inc(S("lam_dot"), 1)
        dve.wait_ge(S("zero"), 1)
        for b in (1, 3):
            dve.wait_ge(S("q"), b + 1)
            for c in range(2):
                ins = dve.tensor_scalar(qz[64 * c:64 * c + 64, c, 2 * b:2 * b + 2, :],
                                        PS[64 * c:64 * c + 64, 4 + b, :].rearrange("p (f n) -> p f n", f=2), 0.125, None, ALU.mult)
            ins.then_inc(S("q_dve"), 1)
        for b in (1, 3):
            dve.wait_ge(S("k"), b + 1)
            dve.tensor_copy(kT[:, 2 * b:2 * b + 2, :], PS[:, b, :].rearrange("p (f n) -> p f n", f=2)).then_inc(S("k_dve"), 1)
        mod_dve(dve, 0, 0, 2)
        for b in range(2):
            dve.wait_ge(S("v"), 2 * b + 2)
            dve.tensor_copy(V[:, b, 512:1024], PS[:, 5 + 2 * b, :]).then_inc(S("v_dve"), 1)
        mod_dve(dve, 0, 1, 3)
        mod_dve(dve, 0, 2, 2)
        dve.wait_ge(S("lam_exp"), 1)
        link(dve.tensor_tensor(neg_lam, lam_s[:, 3:4], lam_s[:, 2:3], ALU.subtract))
        link(dve.tensor_scalar(neg_lam, neg_lam, -LAM_INIT, None, ALU.add))
        dve.wait_ge(S("tab_dma"), 16)

        def logits(u):
            h, i = divmod(u, 2)
            nk = P * (i + 1)
            dve.wait_ge(S("scores"), u + 1)
            if u == 0:
                dve.wait_ge(S("tab_dma"), 32)
            if u >= 2:
                dve.wait_ge(S("da_exp"), u - 1)
            b = view(bias[:, h, P * i + P - 1:P * i + P], [0, 2], [-1, nk])
            dve.tensor_tensor(Lg[:, u % 2, :, 0:nk], PS[:, 4 + u % 2, :].rearrange("p (c n) -> p c n", c=2)[:, :, 0:nk], b,
                              ALU.add).then_inc(S("da_logits"), 1)
            dve.wait_ge(S("da_logits"), u + 1)
            dve.tensor_reduce(nmax[:, 2 * (u % 2):2 * (u % 2) + 2], Lg[:, u % 2, :, 0:nk], AX.X, ALU.max,
                              negate=True).then_inc(S("da_max"), 1)

        def combine(u):
            i = u % 2
            nk = P * (i + 1)
            b = 2 * (u % 2)
            dve.wait_ge(S("da_exp"), u + 1)
            link(dve.reciprocal(rsum[:, b:b + 2], ssum[:, b:b + 2]))
            link(dve.tensor_scalar(rsum[:, b + 1:b + 2], rsum[:, b + 1:b + 2], neg_lam, None, ALU.mult))
            link(dve.tensor_scalar(Ex[:, u % 2, 1, 0:nk], Ex[:, u % 2, 1, 0:nk], rsum[:, b + 1:b + 2], None, ALU.mult))
            if u >= 2:
                dve.wait_ge(S("da_attn_t"), u - 1)
            dve.scalar_tensor_tensor(At[:, u % 2, 0:nk], Ex[:, u % 2, 0, 0:nk], rsum[:, b:b + 1], Ex[:, u % 2, 1, 0:nk],
                                     ALU.mult, ALU.add).then_inc(S("da_attn"), 1)

        logits(0)
        logits(1)
        for u in range(UNITS):
            combine(u)
            if u + 2 < UNITS:
                logits(u + 2)
            if u - 1 in MOD_UNITS:
                m = 3 + MOD_UNITS.index(u - 1)
                mod_dve(dve, 0, m, 2 + m % 2)
        dve.wait_ge(S("values_out"), UNITS)
        sq = view(kT[:, 0, 0:1], [1, 2048])
        Of = view(O[:, 0, 0:1], [1, 2048])
        link(dve.tensor_tensor(sq, Of, Of, ALU.mult))
        dve.tensor_reduce(o_ss, sq.rearrange("p (h e) -> p h e", e=P), AX.X, ALU.add).then_inc(S("da_ms"), 1)
        dve.wait_ge(S("lam_in"), 80)
        link(dve.tensor_scalar(gain, gain, 1.0 - LAM_INIT, None, ALU.mult))
        dve.wait_ge(S("da_sd"), 1)
        link(dve.reciprocal(o_ss, o_ss))
        Oh = Of.rearrange("p (h e) -> p h e", e=P)
        link(dve.tensor_tensor(Oh, Oh, view(o_ss[:, 0:1], [1, 16], [0, P]), ALU.mult))
        dve.tensor_tensor(Oh, Oh, view(gain[:, 0:1], [0, 16], [1, P]), ALU.mult).then_inc(S("da_out"), 1)
        copy_turn_dve(dve, XT, "t1")
        dve_layer_norm(dve, link, lambda tt, h: PS[:, 4 + 2 * tt + h, :],
                       lambda e, tt, h: e.wait_ge(S("mix"), 2 * tt + h + 1),
                       lnp[:, 0:D], lnp[:, D:2 * D], lambda e: e.wait_ge(S("ln_in0"), 32), (xr, st), "ln0")

    CAP = 64
    PAIRS = N_EXPERTS // 2
    UNROLL = 4
    MOE_BASE = MARK + 4096

    def moe(layer, tag, n0, params_free, first_free, ln_tag, x_ready, norm_sp):
        top[0] = MOE_BASE
        s = lambda name: S(f"moe_{name}")
        wr = area(KT * 36).rearrange("p (k n) -> p k n", k=KT)
        brow = area(36)
        lnp = area(2 * D)
        xr = area(D)
        ones = area(P)
        zeros = area(512)
        lg = area(72).rearrange("p (t n) -> p t n", t=NT)
        g4a, g4b = area(8).rearrange("p (t n) -> p t n", t=NT), area(8).rearrange("p (t n) -> p t n", t=NT)
        desc = area(32)
        M, oh1, oh2, tmp, mask, gates, rank = (area(64).rearrange("p (t n) -> p t n", t=NT) for _ in range(7))
        c2 = area(32)
        col = lambda n: c2[:, 2 * n:2 * n + 2]
        gmax, gsum, tm, m1, m2, ex, wa, wb = (col(n) for n in range(8))
        pm, rounds, base = area(16), area(16), area(17)
        sel = area(256).rearrange("p (t e c) -> p t e c", t=NT, e=2)
        selg = area(256).rearrange("p (t s) -> p t s", t=NT)
        sgT = area(256)
        xeT = area(KT * P).rearrange("p (k s) -> p k s", k=KT)
        hs, hh = area(HIDDEN), area(HIDDEN)
        hT = area(512).rearrange("p (k s) -> p k s", k=4)
        Y = area(D)
        st = small[:, 192:204]
        cR, cB = 36 * layer, 36 * layer + 16
        b2 = lambda a, n: view(a, [1, NT], [0, n])

        w_up = lambda name, e: t[name][layer, e, :, :].rearrange("a (k p) n -> p (a k) n", p=P)

        def load(sp, n, name, p):
            dst = ring[:, (n % RING) * SLOT:(n % RING + 1) * SLOT].rearrange("p (e k n) -> p e k n", e=2, k=4 if name == "moe_w2" else KT)
            for e in range(2):
                sp.dma_start(dst[:, e], w_up(name, bass.ds(2 * p + e, 1))).then_inc(S(f"ring{n % RING}"), 16)

        def sp_(sp):
            load(sp, *first(sp, 0))
            norm_sp(sp)
            for c in range(1, 3):
                load(sp, *first(sp, c))
            params_free(sp)
            sp.dma_start(wr[:, :, 0:GROUPS], t["moe_w_group"][layer].rearrange("(k p) n -> p k n", p=P)).then_inc(s("router_in"), 16)
            sp.dma_start(wr[:, :, GROUPS:36], t["moe_w_expert"][layer].rearrange("(k p) n -> p k n", p=P)).then_inc(s("router_in"), 16)
            sp.dma_start(brow[:, 0:GROUPS], bass.AP(t["moe_b_group"].tensor, layer * GROUPS, [[0, P], [1, GROUPS]])).then_inc(s("router_in"), 16)
            sp.dma_start(brow[:, GROUPS:36], bass.AP(t["moe_b_expert"].tensor, layer * N_EXPERTS, [[0, P], [1, N_EXPERTS]])).then_inc(s("router_in"), 16)
            load_ln(sp, "ln_ffn_g", "ln_ffn_b", layer, lnp, "ln_in1")
            load(sp, *first(sp, 3))
            sp.wait_ge(s("ctrl"), layer + 1)

            def step(sp, p, o):
                done = sp.value_load(ctrl[0:1, bass.ds(cB + p, 1)], min_val=1, max_val=128)
                sp.wait_ge(s("h1"), done)
                load(sp, n0 + o + 1, "moe_w3", p)
                sp.wait_ge(s("h3"), done)
                load(sp, n0 + o + 2, "moe_w2", p)
                return done
            with sp.Fori(0, PAIRS // UNROLL - 1) as it:
                for j in range(1, UNROLL + 1):
                    done = step(sp, it * UNROLL + j, 3 * j)
                    sp.wait_ge(s("y"), done)
                    load(sp, n0 + 3 * j + 3, "moe_w1", it * UNROLL + j + 1)
            for p in range(PAIRS - UNROLL + 1, PAIRS):
                done = step(sp, p, 3 * p)
                if p + 1 < PAIRS:
                    sp.wait_ge(s("y"), done)
                    load(sp, n0 + 3 * p + 3, "moe_w1", p + 1)

        def first(sp, c):
            sp.wait_ge(S(first_free[c][0]), first_free[c][1])
            return n0 + c, ("moe_w1", "moe_w3", "moe_w2")[c % 3], c // 3

        def freed(sp, c):
            total = sp.value_load(ctrl[0:1, cB + PAIRS - (c == 0):cB + PAIRS - (c == 0) + 1], min_val=1, max_val=128)
            sp.wait_ge(s(("y", "h1", "h3", "y")[c]), total)

        def for_rounds(eng, body):
            eng.wait_ge(s("ctrl"), layer + 1)
            with eng.Fori(0, PAIRS // UNROLL) as it:
                for j in range(UNROLL):
                    n_rounds = eng.value_load(ctrl[0:1, bass.ds(it * UNROLL + (cR + j), 1)], min_val=1, max_val=4)
                    before = eng.value_load(ctrl[0:1, bass.ds(it * UNROLL + (cB + j), 1)], min_val=0, max_val=128)
                    with eng.Fori(0, n_rounds) as r:
                        body(j, it, r, before + r)

        def pe_(pe):
            pe_turn(pe, X, NT, tag, x_ready)
            pe.wait_ge(s("router_in"), 64 * layer + 64)
            turned(pe, tag)
            for tt in range(NT):
                for k in range(KT):
                    ins = pe.matmul(PS[:, 0, 36 * tt:36 * tt + 36], XT[:, k, tt * P:(tt + 1) * P], wr[:, k, :],
                                    start=(k == 0), stop=(k == KT - 1))
            ins.then_inc(s("router_ps"), 1)
            pe.wait_ge(s("mask"), layer + 1)
            lt = cst[:, C_LT:C_LT + P]
            for o, terms in ((0, ((lt, 0),)), (32, ((ones, 0), (lt, 1))), (64, ((ones, 0), (ones, 1)))):
                for a, (w, tt) in enumerate(terms):
                    ins = pe.matmul(PS[:, 1, o:o + 32], w, mask[:, tt, :], start=(a == 0), stop=(a == len(terms) - 1))
            ins.then_inc(s("router_ps"), 1)
            for b in range(4):
                ins = pe.matmul(PS[:, 4 + b, :], zeros[:, 0:P], zeros, start=True, stop=False, skip_group_check=True)
            ins.then_inc(s("sgT_ps"), 1)

            def scatter(last=False):
                for tt in range(NT):
                    for h in range(2):
                        ins = pe.matmul(PS[:, 4 + 2 * tt + h, :], sgT[:, tt * P:(tt + 1) * P], Y[:, h * 512:(h + 1) * 512],
                                        start=False, stop=last, skip_group_check=True)
                return ins

            def body(j, it, r, g):
                w = [slot(n0 + 3 * j + c).rearrange("p (e k n) -> p e k n", e=2, k=(KT, KT, 4)[c]) for c in range(3)]

                def arrived(c):
                    pe.wait_ge(S(f"ring{(n0 + 3 * j + c) % RING}"),
                               it * (3 * PER_SLOT) + PER_SLOT * uses(n0 + 3 * j + c))
                pe.wait_ge(s("sel"), g + 1)
                pe.wait_ge(s("y_act"), g + (1 + layer))
                pe.wait_ge(s("y_dve"), g + (1 + layer))
                for k in range(KT):
                    for tt in range(NT):
                        ins = pe.matmul(PS[:, k // 4, (k % 4) * P:(k % 4 + 1) * P], X[:, tt, k * P:(k + 1) * P],
                                        view(sel[:, tt, 0, 0:1], [1, P]), start=(tt == 0), stop=(tt == NT - 1))
                    if k == 3:
                        ins.then_inc(s("xe"), 1)
                ins.then_inc(s("xe"), 1)
                scatter()
                for tt in range(NT):
                    ins = pe.transpose(PS[:, 3, tt * P:(tt + 1) * P], selg[:, tt, :], ident)
                ins.then_inc(s("sgT_ps"), 1)
                pe.wait_ge(s("xe_act"), g + 1)
                pe.wait_ge(s("xe_dve"), g + 1)
                for c, sem in ((0, "h1"), (1, "h3")):
                    arrived(c)
                    if c == 1:
                        pe.wait_ge(s("sgT"), g + (2 + layer))
                    for k in range(KT):
                        for e in range(2):
                            ins = pe.matmul(PS[CAP * e:CAP * e + CAP, 2 + c, :], xeT[:, k, CAP * e:CAP * e + CAP], w[c][:, e, k, :],
                                            start=(k == 0), stop=(k == KT - 1))
                    ins.then_inc(s(sem), 1)
                pe.wait_ge(s("h"), g + 1)
                for k in range(4):
                    ins = pe.transpose(PS[:, 2, k * P:(k + 1) * P], hh[:, k * P:(k + 1) * P], ident)
                ins.then_inc(s("hT_ps"), 1)
                pe.wait_ge(s("hT"), g + 1)
                arrived(2)
                for h in range(2):
                    for k in range(4):
                        for e in range(2):
                            ins = pe.matmul(PS[CAP * e:CAP * e + CAP, h, :], hT[:, k, CAP * e:CAP * e + CAP],
                                            w[2][:, e, k, h * 512:(h + 1) * 512], start=(k == 0), stop=(k == 3))
                    if h == 0:
                        ins.then_inc(s("y_half"), 1)
                ins.then_inc(s("y"), 1)
            for_rounds(pe, body)
            total = pe.value_load(ctrl[0:1, cB + PAIRS:cB + PAIRS + 1], min_val=1, max_val=128)
            pe.wait_ge(s("y_act"), total + (1 + layer))
            pe.wait_ge(s("y_dve"), total + (1 + layer))
            scatter(last=True).then_inc(s("done"), 1)

        def act_(act):
            copy_turn_act(act, XT, tag)
            act.wait_ge(s("router_arg"), 2 * layer + 1)
            act.activation(g4a, g4a, ACT.Exp).then_inc(s("router_exp"), 1)
            act.wait_ge(s("router_arg"), 2 * layer + 2)
            act.activation(ex, ex, ACT.Exp).then_inc(s("router_exp"), 1)
            act.wait_ge(s("zeros"), layer + 1)
            act.copy(sgT, view(zeros, [1, 256])).then_inc(s("sgT"), 1)
            act.copy(Y[:, 0:512], zeros).then_inc(s("y_act"), 1)

            def body(j, it, r, g):
                act.wait_ge(s("xe"), g * 2 + 1)
                act.copy(view(xeT[:, 0, 0:1], [1, 512]), PS[:, 0, :]).then_inc(s("xe_act"), 1)
                act.wait_ge(s("sgT_ps"), g + (2 + layer))
                act.copy(sgT, PS[:, 3, 0:256]).then_inc(s("sgT"), 1)
                act.wait_ge(s("h1"), g + 1)
                act.activation(hs, PS[:, 2, :], ACT.Silu).then_inc(s("silu"), 1)
                act.wait_ge(s("hT_ps"), g + 1)
                act.copy(view(hT[:, 0, 0:1], [1, 512]), PS[:, 2, :]).then_inc(s("hT"), 1)
                act.wait_ge(s("y_half"), g + 1)
                act.copy(Y[:, 0:512], PS[:, 0, :]).then_inc(s("y_act"), 1)
            for_rounds(act, body)
            act_layer_norm(act, ln_tag)

        def dve_(dve, link):
            params_free(dve)
            link(dve.memset(ones, 1.0))
            dve.memset(zeros, 0.0).then_inc(s("zeros"), 1)
            dve.wait_ge(s("zeros"), layer + 1)
            dve.tensor_copy(Y[:, 512:D], zeros).then_inc(s("y_dve"), 1)
            link(dve.tensor_scalar(desc, cst[:, C_IOTA:C_IOTA + 32], -1.0, 32.0, ALU.mult, ALU.add))
            copy_turn_dve(dve, XT, tag)
            dve.wait_ge(s("router_in"), 64 * layer + 64)
            dve.wait_ge(s("router_ps"), 2 * layer + 1)
            link(dve.tensor_tensor(lg, PS[:, 0, 0:72].rearrange("p (t n) -> p t n", t=NT), view(brow, [0, NT], [1, 36]), ALU.add))
            l4 = lg[:, :, 0:GROUPS]
            link(dve.tensor_reduce(gmax, l4, AX.X, ALU.max))
            dve.tensor_tensor(g4a, l4, b2(gmax, 4), ALU.subtract).then_inc(s("router_arg"), 1)
            link(dve.tensor_tensor(g4b, l4, b2(gmax, 4), ALU.is_ge))
            link(dve.tensor_tensor(g4b, g4b, view(desc, [0, NT], [1, 4]), ALU.mult))
            link(dve.tensor_reduce(tm, g4b, AX.X, ALU.max))
            link(dve.tensor_tensor(g4b, g4b, b2(tm, 4), ALU.is_equal))
            link(dve.tensor_scalar(g4b, g4b, -NEG, NEG, ALU.mult, ALU.add))
            link(dve.tensor_tensor(M.rearrange("p t (g e) -> p t g e", g=GROUPS),
                                   lg[:, :, GROUPS:36].rearrange("p t (g e) -> p t g e", g=GROUPS),
                                   view(g4b[:, 0, 0:1], [4, NT], [1, GROUPS], [0, PER_GROUP]), ALU.add))

            def best(top_val, onehot):
                link(dve.tensor_reduce(top_val, M, AX.X, ALU.max))
                link(dve.tensor_tensor(onehot, M, b2(top_val, 32), ALU.is_ge))
                link(dve.tensor_tensor(onehot, onehot, view(desc, [0, NT], [1, 32]), ALU.mult))
                link(dve.tensor_reduce(tm, onehot, AX.X, ALU.max))
                link(dve.tensor_tensor(onehot, onehot, b2(tm, 32), ALU.is_equal))
            best(m1, oh1)
            link(dve.scalar_tensor_tensor(M, oh1, NEG, M, ALU.mult, ALU.add))
            best(m2, oh2)
            dve.tensor_tensor(ex, m2, m1, ALU.subtract).then_inc(s("router_arg"), 1)
            dve.tensor_tensor(mask, oh1, oh2, ALU.add).then_inc(s("mask"), 1)
            dve.wait_ge(s("router_exp"), 2 * layer + 1)
            link(dve.tensor_reduce(gsum, g4a, AX.X, ALU.add))
            dve.wait_ge(s("router_exp"), 2 * layer + 2)
            link(dve.scalar_tensor_tensor(gsum, ex, 1.0, gsum, ALU.add, ALU.mult))
            link(dve.reciprocal(wa, gsum))
            link(dve.tensor_tensor(wb, wa, ex, ALU.mult))
            link(dve.tensor_tensor(oh1, oh1, b2(wa, 32), ALU.mult))
            link(dve.tensor_tensor(oh2, oh2, b2(wb, 32), ALU.mult))
            link(dve.tensor_tensor(gates, oh1, oh2, ALU.add))
            dve.wait_ge(s("router_ps"), 2 * layer + 2)
            link(dve.scalar_tensor_tensor(rank, PS[:, 1, 0:64].rearrange("p (t n) -> p t n", t=NT), 1.0, mask, ALU.add, ALU.mult))
            link(dve.tensor_scalar(rank, rank, -1.0, None, ALU.add))
            link(dve.tensor_reduce(pm, PS[:, 1, 64:96].rearrange("p (a e) -> p a e", e=2), AX.X, ALU.max))
            link(dve.tensor_scalar(rounds, pm, CAP + 0.5, 1.0, ALU.is_gt, ALU.add))
            for m in range(2, SEQ // CAP):
                link(dve.scalar_tensor_tensor(rounds, pm, m * CAP + 0.5, rounds, ALU.is_gt, ALU.add))
            if layer:
                link(dve.tensor_copy(base[:, 0:1], ctrl[:, cB - 36 + PAIRS:cB - 36 + PAIRS + 1]))
            else:
                link(dve.memset(base[:, 0:1], 0.0))
            link(dve.tensor_tensor_scan(base[:, 1:17], ones[:, 0:16], rounds, base[:, 0:1], ALU.mult, ALU.add))
            link(dve.tensor_copy(ctrl[:, cR:cR + 16], rounds))
            dve.tensor_copy(ctrl[:, cB:cB + 17], base).then_inc(s("ctrl"), 1)

            def body(j, it, r, g):
                pair = it * (2 * UNROLL) + 2 * j
                dve.wait_ge(s("sgT_ps"), g + (1 + layer))
                slots = cst[:, bass.ds(r * CAP + C_IOTA, CAP)]
                for tt in range(NT):
                    ins = dve.tensor_tensor(sel[:, tt], view(rank[:, tt, bass.ds(pair, 2)], [1, 2], [0, CAP]),
                                            view(slots, [0, 2], [1, CAP]), ALU.is_equal)
                    ins.then_inc(s("eq"), 1)
                dve.wait_ge(s("eq"), g * 2 + 2)
                for tt in range(NT):
                    ins = dve.tensor_tensor(selg[:, tt, :].rearrange("p (e c) -> p e c", e=2), sel[:, tt],
                                            view(gates[:, tt, bass.ds(pair, 2)], [1, 2], [0, CAP]), ALU.mult)
                ins.then_inc(s("sel"), 1)
                dve.wait_ge(s("xe"), g * 2 + 2)
                dve.tensor_copy(view(xeT[:, 4, 0:1], [1, 512]), PS[:, 1, :]).then_inc(s("xe_dve"), 1)
                dve.wait_ge(s("silu"), g + 1)
                dve.wait_ge(s("h3"), g + 1)
                dve.tensor_tensor(hh, PS[:, 3, :], hs, ALU.mult).then_inc(s("h"), 1)
                dve.wait_ge(s("y"), g + 1)
                dve.tensor_copy(Y[:, 512:D], PS[:, 1, :]).then_inc(s("y_dve"), 1)

            for_rounds(dve, body)
            dve_layer_norm(dve, link, lambda tt, h: PS[:, 4 + 2 * tt + h, :],
                           lambda e, tt, h: e.wait_ge(s("done"), layer + 1),
                           lnp[:, 0:D], lnp[:, D:2 * D], lambda e: e.wait_ge(S("ln_in1"), 32 * layer + 32), (xr, st), ln_tag)

        return {"sp": sp_, "pe": pe_, "act": act_, "dve": dve_, "freed": freed}

    m0 = moe(0, "m0", N_M0, lambda e: e.wait_ge(S("da_out"), 1),
             after_mod(0), "ln1", lambda e: e.wait_ge(S("ln_out"), 2), a0_norm_sp)

    top[0] = MARK
    qz1 = area(2 * KT * 256).rearrange("p (c f n) -> p c f n", c=2, f=KT)
    kT1 = area(KT * 256).rearrange("p (f n) -> p f n", f=KT)
    V1 = area(NT * D).rearrange("p (t d) -> p t d", t=NT)
    ZB = (0, 2, 6)
    ONE_SB = 384
    lnv = area(2 * 2 * ONE_SB).rearrange("p (b c n) -> p b c n", b=2, c=2)
    spv = area(2 * 2 * ONE_SB).rearrange("p (b c n) -> p b c n", b=2, c=2)
    wT = area(2 * 2 * ONE_SB).rearrange("p (b c n) -> p b c n", b=2, c=2)
    ones1 = area(P)
    lnp1 = view(qz1[:, 0, 0, 0:1], [1, 2048])
    xr1 = view(qz1[:, 1, 0, 0:1], [1, 1024])

    def a1_sp(sp):
        for c, name in enumerate(("sb_wq", "sb_wk", "sb_wv", "sb_wo")):
            m0["freed"](sp, c)
            load_square(sp, N_A1 + c, t[name][0])
        mod_sp(sp, 1, lambda e: None)

    def a1_norm_sp(sp):
        sp.wait_ge(S("scores"), 16 + KT)
        load_ln(sp, "ln_mix_g", "ln_mix_b", 1, lnp1, "ln_in0")

    def a1_pe(pe):
        pe_turn(pe, X, NT, "t2", lambda e: e.wait_ge(S("ln_out"), 4))
        loaded(pe, N_A1)
        turned(pe, "t2")
        pe_columns(pe, square(N_A1), XT, 4, "q")
        loaded(pe, N_A1 + 1)
        pe_columns(pe, square(N_A1 + 1), XT, 0, "k")
        pe.wait_ge(S("k_act"), 2 + 2)
        pe.wait_ge(S("k_dve"), 2 + 2)
        mod_pe(pe, 1, 0, 2, None)
        loaded(pe, N_A1 + 2)
        pe.wait_ge(S("q_act"), 2 + 2)
        pe.wait_ge(S("q_dve"), 2 + 2)
        pe_rows(pe, square(N_A1 + 2), XT, 4, "v")
        mod_pe(pe, 1, 1, 3, None)
        mod_pe(pe, 1, 2, 2, 0)
        negd, nge = cst[:, C_NEGD:C_NEGD + P], cst[:, C_NGE:C_NGE + P]

        def z(f):
            if f == 1:
                pe.wait_ge(S("modrow"), N_MOD + 3)
            if f == 2:
                pe.wait_ge(S("v_act"), 2 + 2)
                pe.wait_ge(S("v_dve"), 2 + 2)
            if f >= 3:
                pe.wait_ge(S("sb_w"), f - 2)
            for c in range(2):
                b = PS[:, ZB[f % 3] + c, :]
                pe.matmul(b[:, 0:256], kT1[:, f, 0:P], qz1[:, c, f, :], start=True, stop=False, skip_group_check=True)
                pe.matmul(b[:, 256:384], kT1[:, f, P:2 * P], qz1[:, c, f, P:2 * P], start=False, stop=False, skip_group_check=True)
                pe.matmul(b[:, 0:P], ident, negd, start=False, stop=False, skip_group_check=True)
                ins = pe.matmul(b[:, 256:384], ident, negd, start=False, stop=False, skip_group_check=True)
            ins.then_inc(S("scores"), 1)

        def cumulate(f):
            pe.wait_ge(S("sb_soft"), f + 1)
            for c in range(2):
                b, s_ = PS[:, ZB[f % 3] + c, :], spv[:, f % 2, c, :]
                pe.matmul(b[:, 0:384], nge, s_, start=False, stop=False, skip_group_check=True)
                ins = pe.matmul(b[:, P:256], ones1, s_[:, 256:384], start=False, stop=True, skip_group_check=True)
            ins.then_inc(S("sb_cum"), 1)

        def pv(f):
            pe.wait_ge(S("sb_w"), f + 1)
            if f == 0:
                pe.wait_ge(S("v_act"), 2 + 2)
                pe.wait_ge(S("v_dve"), 2 + 2)
            if f:
                pe.wait_ge(S("values_out"), 16 + f)
            for c in range(2):
                o = PS[64 * c:64 * c + 64, 4, 0:256]
                vcol = (2 * f + c) * 64
                pe.matmul(o, V1[:, 0, vcol:vcol + 64], wT[:, f % 2, c, 0:256], start=True, stop=False, skip_group_check=True)
                ins = pe.matmul(o[:, P:256], V1[:, 1, vcol:vcol + 64], wT[:, f % 2, c, 256:384], start=False, stop=True,
                                skip_group_check=True)
            ins.then_inc(S("values"), 1)

        z(0)
        z(1)
        for f in range(KT):
            cumulate(f)
            if f + 2 < KT:
                z(f + 2)
            if f in (2, 4, 6):
                m = 2 + f // 2
                mod_pe(pe, 1, m, 5, m - 1)
            if f:
                pv(f - 1)
        pv(KT - 1)
        loaded(pe, N_A1 + 3)
        pe.wait_ge(S("values_out"), 16 + KT)
        pe_rows(pe, square(N_A1 + 3), XT, 4, "mix")

    def a1_act(act):
        copy_turn_act(act, XT, "t2")
        act.wait_ge(S("zero"), 2 + 1)
        for b in (0, 2):
            act.wait_ge(S("q"), 4 + b + 1)
            for c in range(2):
                ins = act.mul(qz1[64 * c:64 * c + 64, c, 2 * b:2 * b + 2, :],
                              PS[64 * c:64 * c + 64, 4 + b, :].rearrange("p (f n) -> p f n", f=2), 0.125)
            ins.then_inc(S("q_act"), 1)
        for b in (0, 2):
            act.wait_ge(S("k"), 4 + b + 1)
            act.copy(kT1[:, 2 * b:2 * b + 2, :], PS[:, b, :].rearrange("p (f n) -> p f n", f=2)).then_inc(S("k_act"), 1)
        for b in range(2):
            act.wait_ge(S("v"), 4 + 2 * b + 1)
            act.copy(V1[:, b, 0:512], PS[:, 4 + 2 * b, :]).then_inc(S("v_act"), 1)

        def softlog(f):
            l = lnv[:, f % 2]
            act.wait_ge(S("scores"), 16 + f + 1)
            if f >= 2:
                act.wait_ge(S("sb_soft"), f - 1)
            act.activation(l, PS[:, ZB[f % 3]:ZB[f % 3] + 2, 0:384], ACT.Abs).then_inc(S("sb_abs"), 1)
            act.wait_ge(S("sb_abs"), f + 1)
            act.activation(l, l, ACT.Exp, scale=-1.0).then_inc(S("sb_e"), 1)
            act.wait_ge(S("sb_e"), f + 1)
            act.activation(l, l, ACT.Ln, bias=1.0).then_inc(S("sb_ln"), 1)

        softlog(0)
        for f in range(KT):
            if f + 1 < KT:
                softlog(f + 1)
            act.wait_ge(S("sb_cum"), f + 1)
            if f >= 2:
                act.wait_ge(S("values"), 16 + f - 1)
            act.activation(wT[:, f % 2], PS[:, ZB[f % 3]:ZB[f % 3] + 2, 0:384], ACT.Exp).then_inc(S("sb_w"), 1)
        act_layer_norm(act, "ln2")

    def a1_dve(dve, link):
        dve.memset(view(qz1[:, 0, 0, 0:1], [1, 4096]), 0.0).then_inc(S("zero"), 1)
        copy_turn_dve(dve, XT, "t2")
        link(dve.memset(ones1, -1.0))
        dve.wait_ge(S("zero"), 2 + 1)
        for b in (1, 3):
            dve.wait_ge(S("q"), 4 + b + 1)
            for c in range(2):
                ins = dve.tensor_scalar(qz1[64 * c:64 * c + 64, c, 2 * b:2 * b + 2, :],
                                        PS[64 * c:64 * c + 64, 4 + b, :].rearrange("p (f n) -> p f n", f=2), 0.125, None, ALU.mult)
            ins.then_inc(S("q_dve"), 1)
        for b in (1, 3):
            dve.wait_ge(S("k"), 4 + b + 1)
            dve.tensor_copy(kT1[:, 2 * b:2 * b + 2, :], PS[:, b, :].rearrange("p (f n) -> p f n", f=2)).then_inc(S("k_dve"), 1)
        mod_dve(dve, 1, 0, 2)
        for b in range(2):
            dve.wait_ge(S("v"), 4 + 2 * b + 2)
            dve.tensor_copy(V1[:, b, 512:1024], PS[:, 5 + 2 * b, :]).then_inc(S("v_dve"), 1)
        mod_dve(dve, 1, 1, 3)
        mod_dve(dve, 1, 2, 2)

        def outputs(f):
            dve.wait_ge(S("values"), 16 + f + 1)
            dve.tensor_copy(XT[:, f, :], PS[:, 4, 0:256]).then_inc(S("values_out"), 1)

        for f in range(KT):
            dve.wait_ge(S("sb_ln"), f + 1)
            if f >= 2:
                dve.wait_ge(S("sb_cum"), f - 1)
            dve.scalar_tensor_tensor(spv[:, f % 2], PS[:, ZB[f % 3]:ZB[f % 3] + 2, 0:384], 0.0, lnv[:, f % 2],
                                     ALU.max, ALU.add).then_inc(S("sb_soft"), 1)
            if f >= 2:
                outputs(f - 2)
            if f in (3, 5, 7):
                mod_dve(dve, 1, 2 + f // 2, 5)
        outputs(KT - 2)
        outputs(KT - 1)
        dve_layer_norm(dve, link, lambda tt, h: PS[:, 4 + 2 * tt + h, :],
                       lambda e, tt, h: e.wait_ge(S("mix"), 4 + 2 * tt + h + 1),
                       lnp1[:, 0:D], lnp1[:, D:2 * D], lambda e: e.wait_ge(S("ln_in0"), 64), (xr1, small[:, 192:204]), "ln2")

    m1 = moe(1, "m1", N_M1, lambda e: e.wait_ge(S("values"), 16 + KT),
             after_mod(1), "ln3", lambda e: e.wait_ge(S("ln_out"), 6), a1_norm_sp)

    N_HEADS, KV_HEADS, HD = 8, 2, 64
    Q_DIM, KV_DIM, SSD_W, STATE, SSD_H = 512, 128, 512, 128, 8
    XBC = SSD_W + 4 * STATE
    IN_DIM = Q_DIM + 2 * KV_DIM + SSD_W + XBC + SSD_H
    D_FF = 2816
    FT = D_FF // P
    TAPS = 5
    TT = 4
    RING_B = 3
    GU_BANKS = 3
    G2_AT = (10, 14)
    USES_A = uses(N_B) - 1

    X4 = arena[:, 0:4096].rearrange("p (t d) -> p t d", t=TT)
    MULTI, GATES, MISC = 4096, 4096 + 11264, 4096 + 11264 + 2048
    extra = ring[:, 3 * SLOT:4 * SLOT]

    def at(base, off, cols):
        return (extra if base == "extra" else arena)[:, (0 if base == "extra" else MULTI) + off:
                                                     (0 if base == "extra" else MULTI) + off + cols]

    G = arena[:, GATES:GATES + 2048].rearrange("p (v d) -> p v d", v=2)
    VC = arena[:, MISC:MISC + 128]
    modc = arena[:, MISC + 128:MISC + 224].rearrange("p (s v k) -> p s v k", s=6, v=2)
    g2row = arena[:, MISC + 224:MISC + 480]
    affine = arena[:, MISC + 480:MISC + 512].rearrange("p (a v k) -> p a v k", a=2, v=2)
    VR = arena[:, MISC + 768:MISC + 896]
    rs4 = arena[:, MISC + 896:MISC + 912]
    qk_ss = arena[:, MISC + 912:MISC + 952]
    DEEP = 3
    u_max, u_sum, u_r = (arena[:, MISC + 952 + DEEP * a:MISC + 952 + DEEP * (a + 1)] for a in range(3))
    V_BMOD, V_NMP, V_NFP, V_CW, V_CB, N_VEC = 0, 48, 56, 64, 104, 112

    HT = at("extra", 0, 4096).rearrange("p (k n) -> p k n", k=KT)
    xhat = at("extra", 4096, 4096).rearrange("p (t d) -> p t d", t=TT)
    modrow = at("m", 0, 1536).rearrange("p (s n) -> p s n", s=6)
    brow2 = at("m", 2048, 1024)
    prow2 = at("m", 3072, 1024)
    QK = at("m", 0, 2560).rearrange("p (t n) -> p t n", t=TT)
    Vr = at("m", 2560, 512).rearrange("p (t n) -> p t n", t=TT)
    Z = at("m", 3072, 2048).rearrange("p (t n) -> p t n", t=TT)
    cv = at("m", 5120, 4096).rearrange("p (i n) -> p i n", i=8)
    Y = at("m", 5120, 2048).rearrange("p (t n) -> p t n", t=TT)
    catT = at("m", 7168, 4096).rearrange("p (i n) -> p i n", i=8)
    dt = at("m", 9216, 64).rearrange("p (d t h) -> p d t h", d=2, t=TT)
    dA = at("m", 9280, 64).rearrange("p (d t h) -> p d t h", d=2, t=TT)
    EX = at("m", 9344, 128)
    xdt, xde = (at("m", 9472, 512), at("m", 7168, 512)), (at("m", 9984, 512), at("m", 7680, 512))
    ytmp = at("m", 10496, 512)
    CBm = at("m", 11008, 256).rearrange("p (g n) -> p g n", g=2)
    xs = at("extra", 0, 2048).rearrange("p (t n) -> p t n", t=TT)
    Br = at("extra", 2048, 1024).rearrange("p (t n) -> p t n", t=TT)
    Rb = at("extra", 3072, 2048).rearrange("p (b h n) -> p b h n", b=2, h=SSD_H)
    Es = at("extra", 5120, 2048).rearrange("p (b h n) -> p b h n", b=2, h=SSD_H)
    ST = at("extra", 7168, 1024).rearrange("p (d n) -> p d n", d=2)
    qT = at("extra", 0, 2048).rearrange("p (f n) -> p f n", f=4)
    kz = at("extra", 2048, 2048).rearrange("p (g c n) -> p g c n", g=KV_HEADS, c=2)
    Eb = at("extra", 4096, DEEP * 512).rearrange("p (b n) -> p b n", b=DEEP)
    PT = at("extra", 7168, 1024).rearrange("p (b n) -> p b n", b=2)
    L_BANK = (0, 1, 6)
    hT = at("m", 0, FT * 512)
    xh = at("extra", 4096, 4096).rearrange("p (k n) -> p k n", k=KT)
    DOWN_LAST = 4
    N_WH = 3
    rows = small[:, 204:640]
    r_bias, r_A, r_skip = rows[:, 0:16], rows[:, 16:32], rows[:, 32:40]
    r_qk = rows[:, 40:168]
    ones_b = at("m", 9600, 128)

    LAYER0 = dict(
        vec_in=80, vec_ps=2, mod_in=16, rows_in=112, g1_in=32, g2_in=32, ssdn_in=16, A=1, affine=1, y0=3, y_sq=4,
        norm_sq=8, norm_sd=8, norm_hat=8, norm_turned=16, norm_act=8, norm_dve=8,
        gate_ps=4, gate=4, dtx=2, dtabs=2, dtln=1, cv=9, xs=4, Br=4, xsB_ps=4, CB=2, dA=1,
        dec=2, R=8, seg=8, expd=8, xdt=8, st_ps=6, state=6, score=8, y_ps=8, y=8, stat=TT, stat_sd=TT + 1,
        qkT_ps=6, qT=4, kT=4, lg=32, nmax=32, p=32, pn=32, pT_ps=32, PT=32, o_ps=32, oT=16,
        ygated=4, yT_ps=4, yT=4, out=8, res_sq=8, res_sd=8, x1=4, wh=3 * FT + KT, wl=3 * FT + KT, down_r=FT - DOWN_LAST, gu=FT, sg=FT, hT=FT, down=8,
        x2=4, **{"in": 21, "in_act": 9, "in_dve": 12})

    def hybrid(l):
        s = lambda name: S(f"b_{name}")
        past = lambda name: l * LAYER0[name]
        both = l == 0
        tiles = range(TT) if both else range(2)
        PRE = (2, 3, 0, 1) if both else range(TT)
        nv = 2 if both else 1
        ntok = 512 if both else 256
        SSDN = at("extra", 6144, 512)
        PER_LAYER = 13
        p0, p1, p2 = ((0, 1, 2), (2, 1, 0))[l]
        PLACE = (p0, p1, p2, p0) + (p1, p2) * 3 + (p1, p2, p1)
        before_l = ((0, 1, 2, 0) + (1, 2) * 3 + (1, 2, 1)) if l else ()

        def first(tag, what):
            if tag in ("pre", "r1"):
                return 0
            return {"turned": 8, "act": 4, "dve": 4}.get(what, 4) if tag == "ffn" else len(tiles)

        def slot_b(n, space=ring):
            return space[:, PLACE[n] * SLOT:(PLACE[n] + 1) * SLOT]

        def kview(n, cols):
            return slot_b(n)[:, 0:KT * cols].rearrange("p (k c) -> p k c", k=KT)

        def ready(eng, n):
            use = (before_l + PLACE[0:n + 1]).count(PLACE[n])
            eng.wait_ge(S(f"ring{PLACE[n]}"), PER_SLOT * (USES_A + use))

        products = [("xbc", i, "dve") for i in range(8)] + [("dt", 0, "act")]
        n_dt = len(products)
        products += [("z2", tt, "act") for tt in tiles]
        n_z2 = len(products)
        for tt in range(TT):
            if tt in tiles:
                products.append(("q", tt, "act"))
            products.append(("kvz", tt, "dve"))
        seen = {"act": 0, "dve": 0}
        count = []
        for _, _, e in products:
            seen[e] += 1
            count.append(seen[e])

        GU = [(512 * c, min(512, D_FF - 512 * c)) for c in range(6)]
        DOWN = [(8 * c, min(8, FT - 8 * c)) for c in range(3)]
        gu_done = [("gu", (c0 + w) // P) for c0, w in GU]
        frees = [("in", n_z2), ("in", n_dt), ("in", len(products))] + gu_done[0:-1] + [gu_done[-1], ("down_r", 8)]

        wh = [ring[:, p0 * SLOT + 2 * D * b:p0 * SLOT + 2 * D * (b + 1)].rearrange("p (k a c) -> p k a c", k=KT, a=2)
              for b in range(N_WH)]
        brow_g2 = ring[:, p0 * SLOT + 6 * D:p0 * SLOT + 7 * D]
        prow_g2 = ring[:, p0 * SLOT + 7 * D:p0 * SLOT + 8 * D]

        def gu_weights(i):
            c, j = i // 4, i % 4
            wd = GU[c][1]
            return slot_b(4 + c)[:, 0:KT * 2 * wd].rearrange("p (k a c) -> p k a c", k=KT, a=2)[:, :, :, j * P:(j + 1) * P]

        def h_high(r):
            o = r * ntok
            return (extra[:, o:o + ntok] if o + ntok <= SLOT else
                    ring[:, p0 * SLOT + 4 * D + o - SLOT:p0 * SLOT + 4 * D + o - SLOT + ntok])
        N_DH = 4
        down_high = [ring[:, p0 * SLOT + D * b:p0 * SLOT + D * (b + 1)] for b in range(N_DH)]

        spare = [ring[:, p1 * SLOT + D * b:p1 * SLOT + D * (b + 1)] for b in (6, 7)]

        def down_weights(r):
            c = r // 8
            return slot_b(10 + c)[:, (r % 8) * D:(r % 8 + 1) * D]

        def down_split_high(act, r):
            ready(act, 10 + r // 8)
            if r >= N_DH:
                act.wait_ge(s("down_r"), past("down_r") + r - N_DH + 1)
            act.copy(as_r(down_high[r % N_DH]), down_weights(r)).then_inc(s("wh"), 1)
            act.copy(as_r(h_high(r)), hTv[:, r, :]).then_inc(s("wh"), 1)

        def down_split_low(dve, r):
            dve.wait_ge(s("wh"), past("wh") + FT + KT + 2 * r + 1)
            dve.tensor_tensor(as_r(down_weights(r)), down_weights(r), as_r(down_high[r % N_DH]), ALU.subtract).then_inc(s("wl"), 1)
            dve.wait_ge(s("wh"), past("wh") + FT + KT + 2 * r + 2)
            dve.tensor_tensor(as_r(hTv[:, r, :]), hTv[:, r, :], as_r(h_high(r)), ALU.subtract).then_inc(s("wl"), 1)

        w_split = lambda i: i + 1 if i < 2 else i + 1 + KT
        x_split = lambda k: 2 + k + 1

        def weights_high(act, i):
            ready(act, 4 + i // 4)
            if i >= N_WH:
                act.wait_ge(s("gu"), past("gu") + i - N_WH + 1)
            act.copy(as_r(wh[i % N_WH]), gu_weights(i)).then_inc(s("wh"), 1)

        def weights_low(dve, i):
            dve.wait_ge(s("wh"), past("wh") + w_split(i))
            dve.tensor_tensor(as_r(gu_weights(i)), gu_weights(i), as_r(wh[i % N_WH]), ALU.subtract).then_inc(s("wl"), 1)

        IN_SLOTS = (1, 2, 0)

        def load(sp, n):
            sem = S(f"ring{PLACE[n]}")
            if n < 3:
                c0 = IN_SLOTS[n] * D
                cols = min(D, IN_DIM - c0)
                src = t["w_in_2"][l, :, c0:c0 + cols]
            elif n == 3:
                src, cols = t["w_out_2"][l], D
            elif n < 10:
                c0, w = GU[n - 4]
                dst = slot_b(n)[:, 0:KT * 2 * w].rearrange("p (k a c) -> p k a c", k=KT, a=2)
                for a, name in enumerate(("w_gate_2", "w_up_2")):
                    sp.dma_start(dst[:, :, a, :], t[name][l, :, c0:c0 + w].rearrange("(k p) c -> p k c", p=P)).then_inc(sem, 16)
                return
            else:
                r0, nr = DOWN[n - 10]
                dst = slot_b(n)[:, 0:nr * D].rearrange("p (k c) -> p k c", k=nr)
                src = t["w_down_2"][l, r0 * P:(r0 + nr) * P, :].rearrange("(k p) c -> p k c", p=P)
                for a in range(2):
                    sp.dma_start(dst[:, a * nr // 2:(a + 1) * nr // 2], src[:, a * nr // 2:(a + 1) * nr // 2]).then_inc(sem, 16)
                return
            src = src.rearrange("(k p) c -> p k c", p=P)
            for a in range(2):
                sp.dma_start(kview(n, cols)[:, 4 * a:4 * a + 4], src[:, 4 * a:4 * a + 4]).then_inc(sem, 16)

        def row_dma(sp, dst, name, off, n, sem):
            sp.dma_start(dst, bass.AP(t[name].tensor, off, [[0, P], [1, n]])).then_inc(s(sem), 16)

        def sp_(sp):
            def vectors():
                for name, r0, nr, off in (("b_mod_2", V_BMOD, 48, l * 6 * D), ("norm_mix_pre_2", V_NMP, 8, l * D),
                                          ("norm_ffn_pre_2", V_NFP, 8, l * D),
                                          ("conv_w_2", V_CW, 40, l * TAPS * XBC), ("conv_b_2", V_CB, 8, l * XBC)):
                    sp.dma_start(VR[r0:r0 + nr, :], bass.AP(t[name].tensor, off, [[P, nr], [1, P]])).then_inc(s("vec_in"), 16)
                for d, name in enumerate(("dt_bias_fwd_2", "dt_bias_bwd_2")):
                    row_dma(sp, r_bias[:, 8 * d:8 * d + 8], name, l * SSD_H, SSD_H, "rows_in")
                for d, name in enumerate(("a_log_fwd_2", "a_log_bwd_2")):
                    row_dma(sp, r_A[:, 8 * d:8 * d + 8], name, l * SSD_H, SSD_H, "rows_in")
                row_dma(sp, r_skip, "d_skip_2", l * SSD_H, SSD_H, "rows_in")
                row_dma(sp, r_qk[:, 0:64], "q_norm_2", l * HD, HD, "rows_in")
                row_dma(sp, r_qk[:, 64:128], "k_norm_2", l * HD, HD, "rows_in")
                sp.wait_ge(S("mod_out"), 16 * N_MOD * DEPTH)
                sp.dma_start(modrow, mod_rows.ap()[l]).then_inc(s("mod_in"), 16)
                row_dma(sp, brow2, "b_mod_2", l * 6 * D + 2 * D, D, "g1_in")
                row_dma(sp, prow2, "norm_mix_post_2", l * D, D, "g1_in")

            if l == 0:
                sp.wait_ge(S("moe_router_ps"), 3)
                sp.wait_ge(S("ln_out"), 6)
                sp.dma_start(X4[:, 2:4, :], t["ctx_2"].rearrange("b (t p) d -> p (b t) d", p=P)).then_inc(S("ctx_in"), 16)
                vectors()
                for n in range(3):
                    m1["freed"](sp, n)
                    load(sp, n)
            for n in range(3 if l == 0 else 0, PER_LAYER):
                if n >= RING_B:
                    name, v = frees[n - RING_B]
                    sp.wait_ge(s(name), past(name) + v)
                else:
                    name, v = (("down_r", 16), ("down", 8), ("down", 8))[n]
                    sp.wait_ge(S(f"b_{name}"), v)
                load(sp, n)
                if l == 1 and n == RING_B - 1:
                    sp.wait_ge(S("b_x2"), TT)
                    vectors()
                if n == 3:
                    sp.wait_ge(s("y"), past("y") + y_before[-1])
                    row_dma(sp, SSDN, "ssd_norm_2", l * SSD_W, SSD_W, "ssdn_in")
                if n == 6:
                    sp.wait_ge(s("out"), past("out") + 2 * len(tiles))
                    row_dma(sp, brow_g2, "b_mod_2", l * 6 * D + 5 * D, D, "g2_in")
                    row_dma(sp, prow_g2, "norm_ffn_post_2", l * D, D, "g2_in")
            if l == 1:
                for tt in range(2):
                    sp.wait_ge(s("x2"), past("x2") + tt + 1)
                    sp.dma_start(out[0, tt * P:(tt + 1) * P, :], X4[:, tt, :]).then_inc(S("out_dma"), 16)
                sp.wait_ge(S("out_dma"), 32)

        def norm_pe(pe, tag, order):
            for n, tt in enumerate(order):
                pe.wait_ge(s("norm_hat"), past("norm_hat") + first(tag, "hat") + n + 1)
                for k in range(KT):
                    ins = pe.transpose(PS[:, k, tt * P:(tt + 1) * P], xhat[:, tt, k * P:(k + 1) * P], ident)
                    if n == len(order) - 1:
                        ins.then_inc(s("norm_turned"), 1)

        def norm_tile_act(act, tag, n, tt):
            tag_ready(act, tag, tt)
            act.activation(HT[:, 2 * tt:2 * tt + 2, :], X4[:, tt, :].rearrange("p (a n) -> p a n", a=2), ACT.Square,
                           accum_out=rs4[:, tt:tt + 1]).then_inc(s("norm_sq"), 1)
            act.wait_ge(s("norm_sq"), past("norm_sq") + first(tag, "sq") + n + 1)
            act.activation(rs4[:, tt:tt + 1], rs4[:, tt:tt + 1], ACT.Sqrt, scale=1.0 / D, bias=eps).then_inc(s("norm_sd"), 1)

        def norm_act(act, tag, ntiles, a, sh):
            act.wait_ge(s("affine"), past("affine") + 1)
            for k in range(0, KT, 2):
                act.wait_ge(s("norm_turned"), past("norm_turned") + first(tag, "turned") + k + 1)
                for v in range(ntiles // 2):
                    ins = act.activation(HT[:, k, v * 256:(v + 1) * 256], PS[:, k, v * 256:(v + 1) * 256], ACT.Identity,
                                         bias=modc[:, sh, v, k:k + 1], scale=affine[:, a, v, k:k + 1])
                ins.then_inc(s("norm_act"), 1)

        def tag_ready(eng, tag, tt):
            if tag == "pre" and l == 0:
                if tt >= 2:
                    eng.wait_ge(S("ctx_in"), 16)
                else:
                    eng.wait_ge(S("ln_out"), 6 + tt + 1)
            elif tag == "pre":
                eng.wait_ge(S("b_x2"), tt + 1)
            else:
                eng.wait_ge(s("x1"), past("x1") + tt + 1)

        def norm_tile_dve(dve, link, tag, n, tt):
            dve.wait_ge(s("norm_sd"), past("norm_sd") + first(tag, "sd") + n + 1)
            link(dve.reciprocal(rs4[:, tt:tt + 1], rs4[:, tt:tt + 1]))
            dve.tensor_scalar(xhat[:, tt, :], X4[:, tt, :], rs4[:, tt:tt + 1], None, ALU.mult).then_inc(s("norm_hat"), 1)

        def norm_out_dve(dve, tag, ntiles, a, sh):
            for k in range(1, KT, 2):
                dve.wait_ge(s("norm_turned"), past("norm_turned") + first(tag, "turned") + k + 1)
                for v in range(ntiles // 2):
                    ins = dve.tensor_scalar(HT[:, k, v * 256:(v + 1) * 256], PS[:, k, v * 256:(v + 1) * 256],
                                            affine[:, a, v, k:k + 1], modc[:, sh, v, k:k + 1], ALU.mult, ALU.add)
                ins.then_inc(s("norm_dve"), 1)

        def normed(eng, tag):
            eng.wait_ge(s("norm_act"), past("norm_act") + first(tag, "act") + 4)
            eng.wait_ge(s("norm_dve"), past("norm_dve") + first(tag, "dve") + 4)

        def gate_pe(pe, row, v, bank):
            for j in range(4):
                ins = pe.matmul(PS[:, bank + j // 2, (j % 2) * 256:(j % 2) * 256 + 256],
                                view(ident[:, 32 * j + v:32 * j + v + 1], [0, P]), row, start=True, stop=True)
            ins.then_inc(s("gate_ps"), 1)

        def gate_dve(dve, link, tag, v, bank):
            done = v + (0 if tag == "g1" else nv)
            dve.wait_ge(s("gate_ps"), past("gate_ps") + done + 1)
            dve.wait_ge(s(f"{tag}_in"), past(f"{tag}_in") + 32)
            brow, prow = (brow2, prow2) if tag == "g1" else (brow_g2, prow_g2)
            link(dve.tensor_tensor(G[:, v, :], view(PS[:, bank, 0:1], [1, D]), brow, ALU.add))
            dve.tensor_tensor(G[:, v, :], G[:, v, :], prow, ALU.mult).then_inc(s("gate"), 1)
            dve.wait_ge(s("gate"), past("gate") + done + 1)

        def residual_act(act, ps_sem, tag):
            for n, tt in enumerate(tiles):
                act.wait_ge(s(ps_sem), past(ps_sem) + 2 * n + 2)
                junk = xhat[:, tt, :] if tag == "r1" else spare[1]
                act.activation(junk.rearrange("p (a n) -> p a n", a=2), PS[:, 2 * tt:2 * tt + 2, :], ACT.Square,
                               accum_out=rs4[:, 4 + tt:5 + tt]).then_inc(s("res_sq"), 1)
                act.wait_ge(s("res_sq"), past("res_sq") + first(tag, "sq") + n + 1)
                act.activation(rs4[:, 8 + tt:9 + tt], rs4[:, 4 + tt:5 + tt], ACT.Sqrt, scale=1.0 / D, bias=eps).then_inc(s("res_sd"), 1)
                if tag == "r1":
                    norm_tile_act(act, "ffn", n, tt)

        def residual_dve(dve, link, tag, done):
            for n, tt in enumerate(tiles):
                dve.wait_ge(s("res_sd"), past("res_sd") + first(tag, "sd") + n + 1)
                link(dve.reciprocal(rs4[:, 8 + tt:9 + tt], rs4[:, 8 + tt:9 + tt]))
                tmp = xhat[:, tt, :] if tag == "r1" else spare[0]
                link(dve.scalar_tensor_tensor(tmp, view(PS[:, 2 * tt, 0:1], [1, D]), rs4[:, 8 + tt:9 + tt], G[:, tt // 2, :],
                                              ALU.mult, ALU.mult))
                dve.tensor_tensor(X4[:, tt, :], X4[:, tt, :], tmp, ALU.add).then_inc(s(done), 1)
                dve.wait_ge(s(done), past(done) + n + 1)
                if tag == "r1":
                    norm_tile_dve(dve, link, "ffn", n, tt)

        ORDER = ((2, 3, 0, 1), (3, 2, 1, 0))
        STEPS = [(d, c, ORDER[d][c]) for c in range(TT) for d in range(2)]
        y_before = [sum(tt in tiles for _, _, tt in STEPS[:i]) for i in range(len(STEPS) + 1)]
        st_before = [sum(c < TT - 1 for _, c, _ in STEPS[:i]) for i in range(len(STEPS) + 1)]
        MASK = (C_LE, C_GE)
        AFTER = (C_GT, C_LT)

        UN = [(f, tt, c) for f in range(4) for tt in tiles for c in range(2)]

        GATE_U = len(UN) // 2

        def keys(tt):
            return (0, 512) if tt < 2 else (256, 256)

        def pe_(pe):
            pe.wait_ge(s("vec_in"), past("vec_in") + 16 * 5)
            if l == 1:
                pe.wait_ge(S("b_x2"), TT)
            pe.transpose(PS[:, 3, 0:N_VEC], VR[0:N_VEC, :], ident[0:N_VEC, 0:N_VEC]).then_inc(s("vec_ps"), 1)
            pe.wait_ge(s("mod_in"), past("mod_in") + 16)
            for n in range(6):
                for h in range(2):
                    ins = pe.transpose(PS[:, n // 2, (n % 2) * 256 + h * P:(n % 2) * 256 + h * P + P], modrow[:, n, h * P:(h + 1) * P], ident)
            ins.then_inc(s("vec_ps"), 1)
            pe.wait_ge(s("affine"), past("affine") + 1)
            for v in range(nv):
                gate_pe(pe, modrow[:, 2, :], v, 2 * v)
            pe.wait_ge(s("gate"), past("gate") + nv)
            norm_pe(pe, "pre", PRE)
            normed(pe, "pre")
            wB, wC, wA = kview(0, D), kview(1, IN_DIM - 2 * D), kview(2, D)
            for n, (kind, i, _) in enumerate(products):
                if n in (0, 6, n_z2):
                    ready(pe, (0, 6, n_z2).index(n))
                if n >= 8:
                    e = products[n - 8][2]
                    pe.wait_ge(s(f"in_{e}"), past(f"in_{e}") + count[n - 8])
                bank = PS[:, n % 8, :]
                if kind == "dt":
                    for tt in range(TT):
                        for k in range(KT):
                            ins = pe.matmul(bank[:, 8 * tt:8 * tt + 8], HT[:, k, tt * P:(tt + 1) * P], wC[:, k, 256:264],
                                            start=(k == 0), stop=(k == KT - 1))
                    ins.then_inc(s("in"), 1)
                    continue
                for k in range(KT):
                    if kind == "xbc":
                        w = wB[:, k, 256 + i * P:256 + (i + 1) * P] if i < 6 else wC[:, k, (i - 6) * P:(i - 5) * P]
                        o, a, b = bank, w, HT[:, k, :]
                    else:
                        a = HT[:, k, i * P:(i + 1) * P]
                        if kind == "q":
                            o, b = bank, wA[:, k, 0:512]
                        elif kind == "kvz":
                            n_c_ = 512 if i in tiles else 256
                            o, b = bank[:, 0:n_c_], wA[:, k, 512:512 + n_c_]
                        else:
                            o, b = bank[:, 0:256], wB[:, k, 0:256]
                    ins = pe.matmul(o, a, b, start=(k == 0), stop=(k == KT - 1))
                ins.then_inc(s("in"), 1)
            pe.wait_ge(s("in_act"), past("in_act") + seen["act"])
            pe.wait_ge(s("in_dve"), past("in_dve") + seen["dve"])
            pe.wait_ge(s("cv"), past("cv") + 8)
            for tt in range(TT):
                if tt >= 2:
                    pe.wait_ge(s("xs"), past("xs") + tt - 1)
                    pe.wait_ge(s("Br"), past("Br") + tt - 1)
                for i in range(6):
                    b = 2 * (tt % 2) + i // 4
                    ins = pe.transpose(PS[:, b, (i % 4) * P:(i % 4) * P + P], cv[:, i, tt * P:(tt + 1) * P], ident)
                ins.then_inc(s("xsB_ps"), 1)
            for tt in range(TT):
                for g in range(2):
                    ins = pe.matmul(PS[:, 6 + tt // 2, (tt % 2) * 256 + g * P:(tt % 2) * 256 + g * P + P], cv[:, 4 + g, tt * P:(tt + 1) * P],
                                    cv[:, 6 + g, tt * P:(tt + 1) * P], start=True, stop=True)
            ins.then_inc(s("CB"), 1)
            pe.wait_ge(s("dA"), past("dA") + 1)
            for d in range(2):
                for a, w in enumerate((cst[:, MASK[d]:MASK[d] + P], cst[:, AFTER[d]:AFTER[d] + P])):
                    pe.matmul(PS[:, 5, 64 * d + 32 * a:64 * d + 32 * a + 32], w, dA[:, d].rearrange("p t h -> p (t h)"), start=True, stop=True)
            ins = pe.matmul(PS[:, 5, 128:192], ones_b, dA.rearrange("p d t h -> p (d t h)"), start=True, stop=True)
            ins.then_inc(s("CB"), 1)
            pe.wait_ge(s("dec"), past("dec") + 2)
            pe.wait_ge(s("xs"), past("xs") + TT)
            pe.wait_ge(s("Br"), past("Br") + TT)
            def decays(i):
                d, c, tt = STEPS[i]
                if tt in tiles:
                    yi = y_before[i]
                    pe.wait_ge(s("R"), past("R") + yi + 1)
                    pe.wait_ge(s("expd"), past("expd") + yi)
                    for a in range(2):
                        ins = pe.matmul(PS[:, a, :], cst[:, AFTER[d]:AFTER[d] + P], view(Rb[:, yi % 2, 4 * a, 0:1], [1, 512]), start=True, stop=True)
                    ins.then_inc(s("seg"), 1)

            decays(0)
            for i, (d, c, tt) in enumerate(STEPS):
                if i + 1 < len(STEPS):
                    decays(i + 1)
                if c < TT - 1:
                    pe.wait_ge(s("xdt"), past("xdt") + i + 1)
                    if c:
                        pe.wait_ge(s("state"), past("state") + st_before[i - 1])
                    for g in range(2):
                        ins = pe.matmul(PS[:, 2 + d, 256 * g:256 * g + 256], Br[:, tt, P * g:P * g + P], xde[i % 2][:, 256 * g:256 * g + 256],
                                        start=True, stop=True)
                    ins.then_inc(s("st_ps"), 1)
                if tt in tiles:
                    yi = y_before[i]
                    pe.wait_ge(s("score"), past("score") + yi + 1)
                    pe.wait_ge(s("xdt"), past("xdt") + i + 1)
                    pe.wait_ge(s("y"), past("y") + yi)
                    for h in range(SSD_H):
                        ins = pe.matmul(PS[:, 4, 64 * h:64 * h + 64], Es[:, yi % 2, h, :], xdt[i % 2][:, 64 * h:64 * h + 64], start=True, stop=True)
                    if c:
                        pe.wait_ge(s("state"), past("state") + st_before[i - 1])
                        for g in range(2):
                            ins = pe.matmul(PS[:, 5, 256 * g:256 * g + 256], cv[:, 6 + g, tt * P:(tt + 1) * P], ST[:, d, 256 * g:256 * g + 256],
                                            start=True, stop=True)
                    ins.then_inc(s("y_ps"), 1)
            pe.wait_ge(s("y"), past("y") + y_before[-1])
            pe.wait_ge(s("state"), past("state") + st_before[-1])
            for f in range(4):
                for tt in tiles:
                    ins = pe.transpose(PS[:, f, tt * P:(tt + 1) * P], QK[:, tt, f * P:(f + 1) * P], ident)
                ins.then_inc(s("qkT_ps"), 1)
            for g in range(2):
                for tt in range(TT):
                    for c in range(2):
                        ins = pe.matmul(PS[64 * c:64 * c + 64, 4 + g, tt * P:(tt + 1) * P],
                                        QK[:, tt, Q_DIM + HD * g:Q_DIM + HD * (g + 1)], ident, start=True, stop=True)
                ins.then_inc(s("qkT_ps"), 1)
            pe.wait_ge(s("qT"), past("qT") + 4)
            pe.wait_ge(s("kT"), past("kT") + 4)

            def logits(u):
                f, tt, c = UN[u]
                k0, nk = keys(tt)
                if u >= DEEP:
                    pe.wait_ge(s("p"), past("p") + u - DEEP + 1)
                pe.matmul(PS[:, L_BANK[u % DEEP], 0:nk], qT[:, f, tt * P:(tt + 1) * P], kz[:, f // 2, c, k0:k0 + nk], start=True, stop=True)\
                  .then_inc(s("lg"), 1)

            def turn_weights(u):
                nk = keys(UN[u][1])[1]
                pe.wait_ge(s("pn"), past("pn") + u + 1)
                if u >= 2:
                    pe.wait_ge(s("PT"), past("PT") + u - 1)
                for kb in range(nk // P):
                    ins = pe.transpose(PS[:, 2 + u % 2, kb * P:(kb + 1) * P], Eb[:, u % DEEP, kb * P:(kb + 1) * P], ident)
                ins.then_inc(s("pT_ps"), 1)

            def values(u):
                f, tt, c = UN[u]
                k0, nk = keys(tt)
                pe.wait_ge(s("PT"), past("PT") + u + 1)
                pair = u // 2
                if pair >= 2:
                    pe.wait_ge(s("oT"), past("oT") + pair - 1)
                for kb in range(nk // P):
                    ins = pe.matmul(PS[64 * c:64 * c + 64, 4 + pair % 2, 0:P], Vr[:, k0 // P + kb, HD * (f // 2):HD * (f // 2) + HD],
                                    PT[:, u % 2, kb * P:(kb + 1) * P], start=(kb == 0), stop=(kb == nk // P - 1))
                ins.then_inc(s("o_ps"), 1)

            for u in range(DEEP):
                logits(u)
            for u in range(len(UN)):
                if u + DEEP < len(UN):
                    logits(u + DEEP)
                turn_weights(u)
                if u:
                    values(u - 1)
            values(len(UN) - 1)
            pe.wait_ge(s("ygated"), past("ygated") + len(tiles))
            pe.wait_ge(s("p"), past("p") + len(UN))
            for n, tt in enumerate(tiles):
                for i in range(4):
                    ins = pe.transpose(PS[:, 6 + n % 2, i * P:(i + 1) * P], Y[:, tt, i * P:(i + 1) * P], ident)
                ins.then_inc(s("yT_ps"), 1)
                if n:
                    pe.wait_ge(s("yT"), past("yT") + n)
            ready(pe, 3)
            pe.wait_ge(s("yT"), past("yT") + len(tiles))
            pe.wait_ge(s("oT"), past("oT") + len(UN) // 2)
            w = kview(3, D)
            for tt in tiles:
                for h in range(2):
                    for k in range(KT):
                        ins = pe.matmul(PS[:, 2 * tt + h, :], catT[:, k, tt * P:(tt + 1) * P], w[:, k, 512 * h:512 * h + 512],
                                        start=(k == 0), stop=(k == KT - 1))
                    ins.then_inc(s("out"), 1)
            pe.wait_ge(s("x1"), past("x1") + len(tiles))
            norm_pe(pe, "ffn", tiles)
            i = 0
            for c, (c0, wd) in enumerate(GU):
                for j in range(wd // P):
                    if i >= GU_BANKS:
                        pe.wait_ge(s("hT"), past("hT") + i - GU_BANKS + 1)
                    pe.wait_ge(s("wl"), past("wl") + w_split(i))
                    high, low = as_r(wh[i % N_WH]), as_r(gu_weights(i))
                    for a in range(2):
                        for k in range(KT):
                            if i == 0 and a == 0:
                                pe.wait_ge(s("wl"), past("wl") + x_split(k))
                            for n, (w, x) in enumerate(((high, xh), (high, HT), (low, xh))):
                                ins = pe.matmul(PS[:, 2 * (i % GU_BANKS) + a, 0:ntok], w[:, k, a, :], as_r(x[:, k, 0:ntok]),
                                                start=(k == 0 and n == 0), stop=(k == KT - 1 and n == 2))
                    ins.then_inc(s("gu"), 1)
                    if i in G2_AT[0:nv]:
                        v = G2_AT.index(i)
                        pe.wait_ge(s("gate"), past("gate") + nv + v)
                        gate_pe(pe, g2row, v, 6)
                    i += 1
            pe.wait_ge(s("gate"), past("gate") + 2 * nv)
            pe.wait_ge(s("hT"), past("hT") + FT)
            def down_products(r, tt, h):
                cols = slice(512 * h, 512 * h + 512)
                toks = slice(tt * P, (tt + 1) * P)
                xh_, xl_, wh_, wl_ = (as_r(a) for a in (h_high(r), hTv[:, r, :], down_high[r % N_DH], down_weights(r)))
                for n, (x, w) in enumerate(((xh_, wh_), (xh_, wl_), (xl_, wh_))):
                    ins = pe.matmul(PS[:, 2 * tt + h, :], x[:, toks], w[:, cols], start=(r == 0 and n == 0), stop=(r == FT - 1 and n == 2))
                return ins

            for r in range(FT - DOWN_LAST):
                pe.wait_ge(s("wl"), past("wl") + FT + KT + 2 * r + 2)
                for tt in tiles:
                    for h in range(2):
                        ins = down_products(r, tt, h)
                ins.then_inc(s("down_r"), 1)
            pe.wait_ge(s("wl"), past("wl") + 3 * FT + KT)
            for tt in tiles:
                for h in range(2):
                    for r in range(FT - DOWN_LAST, FT):
                        ins = down_products(r, tt, h)
                    ins.then_inc(s("down"), 1)

        hTv = hT[:, 0:FT * ntok].rearrange("p (f n) -> p f n", f=FT)

        def act_(act):
            act.wait_ge(s("rows_in"), past("rows_in") + 16 * 7)
            act.activation(r_A, r_A, ACT.Exp).then_inc(s("A"), 1)
            for n, tt in enumerate(PRE):
                norm_tile_act(act, "pre", n, tt)
            norm_act(act, "pre", TT, 0, 0)
            for i in range(8):
                act.wait_ge(s("in_dve"), past("in_dve") + i + 1)
                act.activation(cv[:, i, :], cv[:, i, :], ACT.Silu).then_inc(s("cv"), 1)
            for n, (kind, i, e) in enumerate(products):
                if e == "act":
                    act.wait_ge(s("in"), past("in") + n + 1)
                bank = PS[:, n % 8, :]
                if kind == "q":
                    act.copy(QK[:, i, 0:512], bank).then_inc(s("in_act"), 1)
                elif kind == "z2":
                    act.copy(Z[:, i, 256:512], bank[:, 0:256]).then_inc(s("in_act"), 1)
                elif kind == "dt":
                    act.copy(dt[:, 0], bank[:, 0:32].rearrange("p (t h) -> p t h", t=TT)).then_inc(s("in_act"), 1)
                    act.wait_ge(s("dtx"), past("dtx") + 2)
                    act.activation(dA, dt, ACT.Abs).then_inc(s("dtabs"), 1)
                    act.wait_ge(s("dtabs"), past("dtabs") + 1)
                    act.activation(dA, dA, ACT.Exp, scale=-1.0).then_inc(s("dtabs"), 1)
                    act.wait_ge(s("dtabs"), past("dtabs") + 2)
                    act.activation(dA, dA, ACT.Ln, bias=1.0).then_inc(s("dtln"), 1)
                elif kind == "kvz":
                    h0 = 0 if i in tiles else 8
                    act.wait_ge(s("stat"), past("stat") + i + 1)
                    act.activation(qk_ss[:, 10 * i + h0:10 * i + 10], qk_ss[:, 10 * i + h0:10 * i + 10], ACT.Sqrt,
                                   scale=1.0 / HD, bias=eps).then_inc(s("stat_sd"), 1)
            act.wait_ge(s("in_dve"), past("in_dve") + seen["dve"])
            nz = len(tiles) * 512
            for tt in range(TT):
                act.wait_ge(s("xsB_ps"), past("xsB_ps") + tt + 1)
                act.copy(xs[:, tt, :], PS[:, 2 * (tt % 2), :]).then_inc(s("xs"), 1)
                act.copy(Br[:, tt, :], PS[:, 2 * (tt % 2) + 1, 0:256]).then_inc(s("Br"), 1)
            act.wait_ge(s("CB"), past("CB") + 2)
            act.activation(EX, PS[:, 5, 0:128], ACT.Exp).then_inc(s("dec"), 1)
            act.activation(small[:, 0:64], PS[:, 5, 128:192], ACT.Exp).then_inc(s("dec"), 1)
            act.activation(view(Z[:, 0, 0:1], [1, nz]), view(Z[:, 0, 0:1], [1, nz]), ACT.Silu).then_inc(s("cv"), 1)
            for n in range(y_before[-1]):
                act.wait_ge(s("seg"), past("seg") + n + 1)
                if n >= 2:
                    act.wait_ge(s("y_ps"), past("y_ps") + n - 1)
                act.activation(view(Es[:, n % 2, 0, 0:1], [1, 1024]), view(PS[:, 0, 0:1], [1, 1024]), ACT.Exp).then_inc(s("expd"), 1)
            for f in range(4):
                act.wait_ge(s("qkT_ps"), past("qkT_ps") + f + 1)
                act.copy(qT[:, f, 0:ntok], PS[:, f, 0:ntok]).then_inc(s("qT"), 1)

            def expo(u):
                nk = keys(UN[u][1])[1]
                b = u % DEEP
                act.wait_ge(s("nmax"), past("nmax") + u + 1)
                if u >= DEEP:
                    act.wait_ge(s("pT_ps"), past("pT_ps") + u - DEEP + 1)
                act.activation(Eb[:, b, 0:nk], PS[:, L_BANK[b], 0:nk], ACT.Exp, bias=u_max[:, b:b + 1], accum_out=u_sum[:, b:b + 1]).then_inc(s("p"), 1)

            for u in range(DEEP):
                expo(u)
            for u in range(len(UN)):
                nk = keys(UN[u][1])[1]
                act.wait_ge(s("pT_ps"), past("pT_ps") + u + 1)
                if u >= 2:
                    act.wait_ge(s("o_ps"), past("o_ps") + u - 1)
                act.copy(PT[:, u % 2, 0:nk], PS[:, 2 + u % 2, 0:nk]).then_inc(s("PT"), 1)
                if u + DEEP < len(UN):
                    expo(u + DEEP)
                if u == GATE_U:
                    act.wait_ge(s("y0"), past("y0") + 3)
                    for tt in tiles:
                        act.activation(Z[:, tt], Y[:, tt], ACT.Square, accum_out=rs4[:, tt:tt + 1]).then_inc(s("y_sq"), 1)
                    act.wait_ge(s("y_sq"), past("y_sq") + len(tiles))
                    act.activation(rs4[:, 0:len(tiles)], rs4[:, 0:len(tiles)], ACT.Sqrt, scale=1.0 / SSD_W, bias=eps).then_inc(s("stat_sd"), 1)
            for n, tt in enumerate(tiles):
                act.wait_ge(s("yT_ps"), past("yT_ps") + n + 1)
                act.copy(catT[:, 4:8, tt * P:(tt + 1) * P], PS[:, 6 + n % 2, :].rearrange("p (i n) -> p i n", i=4)).then_inc(s("yT"), 1)
            residual_act(act, "out", "r1")
            for i in range(2):
                weights_high(act, i)
            norm_act(act, "ffn", len(tiles), 1, 3)
            act.wait_ge(s("norm_turned"), past("norm_turned") + 16)
            for k in range(KT):
                act.wait_ge(s(("norm_act", "norm_dve")[k % 2]), past("norm_act") + first("ffn", "act") + k // 2 + 1)
                act.copy(as_r(xh[:, k, 0:ntok]), HT[:, k, 0:ntok]).then_inc(s("wh"), 1)
            weights_high(act, 2)
            for i in range(FT):
                act.wait_ge(s("gu"), past("gu") + i + 1)
                act.activation(hTv[:, i, :], PS[:, 2 * (i % GU_BANKS), 0:ntok], ACT.Silu).then_inc(s("sg"), 1)
                if i + N_WH < FT:
                    weights_high(act, i + N_WH)
            act.wait_ge(s("hT"), past("hT") + FT)
            for r in range(FT):
                down_split_high(act, r)
            residual_act(act, "down", "r2")

        def softplus(dve, link):
            dve.wait_ge(s("in_act"), past("in_act") + 1)
            dve.wait_ge(s("rows_in"), past("rows_in") + 16 * 7)
            for n, d in enumerate((1, 0)):
                dve.tensor_tensor(dt[:, d], dt[:, 0], view(r_bias[:, 8 * d:8 * d + 1], [0, TT], [1, SSD_H]), ALU.add)\
                   .then_inc(s("dtx"), 1)
                dve.wait_ge(s("dtx"), past("dtx") + n + 1)
            link(dve.memset(ones_b, 1.0))
            dve.wait_ge(s("A"), past("A") + 1)
            link(dve.tensor_scalar(r_A, r_A, -1.0, None, ALU.mult))
            dve.wait_ge(s("dtln"), past("dtln") + 1)
            dve.wait_ge(s("dtx"), past("dtx") + 2)
            flat = lambda a: a.rearrange("p d t h -> p (d t h)")
            link(dve.scalar_tensor_tensor(flat(dt), flat(dt), 0.0, flat(dA), ALU.max, ALU.add))
            dve.tensor_tensor(dA, dt, view(r_A, [8, 2], [0, TT], [1, SSD_H]), ALU.mult).then_inc(s("dA"), 1)

        def head_norm(dve, link, tt):
            hh = lambda a: a.rearrange("p (h e) -> p h e", e=HD)
            h0 = 0 if tt in tiles else 8
            nh = 10 - h0
            w5 = at("extra", 4096, 1920).rearrange("p (t n) -> p t n", t=3)
            if tt == 0:
                link(dve.tensor_scalar(r_qk[:, 0:64], r_qk[:, 0:64], 0.125, None, ALU.mult))
            row = QK[:, tt, HD * h0:640]
            sq = w5[:, 0, HD * h0:640]
            ss = qk_ss[:, 10 * tt + h0:10 * tt + 10]
            link(dve.tensor_tensor(sq, row, row, ALU.mult))
            dve.tensor_reduce(ss, hh(sq), AX.X, ALU.add).then_inc(s("stat"), 1)
            dve.wait_ge(s("stat_sd"), past("stat_sd") + tt + 1)
            link(dve.reciprocal(ss, ss))
            qk = hh(row)
            link(dve.tensor_tensor(qk, qk, view(ss, [1, nh], [0, HD]), ALU.mult))
            if h0 == 0:
                link(dve.tensor_tensor(qk[:, 0:8], qk[:, 0:8], view(r_qk[:, 0:1], [0, 8], [1, HD]), ALU.mult))
            link(dve.tensor_tensor(qk[:, nh - 2:nh], qk[:, nh - 2:nh], view(r_qk[:, 64:65], [0, 2], [1, HD]), ALU.mult))
            if tt < 2:
                quarter = lambda a: a.rearrange("p h (a e) -> p (h a) e", a=2)
                cos, sin = (view(cst[:, o + 32 * tt:o + 32 * tt + 1], [0, 2 * nh], [1, 32]) for o in (C_COS, C_SIN))
                tc, ts = hh(w5[:, 1, :]), hh(w5[:, 2, :])
                link(dve.tensor_tensor(quarter(tc), quarter(qk), cos, ALU.mult))
                link(dve.tensor_tensor(quarter(ts), quarter(qk), sin, ALU.mult))
                link(dve.tensor_tensor(qk[:, :, 0:32], tc[:, :, 0:32], ts[:, :, 32:64], ALU.subtract))
                link(dve.tensor_tensor(qk[:, :, 32:64], ts[:, :, 0:32], tc[:, :, 32:64], ALU.add))

        def dve_(dve, link):
            dve.wait_ge(s("vec_ps"), past("vec_ps") + 1)
            link(dve.tensor_copy(VC[:, 0:N_VEC], PS[:, 3, 0:N_VEC]))
            dve.wait_ge(s("mod_in"), past("mod_in") + 16)
            link(dve.tensor_copy(g2row, modrow[:, 5, :]))
            dve.wait_ge(s("vec_ps"), past("vec_ps") + 2)
            for v in range(2):
                link(dve.tensor_tensor(view(modc[:, 0, v, 0:1], [16, 6], [1, 2], [2, 4]), view(PS[:, 0, v:v + 1], [256, 6], [P, 2], [32, 4]),
                                       view(VC[:, 0:1], [8, 6], [1, 2], [2, 4]), ALU.add))
            for a, (sc, nw) in enumerate(((1, V_NMP), (4, V_NFP))):
                for v in range(2):
                    ins = dve.scalar_tensor_tensor(affine[:, a, v, :], modc[:, sc, v, :], 1.0, VC[:, nw:nw + 8], ALU.add, ALU.mult)
                    if a == 0 or v == 0:
                        link(ins)
            ins.then_inc(s("affine"), 1)
            for n, tt in enumerate(PRE):
                norm_tile_dve(dve, link, "pre", n, tt)
            for v in range(nv):
                gate_dve(dve, link, "g1", v, 2 * v)
            norm_out_dve(dve, "pre", TT, 0, 0)
            for n, (kind, i, e) in enumerate(products):
                if kind == "dt":
                    softplus(dve, link)
                if e != "dve":
                    continue
                dve.wait_ge(s("in"), past("in") + n + 1)
                bank = PS[:, n % 8, :]
                if kind == "kvz":
                    if i in tiles:
                        link(dve.tensor_copy(Z[:, i, 0:256], bank[:, 256:512]))
                    link(dve.tensor_copy(Vr[:, i, :], bank[:, 128:256]))
                    dve.tensor_copy(QK[:, i, 512:640], bank[:, 0:128]).then_inc(s("in_dve"), 1)
                    dve.wait_ge(s("in_dve"), past("in_dve") + count[n])
                    if i in tiles:
                        dve.wait_ge(s("in_act"), past("in_act") + count[n - 1])
                    head_norm(dve, link, i)
                else:
                    src = bank.rearrange("p (v n) -> p v n", v=2)
                    dst = cv[:, i, :].rearrange("p (v n) -> p v n", v=2)
                    tap = lambda w: VC[:, V_CW + 8 * w + i:V_CW + 8 * w + i + 1]
                    link(dve.tensor_scalar(dst, src, tap(2), VC[:, V_CB + i:V_CB + i + 1], ALU.mult, ALU.add))
                    for w in (0, 1, 3, 4):
                        sh = w - 2
                        a, b = max(0, -sh), 256 - max(0, sh)
                        ins = dve.scalar_tensor_tensor(dst[:, :, a:b], src[:, :, a + sh:b + sh], tap(w), dst[:, :, a:b], ALU.mult, ALU.add)
                        if w < 4:
                            link(ins)
                    ins.then_inc(s("in_dve"), 1)
            dve.wait_ge(s("CB"), past("CB") + 1)
            dve.wait_ge(s("dec"), past("dec") + 2)
            hb = lambda a: a.rearrange("p (h n) -> p h n", h=SSD_H)
            e_in = lambda d, tt: view(EX[:, 64 * d + 8 * tt:64 * d + 8 * tt + 1], [1, SSD_H], [0, HD])
            e_tot = lambda d, tt: view(small[:, 32 * d + 8 * tt:32 * d + 8 * tt + 1], [1, SSD_H], [0, HD])

            dve.wait_ge(s("y0"), past("y0") + 1)
            def score(i):
                d, c, tt = STEPS[i]
                if tt in tiles:
                    yi = y_before[i]
                    if yi:
                        dve.wait_ge(s("score"), past("score") + yi)
                    link(dve.tensor_tensor(CBm, PS[:, 6 + tt // 2, (tt % 2) * 256:(tt % 2) * 256 + 256].rearrange("p (g n) -> p g n", g=2),
                                           view(cst[:, MASK[d]:MASK[d] + 1], [0, 2], [1, P]), ALU.mult))
                    dve.wait_ge(s("expd"), past("expd") + yi + 1)
                    e4 = Es[:, yi % 2].rearrange("p (g h) n -> p g h n", g=2)
                    dve.tensor_tensor(e4, e4, view(CBm[:, 0, 0:1], [P, 2], [0, 4], [1, P]), ALU.mult).then_inc(s("score"), 1)

            score(0)
            for i, (d, c, tt) in enumerate(STEPS):
                if i + 1 < len(STEPS):
                    score(i + 1)
                if c < TT - 1:
                    dve.wait_ge(s("st_ps"), past("st_ps") + st_before[i] + 1)
                    if c == 0:
                        dve.tensor_copy(ST[:, d], PS[:, 2 + d, :]).then_inc(s("state"), 1)
                    else:
                        if tt in tiles:
                            dve.wait_ge(s("y_ps"), past("y_ps") + y_before[i] + 1)
                        link(dve.tensor_tensor(hb(ST[:, d]), hb(ST[:, d]), e_tot(d, tt), ALU.mult))
                        dve.tensor_tensor(ST[:, d], ST[:, d], PS[:, 2 + d, :], ALU.add).then_inc(s("state"), 1)
                    dve.wait_ge(s("state"), past("state") + st_before[i] + 1)
                if tt in tiles:
                    yi = y_before[i]
                    dve.wait_ge(s("y_ps"), past("y_ps") + yi + 1)
                    if c:
                        link(dve.tensor_tensor(hb(ytmp), hb(PS[:, 5, :]), e_in(d, tt), ALU.mult))
                        link(dve.tensor_tensor(Y[:, tt], Y[:, tt], ytmp, ALU.add))
                    dve.tensor_tensor(Y[:, tt], Y[:, tt], PS[:, 4, :], ALU.add).then_inc(s("y"), 1)
                    dve.wait_ge(s("y"), past("y") + yi + 1)
            dve.wait_ge(s("y0"), past("y0") + 2)
            for g in range(2):
                dve.wait_ge(s("qkT_ps"), past("qkT_ps") + 4 + g + 1)
                for c in range(2):
                    dve.tensor_copy(kz[64 * c:64 * c + 64, g, c, :], PS[64 * c:64 * c + 64, 4 + g, :]).then_inc(s("kT"), 1)

            def peak(u):
                nk = keys(UN[u][1])[1]
                b = u % DEEP
                dve.wait_ge(s("lg"), past("lg") + u + 1)
                if u >= DEEP:
                    dve.wait_ge(s("p"), past("p") + u - DEEP + 1)
                dve.tensor_reduce(u_max[:, b:b + 1], PS[:, L_BANK[b], 0:nk], AX.X, ALU.max, negate=True).then_inc(s("nmax"), 1)

            for u in range(DEEP):
                peak(u)
            for u in range(len(UN)):
                f, tt, c = UN[u]
                nk = keys(tt)[1]
                b = u % DEEP
                dve.wait_ge(s("p"), past("p") + u + 1)
                link(dve.reciprocal(u_r[:, b:b + 1], u_sum[:, b:b + 1]))
                dve.tensor_scalar(Eb[:, b, 0:nk], Eb[:, b, 0:nk], u_r[:, b:b + 1], None, ALU.mult).then_inc(s("pn"), 1)
                if u + DEEP < len(UN):
                    peak(u + DEEP)
                if u == GATE_U + 3:
                    dve.wait_ge(s("stat_sd"), past("stat_sd") + TT + 1)
                    link(dve.reciprocal(rs4[:, 0:len(tiles)], rs4[:, 0:len(tiles)]))
                    dve.wait_ge(s("ssdn_in"), past("ssdn_in") + 16)
                if GATE_U + 3 <= u < GATE_U + 3 + len(tiles):
                    tt_ = u - GATE_U - 3
                    dve.scalar_tensor_tensor(Y[:, tt_], Y[:, tt_], rs4[:, tt_:tt_ + 1], SSDN, ALU.mult, ALU.mult).then_inc(s("ygated"), 1)
                if u % 2 and u >= 3:
                    o_copy(dve, u // 2 - 1)
            o_copy(dve, len(UN) // 2 - 1)
            residual_dve(dve, link, "r1", "x1")
            for i in range(2):
                weights_low(dve, i)
            norm_out_dve(dve, "ffn", len(tiles), 1, 3)
            for k in range(KT):
                dve.wait_ge(s("wh"), past("wh") + x_split(k))
                dve.tensor_tensor(as_r(HT[:, k, 0:ntok]), HT[:, k, 0:ntok], as_r(xh[:, k, 0:ntok]), ALU.subtract).then_inc(s("wl"), 1)
            weights_low(dve, 2)
            for i in range(FT):
                dve.wait_ge(s("sg"), past("sg") + i + 1)
                dve.tensor_tensor(hTv[:, i, :], hTv[:, i, :], PS[:, 2 * (i % GU_BANKS) + 1, 0:ntok], ALU.mult).then_inc(s("hT"), 1)
                if i + N_WH < FT:
                    weights_low(dve, i + N_WH)
                if i in G2_AT[0:nv]:
                    gate_dve(dve, link, "g2", G2_AT.index(i), 6)
            for r in range(FT):
                down_split_low(dve, r)
            residual_dve(dve, link, "r2", "x2")

        def pool_(pool, link):
            hb = lambda a: a.rearrange("p (h n) -> p h n", h=SSD_H)
            pool.wait_ge(s("dA"), past("dA") + 1)
            pool.wait_ge(s("xs"), past("xs") + TT)
            pool.wait_ge(s("Br"), past("Br") + TT)

            def decay(i):
                d, c, tt = STEPS[i]
                if tt in tiles:
                    yi = y_before[i]
                    if yi >= 2:
                        pool.wait_ge(s("seg"), past("seg") + yi - 1)
                    pool.tensor_tensor(Rb[:, yi % 2], view(cst[:, MASK[d]:MASK[d] + 1], [0, SSD_H], [1, P]),
                                       view(dA[:, d, tt, 0:1], [1, SSD_H], [0, P]), ALU.mult).then_inc(s("R"), 1)

            def inputs(i):
                d, c, tt = STEPS[i]
                if i >= 2:
                    pool.wait_ge(s("y_ps"), past("y_ps") + y_before[i - 1])
                    pool.wait_ge(s("st_ps"), past("st_ps") + st_before[i - 1])
                link(pool.tensor_tensor(hb(xdt[i % 2]), hb(xs[:, tt]), view(dt[:, d, tt, 0:1], [1, SSD_H], [0, HD]), ALU.mult))
                e_end = view(EX[:, 64 * d + 32 + 8 * tt:64 * d + 33 + 8 * tt], [1, SSD_H], [0, HD])
                pool.tensor_tensor(hb(xde[i % 2]), hb(xdt[i % 2]), e_end, ALU.mult).then_inc(s("xdt"), 1)

            decay(0)
            pool.wait_ge(s("dec"), past("dec") + 2)
            inputs(0)
            for tt in tiles:
                ins = pool.tensor_tensor(Y[:, tt].rearrange("p (h n) -> p h n", h=SSD_H), xs[:, tt].rearrange("p (h n) -> p h n", h=SSD_H),
                                         view(r_skip, [1, SSD_H], [0, HD]), ALU.mult)
                if tt == tiles[-1]:
                    ins.then_inc(s("y0"), 1)
                else:
                    link(ins)
            pool.wait_ge(s("CB"), past("CB") + 1)
            for i in range(1, len(STEPS)):
                decay(i)
                inputs(i)
            pool.wait_ge(s("y"), past("y") + y_before[-1])
            pool.wait_ge(s("seg"), past("seg") + y_before[-1])
            pool.memset(view(kz[:, 0, 0, 0:1], [1, 2048]), 0.0).then_inc(s("y0"), 1)
            pool.wait_ge(s("cv"), past("cv") + 9)
            for tt in tiles:
                ins = pool.tensor_tensor(Y[:, tt], Y[:, tt], Z[:, tt], ALU.mult)
                if tt == tiles[-1]:
                    ins.then_inc(s("y0"), 1)
                else:
                    link(ins)

        def o_copy(dve, pair):
            f, tt, _ = UN[2 * pair]
            dve.wait_ge(s("o_ps"), past("o_ps") + 2 * pair + 2)
            dve.tensor_copy(catT[:, f, tt * P:(tt + 1) * P], PS[:, 4 + pair % 2, 0:P]).then_inc(s("oT"), 1)

        return {"sp": sp_, "pe": pe_, "act": act_, "dve": dve_, "pool": pool_}

    b0, b1 = hybrid(0), hybrid(1)

    final = {"a0": ("ln_out", 2), "m0": ("ln_out", 4), "a1": ("ln_out", 6), "m1": ("ln_out", 8), "b0": ("b_x2", 4)}
    block = ctx.enter_context(nc.Block())
    stages = ["a0", "m0", "a1", "m1", "b0", "b1"]
    last = stages.index(stop) if stop else len(stages) - 1

    @block.sync
    def _(sp):
        a0_sp(sp)
        if last >= 1:
            m0["sp"](sp)
        if last >= 2:
            a1_sp(sp)
        if last >= 3:
            m1["sp"](sp)
        if last >= 4:
            b0["sp"](sp)
        if last >= 5:
            b1["sp"](sp)
        if stop and last < 5:
            sp.wait_ge(S(final[stop][0]), final[stop][1])
            sp.dma_start(out.rearrange("b (t p) d -> p (b t) d", p=P), X).then_inc(S("out_dma"), 16)
            sp.wait_ge(S("out_dma"), 16)

    @block.tensor
    def _(pe):
        a0_pe(pe)
        if last >= 1:
            m0["pe"](pe)
        if last >= 2:
            a1_pe(pe)
        if last >= 3:
            m1["pe"](pe)
        if last >= 4:
            b0["pe"](pe)
        if last >= 5:
            b1["pe"](pe)

    @block.scalar
    def _(act):
        a0_act(act)
        if last >= 1:
            m0["act"](act)
        if last >= 2:
            a1_act(act)
        if last >= 3:
            m1["act"](act)
        if last >= 4:
            b0["act"](act)
        if last >= 5:
            b1["act"](act)

    @block.gpsimd
    def _(pool):
        link = chain(pool, "pool_step")
        if last >= 4:
            b0["pool"](pool, link)
        if last >= 5:
            b1["pool"](pool, link)

    @block.vector
    def _(dve):
        link = chain(dve, "dve_step")
        a0_dve(dve, link)
        if last >= 1:
            m0["dve"](dve, link)
        if last >= 2:
            a1_dve(dve, link)
        if last >= 3:
            m1["dve"](dve, link)
        if last >= 4:
            b0["dve"](dve, link)
        if last >= 5:
            b1["dve"](dve, link)


_INS = [
    "x", "rel_table", "da_wq", "da_wk", "da_wv", "da_wo", "da_lq1", "da_lk1", "da_lq2", "da_lk2",
    "da_subln_g", "sb_wq", "sb_wk", "sb_wv", "sb_wo", "ln_mix_g", "ln_mix_b", "ln_ffn_g", "ln_ffn_b",
    "moe_w_group", "moe_b_group", "moe_w_expert", "moe_b_expert", "moe_w1", "moe_w3", "moe_w2", "c_2",
    "ctx_2", "c_ctx_2", "w_mod_2", "b_mod_2", "norm_mix_pre_2", "norm_mix_post_2", "norm_ffn_pre_2",
    "norm_ffn_post_2", "w_in_2", "q_norm_2", "k_norm_2", "conv_w_2", "conv_b_2", "dt_bias_fwd_2",
    "dt_bias_bwd_2", "a_log_fwd_2", "a_log_bwd_2", "d_skip_2", "ssd_norm_2", "w_out_2", "w_gate_2", "w_up_2",
    "w_down_2",
]


def kernel(**inputs):
    import numpy as _np
    import concourse.bacc as _bacc
    from concourse import mybir as _mybir
    from concourse.bass_utils import run_bass_kernel_spmd as _run

    nc = _bacc.Bacc("TRN2", target_bir_lowering=False, num_devices=1)
    arrays, t = {}, {}

    def operand(name, a):
        a = _np.ascontiguousarray(a)
        arrays[f"in_{name}_dram"] = a
        t[name] = nc.dram_tensor(f"in_{name}_dram", a.shape, _mybir.dt.from_np(a.dtype), kind="ExternalInput").ap()

    for name in _INS:
        operand(name, inputs[name])
    consts, hot = const_tables()
    operand("consts", consts)
    operand("hot", hot)
    out = nc.dram_tensor("out_0_dram", (1, SEQ, D), F32, kind="ExternalOutput").ap()
    program(nc, t, out)
    r = _run(nc, [arrays], core_ids=[0])
    return r.results[0]["out_0_dram"]
```
